# Optimizing a Trainium2 kernel written in Bass

```python
import math
import jax, jax.numpy as jnp
from jax import lax
import numpy as np

D_MODEL = 1024
BATCH = 1
SEQ = 256
DEPTH = 1

CHUNK = 64
Q_BLOCK = 128
TOKEN_BLOCK = 128
EPS = 1e-6

SB_HEADS = 8
SB_HEAD_DIM = 64
SB_WIDTH = SB_HEADS * SB_HEAD_DIM

MLA_HEADS = 8
MLA_NOPE_DIM = 64
MLA_ROPE_DIM = 32
MLA_QK_DIM = MLA_NOPE_DIM + MLA_ROPE_DIM
MLA_V_DIM = 64
MLA_Q_RANK = 384
MLA_KV_RANK = 256
MLA_WIDTH = MLA_HEADS * MLA_V_DIM
ROPE_THETA = 10000.0

MIX_WIDTH = SB_WIDTH + MLA_WIDTH
IN_SPLITS = (SB_WIDTH, 2 * SB_WIDTH, 3 * SB_WIDTH,
             3 * SB_WIDTH + MLA_Q_RANK,
             3 * SB_WIDTH + MLA_Q_RANK + MLA_KV_RANK)
IN_PROJ_WIDTH = 3 * SB_WIDTH + MLA_Q_RANK + MLA_KV_RANK + MLA_ROPE_DIM

PEER_HEADS = 8
PEER_N_KEYS = 128
PEER_N_EXPERTS = PEER_N_KEYS * PEER_N_KEYS
PEER_KEY_DIM = 256
PEER_HALF_DIM = PEER_KEY_DIM // 2
PEER_TOPK = 16


def rms_norm(x, g):
    xf = x.astype(jnp.float32)
    y = xf * lax.rsqrt(jnp.mean(xf * xf, axis=-1, keepdims=True) + EPS)
    return (y * g.astype(jnp.float32)).astype(x.dtype)

def rope(x, pos):
    r = x.shape[-1]
    half = r // 2
    inv_freq = 1.0 / (ROPE_THETA ** (jnp.arange(half, dtype=jnp.float32) * (2.0 / r)))
    ang = pos.astype(jnp.float32)[..., None] * inv_freq
    cos = jnp.cos(ang)[:, :, None, :]
    sin = jnp.sin(ang)[:, :, None, :]
    xf = x.astype(jnp.float32)
    x1, x2 = xf[..., :half], xf[..., half:]
    out = jnp.concatenate([x1 * cos - x2 * sin, x1 * sin + x2 * cos], axis=-1)
    return out.astype(x.dtype)

def to_query_blocks(q):
    b, s, h, d = q.shape
    return q.reshape(b, s // Q_BLOCK, Q_BLOCK, h, d).transpose(1, 0, 3, 2, 4)

def from_query_blocks(o):
    nb, b, qb, h, d = o.shape
    return o.transpose(1, 0, 2, 3, 4).reshape(b, nb * qb, h * d)

def stick_breaking_attention(q, k, v):
    b, s, h, d = q.shape
    nb = s // Q_BLOCK
    scale = d ** -0.5
    kpos = jnp.arange(s)

    def block(args):
        qi, bi = args
        z = jnp.einsum('bhqd,bshd->bhqs', qi, k,
                       preferred_element_type=jnp.float32) * scale
        qpos = bi * Q_BLOCK + jnp.arange(Q_BLOCK)
        strict = kpos[None, :] < qpos[:, None]
        log_fail = jnp.where(strict, jax.nn.log_sigmoid(-z), 0.0)
        later = lax.cumsum(log_fail, axis=3, reverse=True) - log_fail
        a = jnp.where(strict, jnp.exp(jax.nn.log_sigmoid(z) + later), 0.0)
        return jnp.einsum('bhqs,bshd->bqhd', a.astype(v.dtype), v)

    out = lax.map(block, (to_query_blocks(q), jnp.arange(nb)))
    return from_query_blocks(out)

def chunk_causal_softmax_attention(q, k, v):
    b, s, h, dq = q.shape
    nb = s // Q_BLOCK
    scale = dq ** -0.5
    kchunk = jnp.arange(s) // CHUNK

    def block(args):
        qi, bi = args
        sc = jnp.einsum('bhqd,bshd->bhqs', qi, k,
                        preferred_element_type=jnp.float32) * scale
        qchunk = (bi * Q_BLOCK + jnp.arange(Q_BLOCK)) // CHUNK
        allowed = kchunk[None, :] <= qchunk[:, None]
        p = jax.nn.softmax(jnp.where(allowed, sc, -jnp.inf), axis=-1)
        return jnp.einsum('bhqs,bshd->bqhd', p.astype(v.dtype), v)

    out = lax.map(block, (to_query_blocks(q), jnp.arange(nb)))
    return from_query_blocks(out)

def peer_ffn(h, w_q, sub_keys, u, v):
    b, s, d = h.shape
    nb = (b * s) // TOKEN_BLOCK
    k = PEER_TOPK

    def block(xt):
        q = (xt @ w_q).reshape(TOKEN_BLOCK, PEER_HEADS, 2, PEER_HALF_DIM)
        sc = jnp.einsum('thcd,chnd->thcn', q, sub_keys,
                        preferred_element_type=jnp.float32)
        top_s, top_i = lax.top_k(sc, k)
        cand_s = top_s[:, :, 0, :, None] + top_s[:, :, 1, None, :]
        cand_i = top_i[:, :, 0, :, None] * PEER_N_KEYS + top_i[:, :, 1, None, :]
        best_s, best_pos = lax.top_k(cand_s.reshape(TOKEN_BLOCK, PEER_HEADS, k * k), k)
        idx = jnp.take_along_axis(cand_i.reshape(TOKEN_BLOCK, PEER_HEADS, k * k),
                                  best_pos, axis=-1)
        g = jax.nn.softmax(best_s, axis=-1)
        pre = jnp.einsum('td,thkd->thk', xt, u[idx], preferred_element_type=jnp.float32)
        coef = (g * jax.nn.gelu(pre, approximate=False)).astype(v.dtype)
        return jnp.einsum('thk,thkd->td', coef, v[idx])

    out = lax.map(block, h.reshape(nb, TOKEN_BLOCK, d))
    return out.reshape(b, s, d)

def first_inputs(seed: int = 0) -> dict:
    key = jax.random.key(seed)
    ks = jax.random.split(key, 20)
    f32 = jnp.float32

    def w(k_, shape, fan_in):
        return jax.random.normal(k_, shape, f32) * (fan_in ** -0.5)

    def gain(k_, shape):
        return 1.0 + 0.02 * jax.random.normal(k_, shape, f32)

    x = jax.random.normal(ks[0], (BATCH, SEQ, D_MODEL), f32)
    offset = jax.random.randint(ks[1], (BATCH, 1), 0, 1024, dtype=jnp.int32)
    positions = (offset + jnp.arange(SEQ, dtype=jnp.int32)[None, :]).astype(jnp.int32)
    return {
        "x": x,
        "positions": positions,
        "attn_norm": gain(ks[2], (DEPTH, D_MODEL)),
        "w_in": w(ks[3], (DEPTH, D_MODEL, IN_PROJ_WIDTH), D_MODEL),
        "cq_norm": gain(ks[4], (DEPTH, MLA_Q_RANK)),
        "w_uq": w(ks[5], (DEPTH, MLA_Q_RANK, MLA_HEADS * MLA_QK_DIM), MLA_Q_RANK),
        "ckv_norm": gain(ks[6], (DEPTH, MLA_KV_RANK)),
        "w_ukv": w(ks[7], (DEPTH, MLA_KV_RANK, MLA_HEADS * (MLA_NOPE_DIM + MLA_V_DIM)), MLA_KV_RANK),
        "q_norm": gain(ks[8], (DEPTH, MLA_QK_DIM)),
        "k_norm": gain(ks[9], (DEPTH, MLA_QK_DIM)),
        "sb_out_norm": gain(ks[10], (DEPTH, SB_WIDTH)),
        "mla_out_norm": gain(ks[11], (DEPTH, MLA_WIDTH)),
        "w_o": w(ks[12], (DEPTH, MIX_WIDTH, D_MODEL), MIX_WIDTH),
        "ffn_norm": gain(ks[13], (DEPTH, D_MODEL)),
        "peer_w_q": w(ks[14], (DEPTH, D_MODEL, PEER_HEADS * PEER_KEY_DIM), D_MODEL),
        "peer_sub_keys": w(ks[15], (DEPTH, 2, PEER_HEADS, PEER_N_KEYS, PEER_HALF_DIM), PEER_HALF_DIM),
        "peer_u": w(ks[16], (DEPTH, PEER_N_EXPERTS, D_MODEL), D_MODEL),
        "peer_v": w(ks[17], (DEPTH, PEER_N_EXPERTS, D_MODEL), D_MODEL),
    }

def first_block(x, positions, attn_norm, w_in, cq_norm, w_uq, ckv_norm, w_ukv, q_norm, k_norm,
              sb_out_norm, mla_out_norm, w_o, ffn_norm, peer_w_q, peer_sub_keys, peer_u, peer_v):
    b, s, _ = x.shape
    for l in range(DEPTH):
        h = rms_norm(x, attn_norm[l])
        proj = h @ w_in[l]
        sb_q, sb_k, sb_v, cq, ckv, k_pe = jnp.split(proj, IN_SPLITS, axis=-1)

        sb = stick_breaking_attention(sb_q.reshape(b, s, SB_HEADS, SB_HEAD_DIM),
                                      sb_k.reshape(b, s, SB_HEADS, SB_HEAD_DIM),
                                      sb_v.reshape(b, s, SB_HEADS, SB_HEAD_DIM))

        q = (rms_norm(cq, cq_norm[l]) @ w_uq[l]).reshape(b, s, MLA_HEADS, MLA_QK_DIM)
        kv = (rms_norm(ckv, ckv_norm[l]) @ w_ukv[l]).reshape(b, s, MLA_HEADS, MLA_NOPE_DIM + MLA_V_DIM)
        k_nope, v = kv[..., :MLA_NOPE_DIM], kv[..., MLA_NOPE_DIM:]
        k_rot = jnp.broadcast_to(k_pe[:, :, None, :], (b, s, MLA_HEADS, MLA_ROPE_DIM))
        k = jnp.concatenate([k_nope, k_rot], axis=-1)
        q = rms_norm(q, q_norm[l])
        k = rms_norm(k, k_norm[l])
        q = jnp.concatenate([q[..., :MLA_NOPE_DIM], rope(q[..., MLA_NOPE_DIM:], positions)], axis=-1)
        k = jnp.concatenate([k[..., :MLA_NOPE_DIM], rope(k[..., MLA_NOPE_DIM:], positions)], axis=-1)
        mla = chunk_causal_softmax_attention(q, k, v)

        mixed = jnp.concatenate([rms_norm(sb, sb_out_norm[l]),
                                 rms_norm(mla, mla_out_norm[l])], axis=-1)
        x = x + mixed @ w_o[l]

        x = x + peer_ffn(rms_norm(x, ffn_norm[l]), peer_w_q[l], peer_sub_keys[l],
                         peer_u[l], peer_v[l])
    return x


DEPTH_2 = 2

GRID_W = 64
CTX_LEN = 256
FOURIER_WIDTH = D_MODEL // 4
FOURIER_GROUPS = 4
FOURIER_GROUP_DIM = FOURIER_WIDTH // FOURIER_GROUPS
DIFF_WIDTH = D_MODEL - FOURIER_WIDTH
DIFF_HEAD_DIM = 64
DIFF_V_DIM = 2 * DIFF_HEAD_DIM
DIFF_HEADS = DIFF_WIDTH // DIFF_V_DIM
IN_WIDTH_EVEN = 3 * DIFF_WIDTH + FOURIER_WIDTH
ATTN_SCALE = DIFF_HEAD_DIM ** -0.5
LAMBDA_STD = 0.1
CONV_WIDTH = 31
D_FF = -(-8 * D_MODEL // (3 * 256)) * 256


def rmsnorm(x, g):
    x32 = x.astype(jnp.float32)
    y = x32 * lax.rsqrt(jnp.mean(x32 * x32, axis=-1, keepdims=True) + EPS)
    return (y * g.astype(jnp.float32)).astype(x.dtype)

def layernorm(x, g, b):
    x32 = x.astype(jnp.float32)
    mu = jnp.mean(x32, axis=-1, keepdims=True)
    xc = x32 - mu
    y = xc * lax.rsqrt(jnp.mean(xc * xc, axis=-1, keepdims=True) + EPS)
    return (y * g.astype(jnp.float32) + b.astype(jnp.float32)).astype(x.dtype)

def modulate(h, shift, scale):
    return h * (1 + scale) + shift

def axial_rope_tables(rows_n):
    row = jnp.repeat(jnp.arange(rows_n, dtype=jnp.float32), GRID_W)
    col = jnp.tile(jnp.arange(GRID_W, dtype=jnp.float32), rows_n)
    axis_dim = DIFF_HEAD_DIM // 2
    inv_freq = ROPE_THETA ** (-jnp.arange(0, axis_dim, 2, dtype=jnp.float32) / axis_dim)
    ang = jnp.concatenate([row[:, None] * inv_freq, col[:, None] * inv_freq], axis=-1)
    return jnp.cos(ang), jnp.sin(ang)

def apply_rope(x, cos, sin):
    x1, x2 = jnp.split(x, 2, axis=-1)
    c = cos[:, None, :].astype(x.dtype)
    s = sin[:, None, :].astype(x.dtype)
    return jnp.concatenate([x1 * c - x2 * s, x1 * s + x2 * c], axis=-1)

def rope_heads(q, cos, sin):
    B, S, H, two, d = q.shape
    return apply_rope(q.reshape(B, S, H * two, d), cos, sin).reshape(q.shape)

def diff_attend(q, k, v, lam):
    s = jnp.einsum('bqhcd,bkhcd->bhcqk', q, k, preferred_element_type=jnp.float32) * ATTN_SCALE
    p = jax.nn.softmax(s, axis=-1)
    a = p[:, :, 0] - lam * p[:, :, 1]
    return jnp.einsum('bhqk,bkhe->bqhe', a.astype(v.dtype), v)

def fourier_groups(f, w):
    B, T, _ = f.shape
    fg = f.reshape(B, T, FOURIER_GROUPS, FOURIER_GROUP_DIM).astype(jnp.float32)
    z = jnp.fft.fft2(fg, axes=(1, 3), norm='ortho').real.astype(f.dtype)
    return jnp.einsum('btgc,gce->btge', z, w).reshape(B, T, FOURIER_WIDTH)

def split_proj(u):
    B, T, _ = u.shape
    q, k, v, f = jnp.split(u, [DIFF_WIDTH, 2 * DIFF_WIDTH, 3 * DIFF_WIDTH], axis=-1)
    return (q.reshape(B, T, DIFF_HEADS, 2, DIFF_HEAD_DIM),
            k.reshape(B, T, DIFF_HEADS, 2, DIFF_HEAD_DIM),
            v.reshape(B, T, DIFF_HEADS, DIFF_V_DIM),
            f)

def merge_heads(o, f, subln_g, fourier_w, w_out, lambda_init):
    B, T = o.shape[:2]
    o = (rmsnorm(o, subln_g) * (1.0 - lambda_init)).reshape(B, T, DIFF_WIDTH)
    return jnp.concatenate([o, fourier_groups(f, fourier_w)], axis=-1) @ w_out

def diff_fourier_mixer(h_l, h_c, cos, sin, w_in, lq1, lk1, lq2, lk2, subln_g, fourier_w, w_out,
                       lambda_init, ctx_update):
    B, S, _ = h_l.shape
    q_l, k_l, v_l, f_l = split_proj(h_l @ w_in)
    q_c, k_c, v_c, f_c = split_proj(h_c @ w_in)
    q_l = rope_heads(q_l, cos, sin)
    k_l = rope_heads(k_l, cos, sin)
    lam = (jnp.exp(jnp.sum(lq1.astype(jnp.float32) * lk1.astype(jnp.float32)))
           - jnp.exp(jnp.sum(lq2.astype(jnp.float32) * lk2.astype(jnp.float32))) + lambda_init)
    k_all = jnp.concatenate([k_c, k_l], axis=1)
    v_all = jnp.concatenate([v_c, v_l], axis=1)
    n_blk = S // Q_BLOCK
    q_blocks = jnp.moveaxis(q_l.reshape(B, n_blk, Q_BLOCK, DIFF_HEADS, 2, DIFF_HEAD_DIM), 1, 0)
    o = lax.map(lambda qb: diff_attend(qb, k_all, v_all, lam), q_blocks)
    o_l = jnp.moveaxis(o, 0, 1).reshape(B, S, DIFF_HEADS, DIFF_V_DIM)
    y_l = merge_heads(o_l, f_l, subln_g, fourier_w, w_out, lambda_init)
    y_c = None
    if ctx_update:
        y_c = merge_heads(diff_attend(q_c, k_c, v_c, lam), f_c, subln_g, fourier_w, w_out, lambda_init)
    return y_l, y_c

def depthwise_conv(u, w):
    return lax.conv_general_dilated(
        u, w[:, None, :].astype(u.dtype), window_strides=(1,),
        padding=[(CONV_WIDTH // 2, CONV_WIDTH // 2)],
        dimension_numbers=('NWC', 'WIO', 'NWC'), feature_group_count=u.shape[-1])

def conformer_conv(h, pw1_w, pw1_b, dw_w, dw_b, ln_g, ln_b, pw2_w, pw2_b):
    a, g = jnp.split(h @ pw1_w + pw1_b, 2, axis=-1)
    u = a * jax.nn.sigmoid(g)
    u = depthwise_conv(u, dw_w) + dw_b
    u = jax.nn.silu(layernorm(u, ln_g, ln_b))
    return u @ pw2_w + pw2_b

def swiglu(h, w1, w3, w2):
    return (jax.nn.silu(h @ w1) * (h @ w3)) @ w2

def second_inputs(seed: int = 0) -> dict:
    key = jax.random.key(seed)
    ks = iter(jax.random.split(key, 32))
    n_even = (DEPTH_2 + 1) // 2
    n_odd = DEPTH_2 // 2
    f32 = jnp.float32

    def nrm(shape):
        return jax.random.normal(next(ks), shape, f32)

    def w(shape, fan_in):
        return nrm(shape) * fan_in ** -0.5

    def gain(shape):
        return 1.0 + 0.05 * nrm(shape)

    def bias(shape):
        return 0.02 * nrm(shape)

    D = D_MODEL
    return {
        'x': nrm((BATCH, SEQ, D)),
        'c': nrm((BATCH, D)),
        'ctx': nrm((BATCH, CTX_LEN, D)),
        'c_ctx': nrm((D,)),
        'ada_w': w((DEPTH_2, D, 6 * D), D),
        'ada_b': bias((DEPTH_2, 6 * D)),
        'mix_norm_g': gain((DEPTH_2, D)),
        'ffn_norm_g': gain((DEPTH_2, D)),
        'ffn_w1': w((DEPTH_2, D, D_FF), D),
        'ffn_w3': w((DEPTH_2, D, D_FF), D),
        'ffn_w2': w((DEPTH_2, D_FF, D), D_FF),
        'ev_w_in': w((n_even, D, IN_WIDTH_EVEN), D),
        'ev_lambda_q1': LAMBDA_STD * nrm((n_even, DIFF_HEAD_DIM)),
        'ev_lambda_k1': LAMBDA_STD * nrm((n_even, DIFF_HEAD_DIM)),
        'ev_lambda_q2': LAMBDA_STD * nrm((n_even, DIFF_HEAD_DIM)),
        'ev_lambda_k2': LAMBDA_STD * nrm((n_even, DIFF_HEAD_DIM)),
        'ev_subln_g': gain((n_even, DIFF_V_DIM)),
        'ev_fourier_w': w((n_even, FOURIER_GROUPS, FOURIER_GROUP_DIM, FOURIER_GROUP_DIM), FOURIER_GROUP_DIM),
        'ev_w_out': w((n_even, D, D), D),
        'od_pw1_w': w((n_odd, D, 2 * D), D),
        'od_pw1_b': bias((n_odd, 2 * D)),
        'od_dw_w': w((n_odd, CONV_WIDTH, D), CONV_WIDTH),
        'od_dw_b': bias((n_odd, D)),
        'od_ln_g': gain((n_odd, D)),
        'od_ln_b': bias((n_odd, D)),
        'od_pw2_w': w((n_odd, D, D), D),
        'od_pw2_b': bias((n_odd, D)),
        'final_g': gain((D,)),
    }

def second_block(x, c, ctx, c_ctx, ada_w, ada_b, mix_norm_g, ffn_norm_g, ffn_w1, ffn_w3, ffn_w2,
              ev_w_in, ev_lambda_q1, ev_lambda_k1, ev_lambda_q2, ev_lambda_k2, ev_subln_g,
              ev_fourier_w, ev_w_out, od_pw1_w, od_pw1_b, od_dw_w, od_dw_b, od_ln_g, od_ln_b,
              od_pw2_w, od_pw2_b, final_g):
    S = x.shape[1]
    ROWS = S // GRID_W
    cos, sin = axial_rope_tables(ROWS)
    silu_c = jax.nn.silu(c)
    silu_cc = jax.nn.silu(c_ctx)
    xc = ctx
    for i in range(DEPTH_2):
        j = i // 2
        even = i % 2 == 0
        ctx_update = any(k % 2 == 0 for k in range(i + 1, DEPTH_2))
        read_ctx = even or ctx_update
        mod_l = jnp.split((silu_c @ ada_w[i] + ada_b[i])[:, None, :], 6, axis=-1)
        h_l = modulate(rmsnorm(x, mix_norm_g[i]), mod_l[0], mod_l[1])
        mod_c = None
        h_c = None
        if read_ctx:
            mod_c = jnp.split((silu_cc @ ada_w[i] + ada_b[i])[None, None, :], 6, axis=-1)
            h_c = modulate(rmsnorm(xc, mix_norm_g[i]), mod_c[0], mod_c[1])
        if even:
            lambda_init = 0.8 - 0.6 * math.exp(-0.3 * i)
            y_l, y_c = diff_fourier_mixer(h_l, h_c, cos, sin, ev_w_in[j], ev_lambda_q1[j], ev_lambda_k1[j],
                                          ev_lambda_q2[j], ev_lambda_k2[j], ev_subln_g[j], ev_fourier_w[j],
                                          ev_w_out[j], lambda_init, ctx_update)
        else:
            conv_args = (od_pw1_w[j], od_pw1_b[j], od_dw_w[j], od_dw_b[j], od_ln_g[j], od_ln_b[j],
                         od_pw2_w[j], od_pw2_b[j])
            y_l = conformer_conv(h_l, *conv_args)
            y_c = conformer_conv(h_c, *conv_args) if ctx_update else None
        x = x + mod_l[2] * y_l
        x = x + mod_l[5] * swiglu(modulate(rmsnorm(x, ffn_norm_g[i]), mod_l[3], mod_l[4]),
                                  ffn_w1[i], ffn_w3[i], ffn_w2[i])
        if ctx_update:
            xc = xc + mod_c[2] * y_c
            xc = xc + mod_c[5] * swiglu(modulate(rmsnorm(xc, ffn_norm_g[i]), mod_c[3], mod_c[4]),
                                        ffn_w1[i], ffn_w3[i], ffn_w2[i])
    return rmsnorm(x, final_g)


def setup_inputs(seed=0):
    out = dict(first_inputs(seed))
    for name, value in second_inputs(seed + 1).items():
        if name != "x":
            out[name + "_2"] = value
    return out


def reference(
    x, positions, attn_norm, w_in, cq_norm, w_uq, ckv_norm, w_ukv, q_norm, k_norm, sb_out_norm,
    mla_out_norm, w_o, ffn_norm, peer_w_q, peer_sub_keys, peer_u, peer_v, c_2, ctx_2, c_ctx_2,
    ada_w_2, ada_b_2, mix_norm_g_2, ffn_norm_g_2, ffn_w1_2, ffn_w3_2, ffn_w2_2, ev_w_in_2,
    ev_lambda_q1_2, ev_lambda_k1_2, ev_lambda_q2_2, ev_lambda_k2_2, ev_subln_g_2,
    ev_fourier_w_2, ev_w_out_2, od_pw1_w_2, od_pw1_b_2, od_dw_w_2, od_dw_b_2, od_ln_g_2,
    od_ln_b_2, od_pw2_w_2, od_pw2_b_2, final_g_2,
):
    x = first_block(
        x, positions, attn_norm, w_in, cq_norm, w_uq, ckv_norm, w_ukv, q_norm, k_norm,
        sb_out_norm, mla_out_norm, w_o, ffn_norm, peer_w_q, peer_sub_keys, peer_u, peer_v,
    )
    return second_block(
        x, c_2, ctx_2, c_ctx_2, ada_w_2, ada_b_2, mix_norm_g_2, ffn_norm_g_2, ffn_w1_2,
        ffn_w3_2, ffn_w2_2, ev_w_in_2, ev_lambda_q1_2, ev_lambda_k1_2, ev_lambda_q2_2,
        ev_lambda_k2_2, ev_subln_g_2, ev_fourier_w_2, ev_w_out_2, od_pw1_w_2, od_pw1_b_2,
        od_dw_w_2, od_dw_b_2, od_ln_g_2, od_ln_b_2, od_pw2_w_2, od_pw2_b_2, final_g_2,
    )


_drawn_inputs = setup_inputs


def setup_inputs(seed=0):
    import zlib

    import numpy as np

    out = dict(_drawn_inputs(seed))
    spreads = {}
    factors = {'cq_norm': 5.559,
     'ckv_norm': 3.715,
     'q_norm': 4.879,
     'k_norm': 4.94,
     'sb_out_norm': 4.996,
     'mla_out_norm': 5.003,
     'ffn_norm': 8.0,
     'peer_w_q': 4.932,
     'peer_sub_keys': 4.917,
     'peer_u': 5.431,
     'peer_v': 4.919,
     'mix_norm_g_2': 2.792,
     'ev_lambda_q2_2': 8.0,
     'ev_lambda_k2_2': 8.0,
     'ev_subln_g_2': 25.98,
     'od_pw1_b_2': 43.292,
     'od_dw_b_2': 34.499,
     'od_ln_g_2': 91.336,
     'od_ln_b_2': 200.0,
     'od_pw2_b_2': 156.907,
     'ada_b_2': 3.474,
     'ffn_norm_g_2': 8.0,
     'ev_lambda_q1_2': 6.025,
     'ev_lambda_k1_2': 3.77}
    for name, (base, spread) in spreads.items():
        noise = np.random.default_rng([zlib.crc32(name.encode()), seed]).standard_normal(out[name].shape)
        drawn = base * np.exp(spread * noise) if base else spread * noise
        out[name] = __import__('jax').numpy.asarray(drawn.astype(out[name].dtype))
    for name, factor in factors.items():
        out[name] = (out[name] * factor).astype(out[name].dtype)
    return out
```

```python
from contextlib import ExitStack

import numpy as np

import concourse.bass as bass
from concourse import mybir

ALU = mybir.AluOpType
ACT = mybir.ActivationFunctionType
F32 = mybir.dt.float32
I32 = mybir.dt.int32
U32 = mybir.dt.uint32
AX = mybir.AxisListType

P = 128
T = 256
TB = T // P
D = 1024
KC = D // P
EPS = 1e-6
H1 = 8
SBD = 64
QKD, NOPE, ROPE = 96, 64, 32
ATT = 3 * P
NKEY, TOPK, PH = 128, 16, 8
J = 128
UT = J // 2
H2, VD = 6, 128
S2 = 2 * T
FF = 2816
NF = FF // P
CONV = 31
PADL = CONV // 2
NADA = 96
NS = 4
SLOT = 2048
NB = 4
LAMBDA_INIT = 0.2
GB = 4
ROUND = 12582912.0


def plan_tiles():
    t = [("in", c) for c in range(9)]
    t += [("uq", 0), ("uq", 1), ("ukv", 0)]
    t += [("wo", c) for c in range(4)]
    t += [("pq", c) for c in range(8)] + [("sk", 0)]
    t += [("u", c) for c in range(UT)]
    t += [("ada", c) for c in range(NADA // 2)]
    t += [("v", c) for c in range(UT)]
    t += [("ek", c) for c in range(3)] + [("ev", c) for c in range(3)]
    t += [("eq", c) for c in range(3)] + [("ef", 0)]
    t += [("eo", c) for c in range(4)]
    for layer in range(2):
        if layer:
            t += [("pw1", c) for c in range(8)] + [("pw2", c) for c in range(4)]
        for f in range(0, NF, 2):
            t += [("up", layer, f), ("up", layer, f + 1), ("down", layer, f), ("down", layer, f + 1)]
    return t


def sb_order():
    for i in range(H1 + 2):
        if i < H1:
            yield "z", i
        if 1 <= i <= H1:
            yield "t", i - 1
        if i >= 2:
            yield "o", i - 2


def mla_order():
    for i in range(H1 + 4):
        if i < H1:
            yield "qkT", i
        if 1 <= i <= H1:
            yield "s", i - 1
        if 3 <= i < H1 + 3:
            yield "pT", i - 3
        if i >= 4:
            yield "mo", i - 4


def diff_order():
    for i in range(2 * H2 + 3):
        if i < 2 * H2:
            yield "s2", i
        if 2 <= i < 2 * H2 + 2:
            yield "aT", i - 2
        if i >= 3 and i % 2 == 0:
            yield "o2", (i - 4) // 2


def plan_groups():
    g = [("lam",), ("norm", 0)] + [("in", c) for c in range(9)]
    for what, h in sb_order():
        if what == "o":
            if h % 2 == 0:
                g.append(("o", h // 2))
        else:
            g.append((what, h))
    g += [("norm", 1), ("norm", 2), ("norm", 3)]
    g += [("uq", tb, hf) for hf in range(2) for tb in range(TB)]
    g += [("ukv", tb, hf) for hf in range(2) for tb in range(TB)]
    for what, h in mla_order():
        if what == "mo":
            if h % 2 == 0:
                g.append(("mo", h // 2))
        else:
            g.append((what, h))
    g += [("norm", 4)] + [("wo", c) for c in range(4)]
    g += [("norm", 5)] + [("pq", c) for c in range(8)]
    g += [("ss", tb, q) for tb in range(TB) for q in range(4)]
    g += [("u", c) for c in range(UT)]
    g += [("rt", 0), ("rt", 1)]
    g += [("g", c) for c in range(T // GB)]
    g += [("norm", 6), ("norm", 7)]
    for c in range(3):
        g += [("k", c), ("kc", c)]
    for c in range(3):
        g += [("v2", c), ("vc", c)]
    g += [("q", c) for c in range(3)] + [("f", 0), ("fy", 0), ("fy", 1), ("fz", 0), ("fw", 0)]
    for what, i in diff_order():
        if what == "s2":
            g += [("s2", i, 0), ("s2", i, 1)]
        else:
            g.append((what, i))
    g += [("sn", p) for p in range(3)] + [("eo", c) for c in range(4)]
    g.append(("norm", 8))
    g += [(x, 0, f) for f in range(NF) for x in ("fa", "fb")]
    g.append(("norm", 9))
    g += [("pw1", c) for c in range(8)]
    g += [("mean", 0), ("norm", 10)] + [("pw2", c) for c in range(4)]
    g.append(("norm", 11))
    g += [(x, 1, f) for f in range(NF) for x in ("fa", "fb")]
    g.append(("norm", 12))
    return g


TILES = plan_tiles()
GROUPS = plan_groups()
TILE_NO = {name: n for n, name in enumerate(TILES)}
GROUP_NO = {name: n for n, name in enumerate(GROUPS)}
assert len(TILE_NO) == len(TILES) and len(GROUP_NO) == len(GROUPS)

PARAMS = [("attn_norm", 8), ("cq_norm", 3), ("ckv_norm", 2), ("sb_out_norm", 4), ("mla_out_norm", 4),
          ("ffn_norm", 8), ("ada_b", 96), ("mix_norm_g", 16), ("ffn_norm_g", 16), ("subln", 1),
          ("pw1_b", 16), ("dw_w", 8 * CONV), ("dw_b", 8), ("ln_g", 8), ("ln_b", 8), ("pw2_b", 8),
          ("final_g", 8), ("cc", 16), ("lambdas", 4), ("q_norm", 96), ("k_norm", 96), ("fw", 128)]
CONSTS = [("ident", 128), ("ones", 128), ("iota", 128), ("ntri", 128), ("nones", 128),
          ("mask", ATT), ("invf", 16)]
CONSTS2 = [("cos", T), ("sin", T), ("dc", 128), ("ds", 128), ("ct", 2 * T), ("nst", 2 * T)]


def offsets(table):
    at, out = 0, {}
    for name, n in table:
        out[name] = (at, at + n)
        at += n
    return out, at


def build(nc, d):
    with ExitStack() as ctx:
        def sb(name, shape, dt=F32):
            return ctx.enter_context(nc.sbuf_tensor(name, shape, dt))

        def sem(name):
            return ctx.enter_context(nc.semaphore(name))

        ring = sb("ring", [P, NS, SLOT])
        arena = sb("arena", [P, J * T])
        x = sb("x", [P, KC, T])
        h = sb("h", [P, KC, T])
        sq = sb("sq", [P, 2048])
        po, pn = offsets(PARAMS)
        co, cn = offsets(CONSTS)
        prm = sb("prm", [P, pn])
        cst = sb("cst", [P, cn])
        pos_i = sb("pos_i", [P, TB], I32)
        ms = sb("ms", [P, T])
        rms = sb("rms", [P, T])
        rinv = sb("rinv", [P, T])
        rT = sb("rT", [P, 3, T])
        ada = sb("ada", [P, NADA, 2])
        gsc = sb("gsc", [P, 5, KC])
        csil = sb("csil", [P, KC, 2])
        small = sb("small", [P, 64])
        stat = sb("stat", [P, 2, 8])
        psr = [ctx.enter_context(nc.psum_tensor(f"psr{i}", [P, 512], F32)) for i in range(NB)]
        acc = [ctx.enter_context(nc.psum_tensor(f"acc{i}", [P, 512], F32)) for i in range(4)]

        def par(name):
            return prm[:, po[name][0]:po[name][1]]

        def con(name):
            return cst[:, co[name][0]:co[name][1]]

        ident, ones, iota = con("ident"), con("ones"), con("iota")
        ntri, nones, mask = con("ntri"), con("nones"), con("mask")

        def cut(spec, base=0):
            out, at = {}, base
            for name, n in spec:
                out[name] = arena[:, at:at + n]
                at += n
            assert at <= J * T, at
            return out

        a1 = cut([("sbq", 1024), ("sbk", 1024), ("sbv", 1024), ("cq", 768), ("ckv", 512), ("kpe", 64),
                  ("az", 2 * ATT), ("sp", 2 * ATT), ("spm", 2 * ATT), ("dd", 2 * ATT), ("la", 2 * ATT),
                  ("pa", 2 * ATT), ("sbT", 1024), ("mlaT", 1024), ("mixed", 2048),
                  ("cqn", 768), ("ckvn", 512), ("qt", 1536), ("kt", 1536), ("vt", 1024),
                  ("qkT", 4096), ("E", 2 * ATT), ("PT", 2 * ATT), ("tsq", 1536), ("rope", 6 * 256)])
        sbq = a1["sbq"].rearrange("p (c t) -> p c t", t=T)
        sbk = a1["sbk"].rearrange("p (c t) -> p c t", t=T)
        sbv = a1["sbv"].rearrange("p (b n) -> p b n", b=TB)
        cq = a1["cq"].rearrange("p (c t) -> p c t", t=T)
        ckv = a1["ckv"].rearrange("p (c t) -> p c t", t=T)
        kpe = a1["kpe"].rearrange("p (b n) -> p b n", b=TB)
        cqn = a1["cqn"].rearrange("p (c t) -> p c t", t=T)
        ckvn = a1["ckvn"].rearrange("p (c t) -> p c t", t=T)
        two = {k: a1[k].rearrange("p (b n) -> p b n", b=2) for k in ("az", "sp", "spm", "dd", "la", "pa", "E", "PT")}
        sbT = a1["sbT"].rearrange("p (c t) -> p c t", t=T)
        mlaT = a1["mlaT"].rearrange("p (c t) -> p c t", t=T)
        mixed = a1["mixed"].rearrange("p (c t) -> p c t", t=T)
        qt = a1["qt"].rearrange("p (b h e) -> p b h e", b=TB, h=H1)
        kt = a1["kt"].rearrange("p (b h e) -> p b h e", b=TB, h=H1)
        vt = a1["vt"].rearrange("p (b h e) -> p b h e", b=TB, h=H1)
        qkT = a1["qkT"].rearrange("p (h n) -> p h n", h=H1)
        tsq = a1["tsq"].rearrange("p (n e) -> p n e", e=QKD)
        rope_t = a1["rope"].rearrange("p (k n) -> p k n", k=6)

        a2 = cut([("qT", 4096), ("sc", 4096), ("cand", 2048), ("oh", 2048)], base=J * T // 2)
        qT = a2["qT"].rearrange("p (m t) -> p m t", t=T)
        sc = a2["sc"].rearrange("p (b m n) -> p b m n", b=TB, n=NKEY)
        cand = a2["cand"].rearrange("p (h n) -> p h n", h=PH)
        oh = a2["oh"].rearrange("p (n a) -> p n a", a=TOPK)
        r_s = sb("r_s", [P, 16, TOPK])
        r_iu = sb("r_iu", [P, 16, TOPK], U32)
        r_i = sb("r_i", [P, 16, TOPK])
        r_b = sb("r_b", [P, PH, TOPK])
        r_bu = sb("r_bu", [P, PH, TOPK], U32)
        r_ab = sb("r_ab", [P, 2, PH * TOPK])
        r_au = sb("r_au", [P, 2, PH * TOPK], U32)
        r_out = sb("r_out", [P, TB, 3, PH * TOPK])
        gelu = arena[:, :].rearrange("p (j t) -> p j t", t=T)
        oneA = sq[:, 0:2 * GB * P].rearrange("p (b g n) -> p b g n", b=2, g=GB)
        oneB = sq[:, 1024:1024 + 2 * GB * P].rearrange("p (b g n) -> p b g n", b=2, g=GB)

        c2o, c2n = offsets(CONSTS2)
        a3 = cut([("cst2", c2n), ("ctx", 2048), ("hc", 2048), ("kall", H2 * S2), ("vall", 4 * H2 * VD),
                  ("qf", H2 * T), ("rot", H2 * T), ("fT", 2 * T), ("Y", TB * 512), ("ZT", 2 * T),
                  ("E0", 2 * S2), ("E1", 2 * S2), ("aT", 4 * T), ("oT", H2 * T), ("osq", H2 * T),
                  ("orn", H2 * T), ("mix2", 2048), ("fs", 2 * T), ("fg", 2 * T)])
        c2 = {k: a3["cst2"][:, a:b] for k, (a, b) in c2o.items()}
        ctxT = a3["ctx"].rearrange("p (c t) -> p c t", t=T)
        hc = a3["hc"].rearrange("p (c t) -> p c t", t=T)
        kall = a3["kall"].rearrange("p (h s) -> p h s", h=H2)
        vall = a3["vall"].rearrange("p (s n) -> p s n", s=4)
        qf = a3["qf"].rearrange("p (h t) -> p h t", h=H2)
        rot = a3["rot"].rearrange("p (h t) -> p h t", h=H2)
        fT = a3["fT"].rearrange("p (c t) -> p c t", c=2)
        Y = a3["Y"].rearrange("p (b n) -> p b n", b=TB)
        ZT = a3["ZT"].rearrange("p (c t) -> p c t", c=2)
        E01 = [a3[k].rearrange("p (b s) -> p b s", b=2) for k in ("E0", "E1")]
        aT = a3["aT"].rearrange("p (s t) -> p s t", s=4)
        oT = a3["oT"].rearrange("p (h t) -> p h t", h=H2)
        mix2 = a3["mix2"].rearrange("p (c t) -> p c t", t=T)
        fs = a3["fs"].rearrange("p (b t) -> p b t", b=2)
        fg = a3["fg"].rearrange("p (b t) -> p b t", b=2)
        a4 = cut([("up", KC * (T + 2 * PADL)), ("cv", 2048), ("cv2", 2048), ("xc", 2048), ("sig", 512)], base=c2n + 4096)
        upad = a4["up"].rearrange("p (c n) -> p c n", c=KC)
        cv = a4["cv"].rearrange("p (c t) -> p c t", t=T)
        cv2 = a4["cv2"].rearrange("p (c t) -> p c t", t=T)
        xc = a4["xc"].rearrange("p (c t) -> p c t", t=T)
        csig = a4["sig"].rearrange("p (b t) -> p b t", b=2)

        tile_ready = [sem(f"tile_ready{i}") for i in range(NS)]
        bank_full = [sem(f"bank_full{i}") for i in range(NB)]
        bank_drained = [sem(f"bank_drained{i}") for i in range(NB)]
        x_loaded = sem("x_loaded")
        small_loaded = sem("small_loaded")
        late_loaded = sem("late_loaded")
        out_stored = sem("out_stored")
        act_step, dve_step, pool_step = sem("act_step"), sem("dve_step"), sem("pool_step")
        squares = sem("squares")
        root = sem("root")
        normed = sem("normed")
        lam_in = sem("lam_in")
        lam_exp = sem("lam_exp")
        angles = sem("angles")
        sincos = sem("sincos")
        log_part = sem("log_part")
        fails = sem("fails")
        weights_in = sem("weights_in")
        sb_probs = sem("sb_probs")
        head_ms = sem("head_ms")
        head_root = sem("head_root")
        qk_ready = sem("qk_ready")
        neg_max = sem("neg_max")
        probs = sem("probs")
        c_silu = sem("c_silu")
        router_max = sem("router_max")
        router_exp = sem("router_exp")
        routed = sem("routed")
        one_hot = sem("one_hot")
        ada_used = sem("ada_used")
        ada_ready = sem("ada_ready")
        v_used = sem("v_used")
        x_added = sem("x_added")
        rotated = sem("rotated")
        neg_max2 = sem("neg_max2")
        diff_probs = sem("diff_probs")
        o_squares = sem("o_squares")
        o_root = sem("o_root")
        mixed2 = sem("mixed2")
        down_used = sem("down_used")
        conv_sum = sem("conv_sum")
        centred = sem("centred")
        silued = sem("silued")
        final = sem("final")
        half_out = sem("half_out")
        gates = sem("gates")
        padded = sem("padded")

        def use(n, k):
            return n % k, n // k

        def full(eng, name):
            b, u = use(GROUP_NO[name], NB)
            eng.wait_ge(bank_full[b], u + 1)
            return psr[b]

        def drains(ins, name):
            return ins.then_inc(bank_drained[GROUP_NO[name] % NB], 1)

        def drained(eng, name):
            b, u = use(GROUP_NO[name], NB)
            eng.wait_ge(bank_drained[b], u + 1)

        def sm(b, k):
            return stat[:, b, k:k + 1]

        def pair_done(eng, name, base, hd):
            if hd % 2 == 0:
                eng.wait_ge(half_out, base + hd // 2 + 1)
            else:
                full(eng, (name, hd // 2))

        class Steps:

            def __init__(self, eng, s):
                self.eng, self.s, self.n = eng, s, 0

            def do(self, ins):
                ins.then_inc(self.s, 1)
                self.n += 1
                self.eng.wait_ge(self.s, self.n)

        X_ADDS = {"peer": 4, "ffn0": 12, "pw2": 13, "ffn1": 21}
        block = ctx.enter_context(nc.Block())

        @block.sync
        def _(sp):
            src = {"in": d["w_in"], "uq": d["w_uq"], "ukv": d["w_ukv"], "wo": d["w_o"], "pq": d["w_q"],
                   "sk": d["sub_keys"], "u": d["peer_u"], "ada": d["ada_w"], "v": d["peer_v"],
                   "ek": d["ev_k"], "ev": d["ev_v"], "eq": d["ev_q"], "ef": d["ev_f"], "eo": d["ev_o"],
                   "pw1": d["pw1"], "pw2": d["pw2"]}
            last_group = {("uq", 0): ("uq", 1, 0), ("uq", 1): ("uq", 1, 1), ("ukv", 0): ("ukv", 1, 1),
                          ("sk", 0): ("ss", 1, 3), ("ef", 0): ("f", 0)}
            for c in range(3):
                last_group["ek", c], last_group["ev", c], last_group["eq", c] = ("kc", c), ("vc", c), ("q", c)

            def released(n):
                name = TILES[n]
                if name[0] == "ada":
                    sp.wait_ge(ada_used, name[1] + 1)
                elif name[0] == "v":
                    sp.wait_ge(v_used, name[1] + 1)
                elif name[0] == "down":
                    sp.wait_ge(down_used, NF * name[1] + name[2] + 1)
                else:
                    if name[0] == "up":
                        name = ("fb", *name[1:])
                    full(sp, last_group.get(name, name))

            def load(n):
                name = TILES[n]
                if n >= NS:
                    released(n - NS)
                if name[0] in ("up", "down"):
                    a = d[f"ffn_{name[0]}"][name[1], name[2]]
                else:
                    a = src[name[0]][name[1]]
                sp.dma_start(ring[:, n % NS, 0:a.shape[1]], a).then_inc(tile_ready[n % NS], 16)

            sp.dma_start(x[:, :, :], d["x"]).then_inc(x_loaded, 16)
            sp.dma_start(cst[:, :], d["consts"]).then_inc(small_loaded, 16)
            sp.dma_start(prm[:, :], d["params"]).then_inc(small_loaded, 16)
            sp.dma_start(pos_i[:, :], d["positions"]).then_inc(small_loaded, 16)
            n = 0
            while n < len(TILES):
                name = TILES[n]
                load(n)
                n += 1
                kind = name[0]
                if kind in ("u", "v", "ada") and name[1] == NS - 1:
                    count = (UT if kind != "ada" else NADA // 2) // NS - 1
                    g0 = GROUP_NO["u", 0]
                    with sp.Fori(0, count) as it:
                        for i in range(NS):
                            if kind == "u":
                                b, u = use(g0 + i, NB)
                                sp.wait_ge(bank_full[b], it + (u + 1))
                            else:
                                sp.wait_ge(ada_used if kind == "ada" else v_used, it * NS + (i + 1))
                            s = (n - NS + i) % NS
                            sp.dma_start(ring[:, s, :], src[kind][it * NS + (NS + i)]).then_inc(tile_ready[s], 16)
                    n += NS * count
                if kind == "down" and name[2] == 1:
                    layer = name[1]
                    g0 = GROUP_NO["fa", layer, 0]
                    count = NF // 2 - 1
                    with sp.Fori(0, count) as it:
                        for i in range(4):
                            s = (n - NS + i) % NS
                            if i < 2:
                                b, u = use(g0 + 2 * i + 1, NB)
                                sp.wait_ge(bank_full[b], it + (u + 1))
                                a = d["ffn_up"][layer, it * 2 + (2 + i)]
                            else:
                                sp.wait_ge(down_used, it * 2 + (NF * layer + i - 1))
                                a = d["ffn_down"][layer, it * 2 + i]
                            sp.dma_start(ring[:, s, 0:a.shape[1]], a).then_inc(tile_ready[s], 16)
                    n += 4 * count
            sp.wait_ge(final, 1)
            sp.dma_start(d["out"], h[:, :, :]).then_inc(out_stored, 16)
            sp.wait_ge(out_stored, 16)

        @block.tensor
        def _(pe):
            mm = nc.tensor.matmul
            at = [0]

            def bank(name):
                assert GROUPS[at[0]] == name, (GROUPS[at[0]], name)
                b, u = use(at[0], NB)
                at[0] += 1
                if u:
                    pe.wait_ge(bank_drained[b], u)
                return psr[b]

            def fills(ins, name):
                ins.then_inc(bank_full[GROUP_NO[name] % NB], 1)

            def tile(*name):
                s, u = use(TILE_NO[name], NS)
                pe.wait_ge(tile_ready[s], 16 * (u + 1))
                return ring[:, s, :]

            def norm(k, n, src=None):
                ps = bank(("norm", k))
                pe.wait_ge(squares, k + 1)
                for c in range(n):
                    last = mm(ps[:, 0:T], ones, sq[:, c * T:(c + 1) * T], start=(c == 0), stop=(c == n - 1))
                fills(last, ("norm", k))

            def features(ps, w, src, chunks, kc=KC):
                for m in chunks:
                    for k in range(kc):
                        last = mm(ps[:, m * T:(m + 1) * T], w[:, k, m * P:(m + 1) * P], src[:, k, :],
                                  start=(k == 0), stop=(k == kc - 1))
                return last

            def tokens(ps, w, src, kc=KC, n=T, col=0):
                for tb in range(TB):
                    for k in range(kc):
                        last = mm(ps[:, col + tb * n:col + (tb + 1) * n], src[:, k, tb * P:(tb + 1) * P],
                                  w[:, k, :], start=(k == 0), stop=(k == kc - 1))
                return last

            def w8(t):
                return t.rearrange("p (k n) -> p k n", k=KC)

            pe.wait_ge(small_loaded, 48)
            ps = bank(("lam",))
            pe.wait_ge(lam_in, 1)
            fills(mm(ps[:, 0:2], ones[0:64, :], small[0:64, 0:2], start=True, stop=True), ("lam",))

            norm(0, KC)
            pe.wait_ge(normed, 1)
            for c in range(9):
                ps = bank(("in", c))
                w = w8(tile("in", c))
                if c in (4, 5):
                    last = tokens(ps, w, h)
                elif c < 8:
                    last = features(ps, w, h, (0, 1))
                else:
                    features(ps, w, h, (0,))
                    last = tokens(ps, w[:, :, P:P + ROPE], h, n=ROPE, col=T)
                fills(last, ("in", c))

            drained(pe, ("in", 3))
            drained(pe, ("in", 5))
            for what, hd in sb_order():
                r = 64 * (hd % 2)
                c = hd // 2
                if what == "z":
                    ps = bank(("z", hd))
                    mm(ps[:, 0:T], sbk[r:r + 64, c, 0:P], sbq[r:r + 64, c, :], start=True, stop=True)
                    fills(mm(ps[:, T:ATT], sbk[r:r + 64, c, P:T], sbq[r:r + 64, c, P:T], start=True, stop=True),
                          ("z", hd))
                elif what == "t":
                    ps = bank(("t", hd))
                    pe.wait_ge(fails, hd + 1)
                    f = two["spm"][:, hd % 2, :]
                    mm(ps[:, 0:T], ntri, f[:, 0:T], start=True, stop=False, skip_group_check=True)
                    mm(ps[:, P:T], nones, f[:, T:ATT], start=False, stop=False, skip_group_check=True)
                    fills(mm(ps[:, T:ATT], ntri, f[:, T:ATT], start=False, stop=True, skip_group_check=True),
                          ("t", hd))
                else:
                    if hd % 2 == 0:
                        ps_o = bank(("o", c))
                    pe.wait_ge(sb_probs, hd + 1)
                    a = two["pa"][:, hd % 2, :]
                    o = ps_o[r:r + 64, 0:T]
                    mm(o, sbv[:, 0, 64 * hd:64 * hd + 64], a[:, 0:T], start=True, stop=False, skip_group_check=True)
                    last = mm(ps_o[r:r + 64, P:T], sbv[:, 1, 64 * hd:64 * hd + 64], a[:, T:ATT],
                              start=False, stop=True, skip_group_check=True)
                    if hd % 2:
                        fills(last, ("o", c))
                    else:
                        last.then_inc(half_out, 1)

            norm(1, 3)
            norm(2, 2)
            norm(3, 4)
            pe.wait_ge(normed, 3)
            for hf in range(2):
                w = tile("uq", hf)[:, 0:3 * 384].rearrange("p (k n) -> p k n", k=3)
                for tb in range(TB):
                    ps = bank(("uq", tb, hf))
                    for k in range(3):
                        last = mm(ps[:, 0:384], cqn[:, k, tb * P:(tb + 1) * P], w[:, k, :],
                                  start=(k == 0), stop=(k == 2))
                    fills(last, ("uq", tb, hf))
            w = tile("ukv", 0).rearrange("p (k n) -> p k n", k=2)
            for hf in range(2):
                for tb in range(TB):
                    ps = bank(("ukv", tb, hf))
                    for k in range(2):
                        last = mm(ps[:, :], ckvn[:, k, tb * P:(tb + 1) * P], w[:, k, hf * 512:(hf + 1) * 512],
                                  start=(k == 0), stop=(k == 1))
                    fills(last, ("ukv", tb, hf))
            pe.wait_ge(qk_ready, 2)
            for what, hd in mla_order():
                r = 64 * (hd % 2)
                if what == "qkT":
                    ps = bank(("qkT", hd))
                    for n, src in enumerate((qt, kt)):
                        for tb in range(TB):
                            at_ = (2 * n + tb) * P
                            last = nc.tensor.transpose(ps[0:QKD, at_:at_ + P], src[:, tb, hd, :], ident)
                    fills(last, ("qkT", hd))
                elif what == "s":
                    ps = bank(("s", hd))
                    drained(pe, ("qkT", hd))
                    w = qkT[0:QKD, hd, :]
                    mm(ps[:, 0:P], w[:, 0:P], w[:, T:T + P], start=True, stop=True)
                    fills(mm(ps[:, P:ATT], w[:, P:T], w[:, T:2 * T], start=True, stop=True), ("s", hd))
                elif what == "pT":
                    ps = bank(("pT", hd))
                    pe.wait_ge(probs, hd + 1)
                    for n in range(3):
                        last = nc.tensor.transpose(ps[:, n * P:(n + 1) * P], two["E"][:, hd % 2, n * P:(n + 1) * P],
                                                   ident)
                    fills(last, ("pT", hd))
                else:
                    if hd % 2 == 0:
                        ps_o = bank(("mo", hd // 2))
                    drained(pe, ("pT", hd))
                    a = two["PT"][:, hd % 2, :]
                    mm(ps_o[r:r + 64, 0:T], vt[:, 0, hd, :], a[:, 0:T], start=True, stop=False,
                       skip_group_check=True)
                    last = mm(ps_o[r:r + 64, P:T], vt[:, 1, hd, :], a[:, T:ATT], start=False, stop=True,
                              skip_group_check=True)
                    if hd % 2:
                        fills(last, ("mo", hd // 2))
                    else:
                        last.then_inc(half_out, 1)
            norm(4, 4)
            pe.wait_ge(normed, 5)
            for c in range(4):
                ps = bank(("wo", c))
                fills(features(ps, w8(tile("wo", c)), mixed, (0, 1)), ("wo", c))

            norm(5, KC)
            pe.wait_ge(normed, 6)
            for c in range(8):
                ps = bank(("pq", c))
                fills(features(ps, w8(tile("pq", c)), h, (0, 1)), ("pq", c))
            w = tile("sk", 0).rearrange("p (m n) -> p m n", n=NKEY)
            drained(pe, ("pq", 6))
            drained(pe, ("pq", 7))
            for tb in range(TB):
                for q in range(4):
                    ps = bank(("ss", tb, q))
                    for m in range(4):
                        last = mm(ps[:, m * P:(m + 1) * P], qT[:, 4 * q + m, tb * P:(tb + 1) * P],
                                  w[:, 4 * q + m, :], start=True, stop=True)
                    fills(last, ("ss", tb, q))
            t0, g0 = TILE_NO["u", 0], GROUP_NO["u", 0]
            with pe.Fori(0, UT // NS) as it:
                for i in range(NS):
                    s, u = use(t0 + i, NS)
                    b, ub = use(g0 + i, NB)
                    pe.wait_ge(tile_ready[s], it * 16 + 16 * (u + 1))
                    pe.wait_ge(bank_drained[b], it + ub)
                    w = ring[:, s, :].rearrange("p (j k n) -> p j k n", j=2, k=KC)
                    for j in range(2):
                        for k in range(KC):
                            last = mm(psr[b][:, j * T:(j + 1) * T], w[:, j, k, :], h[:, k, :],
                                      start=(k == 0), stop=(k == KC - 1))
                    last.then_inc(bank_full[b], 1)
            at[0] += UT
            pe.wait_ge(routed, 2)
            for n in range(2):
                ps = bank(("rt", n))
                for q in range(3):
                    last = nc.tensor.transpose(ps[:, q * P:(q + 1) * P], r_out[:, n, q, :], ident)
                fills(last, ("rt", n))
            pe.wait_ge(c_silu, 1)
            t0, g0 = TILE_NO["ada", 0], GROUP_NO["g", 0]
            per = T // GB // 4
            with pe.Fori(0, 4) as it:
                m = 0
                for q in range(per):
                    b, ub = use(g0 + q, NB)
                    pe.wait_ge(bank_drained[b], it * (per // NB) + ub)
                    pe.wait_ge(one_hot, it * per + (q + 1))
                    for g in range(GB):
                        last = mm(psr[b][:, g * P:(g + 1) * P], oneA[:, q % 2, g, :], oneB[:, q % 2, g, :],
                                  start=True, stop=True)
                    last.then_inc(bank_full[b], 1)
                    if q % 4 < 3:
                        s, u = use(t0 + m, NS)
                        pe.wait_ge(tile_ready[s], it * 48 + 16 * (u + 1))
                        w = w8(ring[:, s, :])
                        for c in range(2):
                            for k in range(KC):
                                last = mm(acc[0][:, bass.ds(it * 48 + (2 * m + c) * 2, 2)],
                                          w[:, k, c * P:(c + 1) * P], csil[:, k, :],
                                          start=(k == 0), stop=(k == KC - 1))
                        last.then_inc(ada_used, 1)
                        m += 1
            at[0] += T // GB
            pe.wait_ge(ada_ready, 1)
            drained(pe, ("g", T // GB - 1))
            drained(pe, ("g", T // GB - 2))
            t0 = TILE_NO["v", 0]

            def expert_out(i, it, first=False, last_one=False):
                s, u = use(t0 + i, NS)
                pe.wait_ge(tile_ready[s], it * 16 + 16 * (u + 1))
                w = ring[:, s, :].rearrange("p (j n) -> p j n", j=2)
                for j in range(2):
                    for c in range(KC):
                        ins = mm(acc[c // 2][:, (c % 2) * T:(c % 2 + 1) * T], w[:, j, c * P:(c + 1) * P],
                                 arena[:, bass.ds(it * (8 * T) + (2 * i + j) * T, T)],
                                 start=(first and j == 0 and c % 2 == 0), stop=(last_one and j == 1),
                                 skip_group_check=True)
                ins.then_inc(v_used, 1)

            for i in range(NS):
                expert_out(i, 0, first=(i == 0))
            with pe.Fori(1, UT // NS - 1) as it:
                for i in range(NS):
                    expert_out(i, it)
            for i in range(NS):
                expert_out(i, UT // NS - 1, last_one=(i == NS - 1))

            norm(6, KC)
            norm(7, KC)
            pe.wait_ge(normed, 8)
            for c in range(3):
                w = w8(tile("ek", c))
                ps = bank(("k", c))
                fills(features(ps, w, h, (0, 1)), ("k", c))
                ps = bank(("kc", c))
                fills(features(ps, w, hc, (0, 1)), ("kc", c))
            for c in range(3):
                w = w8(tile("ev", c))
                ps = bank(("v2", c))
                fills(tokens(ps, w, h), ("v2", c))
                ps = bank(("vc", c))
                fills(tokens(ps, w, hc), ("vc", c))
            for c in range(3):
                ps = bank(("q", c))
                fills(features(ps, w8(tile("eq", c)), h, (0, 1)), ("q", c))
            ps = bank(("f", 0))
            fills(features(ps, w8(tile("ef", 0)), h, (0, 1)), ("f", 0))
            drained(pe, ("f", 0))
            for tb in range(TB):
                ps = bank(("fy", tb))
                for n, m in enumerate(("dc", "ds")):
                    for c in range(2):
                        last = mm(ps[:, (2 * n + c) * P:(2 * n + c + 1) * P], fT[:, c, tb * P:(tb + 1) * P], c2[m],
                                  start=True, stop=True)
                fills(last, ("fy", tb))
            ps = bank(("fz", 0))
            drained(pe, ("fy", 0))
            drained(pe, ("fy", 1))
            for c in range(2):
                for n, m in enumerate(("ct", "nst")):
                    for tb in range(TB):
                        last = mm(ps[:, c * T:(c + 1) * T], Y[:, tb, (2 * n + c) * P:(2 * n + c + 1) * P],
                                  c2[m][:, tb * T:(tb + 1) * T], start=(n + tb == 0), stop=(n + tb == 2))
            fills(last, ("fz", 0))
            ps = bank(("fw", 0))
            drained(pe, ("fz", 0))
            fw = par("fw").rearrange("p (c n) -> p c n", c=2)
            for g in range(4):
                r, c = 64 * (g % 2), g // 2
                last = mm(ps[r:r + 64, c * T:(c + 1) * T], fw[r:r + 64, c, :], ZT[r:r + 64, c, :],
                          start=True, stop=True)
            fills(last, ("fw", 0))
            pe.wait_ge(rotated, 2)
            for what, i in diff_order():
                hd, tb = i // 2, i % 2
                if what == "s2":
                    for c in range(2):
                        ps = bank(("s2", i, c))
                        fills(mm(ps[:, :], qf[64 * c:64 * c + 64, hd, tb * P:(tb + 1) * P],
                                 kall[64 * c:64 * c + 64, hd, :], start=True, stop=True), ("s2", i, c))
                elif what == "aT":
                    ps = bank(("aT", i))
                    pe.wait_ge(diff_probs, i + 1)
                    for s in range(4):
                        last = nc.tensor.transpose(ps[:, s * P:(s + 1) * P], E01[0][:, i % 2, s * P:(s + 1) * P],
                                                   ident)
                    fills(last, ("aT", i))
                else:
                    ps = bank(("o2", i))
                    drained(pe, ("aT", 2 * i))
                    drained(pe, ("aT", 2 * i + 1))
                    for s in range(4):
                        last = mm(ps[:, 0:T], vall[:, s, i * VD:(i + 1) * VD], aT[:, s, :],
                                  start=(s == 0), stop=(s == 3))
                    fills(last, ("o2", i))
            pe.wait_ge(o_squares, 1)
            for p_ in range(3):
                ps = bank(("sn", p_))
                fills(mm(ps[:, :], ones, a3["osq"][:, p_ * 512:(p_ + 1) * 512], start=True, stop=True), ("sn", p_))
            pe.wait_ge(mixed2, 1)
            drained(pe, ("fw", 0))
            for c in range(4):
                ps = bank(("eo", c))
                fills(features(ps, w8(tile("eo", c)), mix2, (0, 1)), ("eo", c))

            def ffn(layer):
                t0, g0 = TILE_NO["up", layer, 0], GROUP_NO["fa", layer, 0]

                def pair(it, first=False, final_one=False):
                    for i in range(2):
                        s, u = use(t0 + i, NS)
                        pe.wait_ge(tile_ready[s], it * 16 + 16 * (u + 1))
                        w = w8(ring[:, s, :])
                        for n in range(2):
                            b, ub = use(g0 + 2 * i + n, NB)
                            pe.wait_ge(bank_drained[b], it + ub)
                            for k in range(KC):
                                last = mm(psr[b][:, 0:T], w[:, k, n * P:(n + 1) * P], h[:, k, :],
                                          start=(k == 0), stop=(k == KC - 1))
                            last.then_inc(bank_full[b], 1)
                    for i in range(2):
                        s, u = use(t0 + 2 + i, NS)
                        pe.wait_ge(tile_ready[s], it * 16 + 16 * (u + 1))
                        b, ub = use(g0 + 2 * i + 1, NB)
                        pe.wait_ge(bank_drained[b], it + (ub + 1))
                        for c in range(KC):
                            last = mm(acc[c // 2][:, (c % 2) * T:(c % 2 + 1) * T],
                                      ring[:, s, c * P:(c + 1) * P], fg[:, i, :],
                                      start=(first and i == 0 and c % 2 == 0),
                                      stop=(final_one and i == 1), skip_group_check=True)
                        last.then_inc(down_used, 1)

                pair(0, first=True)
                with pe.Fori(1, NF // 2 - 1) as it:
                    pair(it)
                pair(NF // 2 - 1, final_one=True)
                at[0] += 2 * NF

            norm(8, KC)
            pe.wait_ge(normed, 9)
            ffn(0)

            norm(9, KC)
            pe.wait_ge(normed, 10)
            for c in range(8):
                ps = bank(("pw1", c))
                fills(features(ps, w8(tile("pw1", c)), h, (0, 1)), ("pw1", c))
            ps = bank(("mean", 0))
            pe.wait_ge(conv_sum, 1)
            for c in range(KC):
                last = mm(ps[:, 0:T], ones, cv[:, c, :], start=(c == 0), stop=(c == KC - 1))
            fills(last, ("mean", 0))
            norm(10, KC)
            pe.wait_ge(silued, 1)
            for c in range(4):
                ps = bank(("pw2", c))
                fills(features(ps, w8(tile("pw2", c)), cv, (0, 1)), ("pw2", c))
            norm(11, KC)
            pe.wait_ge(normed, 12)
            ffn(1)
            norm(12, KC)
            assert at[0] == len(GROUPS)

        @block.scalar
        def _(act):
            st = Steps(act, act_step)
            A = nc.scalar.activation

            def norm(k, src, n, waits, prev=None):
                for s, v in waits:
                    if v is None:
                        drained(act, s)
                    else:
                        act.wait_ge(s, v)
                if prev is not None:
                    full(act, prev)
                A(sq[:, 0:n * T], src, ACT.Square).then_inc(squares, 1)

            def rootof(k):
                drained(act, ("norm", k))
                A(rms[:, :], ms[:, :], ACT.Sqrt).then_inc(root, 1)

            act.wait_ge(small_loaded, 48)
            norm(0, x[:, :, :], KC, [(x_loaded, 16)])
            rootof(0)
            A(csil[:, :, :], par("cc").rearrange("p (k n) -> p k n", k=KC), ACT.Silu).then_inc(c_silu, 1)
            ps = full(act, ("lam",))
            drains(A(small[:, 2:4], ps[:, 0:2], ACT.Exp), ("lam",))
            act.wait_ge(angles, 1)
            A(rope_t[:, 4, 0:64], rope_t[:, 3, 0:64], ACT.Sin).then_inc(sincos, 1)

            for c in range(9):
                ps = full(act, ("in", c))
                if c < 2:
                    ins = A(sbq[:, 2 * c:2 * c + 2, :], ps[:, :], ACT.Copy, scale=SBD ** -0.5)
                elif c < 4:
                    ins = A(sbk[:, 2 * c - 4:2 * c - 2, :], ps[:, :], ACT.Copy)
                elif c < 6:
                    ins = A(sbv[:, :, (c - 4) * T:(c - 3) * T], ps[:, :].rearrange("p (b n) -> p b n", b=TB), ACT.Copy)
                elif c == 6:
                    ins = A(cq[:, 0:2, :], ps[:, :], ACT.Copy)
                elif c == 7:
                    A(cq[:, 2, :], ps[:, 0:T], ACT.Copy).then_inc(act_step, 1)
                    st.n += 1
                    ins = A(ckv[:, 0, :], ps[:, T:2 * T], ACT.Copy)
                else:
                    A(ckv[:, 1, :], ps[:, 0:T], ACT.Copy).then_inc(act_step, 1)
                    st.n += 1
                    ins = A(kpe[:, :, :], ps[:, T:T + 64].rearrange("p (b n) -> p b n", b=TB), ACT.Copy)
                drains(ins, ("in", c))

            for i in range(H1 + 2):
                if i < H1:
                    b = i % 2
                    ps = full(act, ("z", i))
                    if i >= 2:
                        act.wait_ge(fails, i - 1)
                    az = two["az"][:, b, :]
                    st.do(A(az, ps[:, 0:ATT], ACT.Abs))
                    st.do(A(az, az, ACT.Exp, scale=-1.0))
                    A(az, az, ACT.Ln, bias=1.0).then_inc(log_part, 1)
                if 1 <= i <= H1:
                    hd = i - 1
                    drained(act, ("t", hd))
                    A(two["dd"][:, hd % 2, :], two["la"][:, hd % 2, :], ACT.Exp).then_inc(weights_in, 1)
                if i >= 2 and (i - 2) % 2 == 1:
                    c = (i - 2) // 2
                    ps = full(act, ("o", c))
                    drains(A(sbT[:, c, :], ps[:, 0:T], ACT.Copy), ("o", c))

            act.wait_ge(act_step, st.n)
            drained(act, ("in", 8))
            norm(1, cq[:, :, :], 3, [], prev=("norm", 0))
            rootof(1)
            norm(2, ckv[:, :, :], 2, [], prev=("norm", 1))
            rootof(2)
            drained(act, ("o", 3))
            norm(3, sbT[:, :, :], 4, [], prev=("norm", 2))
            rootof(3)
            for hf in range(2):
                for tb in range(TB):
                    ps = full(act, ("uq", tb, hf))
                    drains(A(qt[:, tb, 4 * hf:4 * hf + 4, :], ps[:, 0:384].rearrange("p (h e) -> p h e", h=4),
                             ACT.Copy), ("uq", tb, hf))
            for hf in range(2):
                for tb in range(TB):
                    ps = full(act, ("ukv", tb, hf))
                    kv = ps[:, :].rearrange("p (h e) -> p h e", h=4)
                    A(kt[:, tb, 4 * hf:4 * hf + 4, 0:NOPE], kv[:, :, 0:NOPE], ACT.Copy).then_inc(act_step, 1)
                    st.n += 1
                    drains(A(vt[:, tb, 4 * hf:4 * hf + 4, :], kv[:, :, NOPE:2 * NOPE], ACT.Copy), ("ukv", tb, hf))
            for n in range(2):
                act.wait_ge(head_ms, n + 1)
                A(small[:, 24 + 16 * n:40 + 16 * n], small[:, 8:24], ACT.Sqrt).then_inc(head_root, 1)
            for i in range(H1 + 4):
                if i < H1:
                    ps = full(act, ("qkT", i))
                    drains(A(qkT[0:QKD, i, :], ps[0:QKD, :], ACT.Copy), ("qkT", i))
                if 1 <= i <= H1:
                    hd = i - 1
                    b = hd % 2
                    ps = full(act, ("s", hd))
                    act.wait_ge(neg_max, hd + 1)
                    if hd >= 2:
                        full(act, ("pT", hd - 2))
                    for n, (lo, hi) in enumerate(((0, P), (P, ATT))):
                        ins = A(two["E"][:, b, lo:hi], ps[:, lo:hi], ACT.Exp, scale=QKD ** -0.5,
                                bias=sm(b, 2 + n), accum_out=sm(b, 4 + n))
                        if n == 0:
                            ins.then_inc(act_step, 1)
                            st.n += 1
                    drains(ins, ("s", hd))
                if 3 <= i < H1 + 3:
                    hd = i - 3
                    ps = full(act, ("pT", hd))
                    if hd >= 2:
                        pair_done(act, "mo", H1 // 2, hd - 2)
                    drains(A(two["PT"][:, hd % 2, :], ps[:, 0:ATT], ACT.Copy), ("pT", hd))
                if i >= 4 and (i - 4) % 2 == 1:
                    c = (i - 4) // 2
                    ps = full(act, ("mo", c))
                    drains(A(mlaT[:, c, :], ps[:, 0:T], ACT.Copy), ("mo", c))
            drained(act, ("mo", 3))
            norm(4, mlaT[:, :, :], 4, [], prev=("norm", 3))
            rootof(4)
            norm(5, x[:, :, :], KC, [(("wo", 3), None)], prev=("norm", 4))
            rootof(5)
            for c in range(8):
                ps = full(act, ("pq", c))
                drains(A(qT[:, 2 * c:2 * c + 2, :], ps[:, :], ACT.Copy), ("pq", c))
            for tb in range(TB):
                for q in range(4):
                    ps = full(act, ("ss", tb, q))
                    drains(A(sc[:, tb, 4 * q:4 * q + 4, :], ps[:, :].rearrange("p (m n) -> p m n", n=NKEY), ACT.Copy),
                           ("ss", tb, q))
            for tb in range(TB):
                act.wait_ge(router_max, tb + 1)
                A(r_b[:, :, :], r_b[:, :, :], ACT.Exp).then_inc(router_exp, 1)
            g0 = GROUP_NO["u", 0]

            def activate(it):
                for i in range(NB):
                    b, u = use(g0 + i, NB)
                    act.wait_ge(bank_full[b], it + (u + 1))
                    A(arena[:, bass.ds(it * (NB * 512) + i * 512, 512)], psr[b][:, :], ACT.Gelu)\
                        .then_inc(bank_drained[b], 1)

            with act.Fori(0, UT // NB // 2) as it:
                activate(it)
            act.wait_ge(routed, 2)
            with act.Fori(UT // NB // 2, UT // NB) as it:
                activate(it)
            for n in range(2):
                ps = full(act, ("rt", n))
                drains(A(rT[:, :, n * P:(n + 1) * P], ps[:, 0:3 * P].rearrange("p (q t) -> p q t", q=3), ACT.Copy),
                       ("rt", n))

            act.wait_ge(late_loaded, 32)
            norm(6, ctxT[:, :, :], KC, [(x_added, X_ADDS["peer"])], prev=("g", T // GB - 1))
            rootof(6)
            norm(7, x[:, :, :], KC, [], prev=("norm", 6))
            rootof(7)
            for c in range(3):
                ps = full(act, ("k", c))
                drains(A(kall[:, 2 * c:2 * c + 2, T:S2], ps[:, :].rearrange("p (h t) -> p h t", h=2), ACT.Copy), ("k", c))
                ps = full(act, ("kc", c))
                drains(A(kall[:, 2 * c:2 * c + 2, 0:T], ps[:, :].rearrange("p (h t) -> p h t", h=2), ACT.Copy), ("kc", c))
            for c in range(3):
                ps = full(act, ("v2", c))
                drains(A(vall[:, 2:4, c * T:(c + 1) * T], ps[:, :].rearrange("p (b n) -> p b n", b=2), ACT.Copy), ("v2", c))
                ps = full(act, ("vc", c))
                drains(A(vall[:, 0:2, c * T:(c + 1) * T], ps[:, :].rearrange("p (b n) -> p b n", b=2), ACT.Copy), ("vc", c))
            for c in range(3):
                ps = full(act, ("q", c))
                drains(A(qf[:, 2 * c:2 * c + 2, :], ps[:, :].rearrange("p (h t) -> p h t", h=2), ACT.Copy), ("q", c))
            ps = full(act, ("f", 0))
            drains(A(fT[:, :, :], ps[:, :].rearrange("p (h t) -> p h t", h=2), ACT.Copy), ("f", 0))
            for tb in range(TB):
                ps = full(act, ("fy", tb))
                drains(A(Y[:, tb, :], ps[:, :], ACT.Copy), ("fy", tb))
            ps = full(act, ("fz", 0))
            drains(A(ZT[:, :, :], ps[:, :].rearrange("p (h t) -> p h t", h=2), ACT.Copy), ("fz", 0))
            ps = full(act, ("fw", 0))
            drains(A(mix2[:, 6:8, :], ps[:, :].rearrange("p (h t) -> p h t", h=2), ACT.Copy), ("fw", 0))
            for i in range(2 * H2 + 3):
                if i < 2 * H2:
                    b = i % 2
                    act.wait_ge(neg_max2, i + 1)
                    for c in range(2):
                        ps = full(act, ("s2", i, c))
                        if i >= 2 and c == 0:
                            full(act, ("aT", i - 2))
                            act.wait_ge(diff_probs, i - 1)
                        drains(A(E01[c][:, b, :], ps[:, :], ACT.Exp, scale=SBD ** -0.5,
                                 bias=sm(b, 2 + c), accum_out=sm(b, 4 + c)), ("s2", i, c))
                if 2 <= i < 2 * H2 + 2:
                    n = i - 2
                    ps = full(act, ("aT", n))
                    if n >= 2:
                        full(act, ("o2", n // 2 - 1))
                    drains(A(aT[:, :, (n % 2) * P:(n % 2 + 1) * P], ps[:, :].rearrange("p (s t) -> p s t", s=4),
                             ACT.Copy), ("aT", n))
                if i >= 3 and i % 2 == 0:
                    hd = (i - 4) // 2
                    ps = full(act, ("o2", hd))
                    drains(A(oT[:, hd, :], ps[:, 0:T], ACT.Copy), ("o2", hd))
            drained(act, ("o2", H2 - 1))
            drained(act, ("o2", H2 - 2))
            A(a3["osq"], a3["oT"], ACT.Square).then_inc(o_squares, 1)
            for p_ in range(3):
                drained(act, ("sn", p_))
            A(a3["orn"], a3["osq"], ACT.Sqrt).then_inc(o_root, 1)

            def ffn(layer):
                g0 = GROUP_NO["fa", layer, 0]

                def pair(it, first=False):
                    for i in range(2):
                        b, u = use(g0 + 2 * i, NB)
                        act.wait_ge(bank_full[b], it + (u + 1))
                        if not first:
                            b2, u2 = use(g0 + 2 * i + 1, NB)
                            act.wait_ge(bank_drained[b2], it + u2)
                        A(fs[:, i, :], psr[b][:, 0:T], ACT.Silu).then_inc(bank_drained[b], 1)

                pair(0, first=True)
                with act.Fori(1, NF // 2) as it:
                    pair(it)

            norm(8, x[:, :, :], KC, [(("eo", 3), None)], prev=("norm", 7))
            rootof(8)
            ffn(0)
            norm(9, x[:, :, :], KC, [(x_added, X_ADDS["ffn0"])], prev=("norm", 8))
            rootof(9)
            pb = par("pw1_b")
            for c in range(8):
                ps = full(act, ("pw1", c))
                if c >= 2:
                    drained(act, ("pw1", c - 2))
                A(csig[:, c % 2, :], ps[:, T:2 * T], ACT.Sigmoid, bias=pb[:, 2 * c + 1:2 * c + 2]).then_inc(gates, 1)
            act.wait_ge(centred, 1)
            norm(10, xc[:, :, :], KC, [], prev=("norm", 9))
            rootof(10)
            act.wait_ge(normed, 11)
            A(cv[:, :, :], xc[:, :, :], ACT.Silu).then_inc(silued, 1)
            norm(11, x[:, :, :], KC, [(x_added, X_ADDS["pw2"])], prev=("norm", 10))
            rootof(11)
            ffn(1)
            norm(12, x[:, :, :], KC, [(x_added, X_ADDS["ffn1"])], prev=("norm", 11))
            rootof(12)

        @block.vector
        def _(dve):
            V = nc.vector
            st = Steps(dve, dve_step)
            TT, TS, STT = V.tensor_tensor, V.tensor_scalar, V.scalar_tensor_tensor

            def norm(k, n=D):
                ps = full(dve, ("norm", k))
                drains(TS(ms[:, :], ps[:, 0:T], 1.0 / n, EPS, ALU.mult, ALU.add), ("norm", k))
                dve.wait_ge(root, k + 1)
                st.do(V.reciprocal(rinv[:, :], rms[:, :]))

            def apply(src, dst, gain, n, signal):
                for c in range(n):
                    ins = STT(out=dst[:, c, :], in0=src[:, c, :], scalar=gain[:, c:c + 1], in1=rinv[:, :],
                              op0=ALU.mult, op1=ALU.mult)
                ins.then_inc(signal, 1)

            def modulate(src, dst, gain, shift, signal):
                st.do(TT(dst[:, :, :], src[:, :, :], rinv[:, :].unsqueeze(1).broadcast_to([P, KC, T]), ALU.mult))
                for c in range(KC):
                    ins = TS(dst[:, c, :], dst[:, c, :], gain[:, c:c + 1], shift[:, c:c + 1], ALU.mult, ALU.add)
                ins.then_inc(signal, 1)

            def mod(layer, part, col=0):
                a = 48 * layer + 8 * part
                return ada[:, a:a + 8, col]

            dve.wait_ge(small_loaded, 48)
            lam = par("lambdas")
            TT(small[0:64, 0:2], lam[0:64, 0:4:2], lam[0:64, 1:4:2], ALU.mult).then_inc(lam_in, 1)
            norm(0)
            dve.wait_ge(x_loaded, 16)
            apply(x, h, par("attn_norm"), KC, normed)
            drained(dve, ("lam",))
            st.do(TT(small[:, 4:5], small[:, 2:3], small[:, 3:4], ALU.subtract))
            st.do(TS(small[:, 5:6], small[:, 4:5], LAMBDA_INIT, None, ALU.add))
            lam_s = small[:, 5:6]
            st.do(TS(small[:, 6:7], par("subln"), 1.0 - LAMBDA_INIT, None, ALU.mult))
            subln = small[:, 6:7]
            pos, ang, turns, args = small[:, 56:58], rope_t[:, 0, 0:32], rope_t[:, 1, 0:32], rope_t[:, 3, 0:32]
            st.do(V.tensor_copy(pos, pos_i[:, :]))
            st.do(TT(ang.rearrange("p (b n) -> p b n", b=TB), con("invf").unsqueeze(1).broadcast_to([P, TB, 16]),
                     pos.unsqueeze(2).broadcast_to([P, TB, 16]), ALU.mult))
            st.do(TS(turns, ang, 1.0 / (2 * np.pi), ROUND, ALU.mult, ALU.add))
            st.do(TS(turns, turns, ROUND, None, ALU.subtract))
            c1 = 6.28125
            c2_ = float(np.float32(np.round((2 * np.pi - c1) * 2 ** 22) / 2 ** 22))
            c3 = float(2 * np.pi - c1 - c2_)
            for part in (c1, c2_, c3):
                st.do(STT(out=ang, in0=turns, scalar=-part, in1=ang, op0=ALU.mult, op1=ALU.add))
            st.do(TS(args, ang, 3.1415925, -3.1415925, ALU.min, ALU.max))
            st.do(TS(rope_t[:, 3, 32:64], args, -1.0, None, ALU.mult))
            st.do(TT(rope_t[:, 3, 32:64], rope_t[:, 3, 32:64], args, ALU.max))
            TS(rope_t[:, 3, 32:64], rope_t[:, 3, 32:64], -1.0, float(np.pi / 2), ALU.mult, ALU.add)\
                .then_inc(angles, 1)

            for i in range(H1 + 2):
                if i >= 2:
                    hd = i - 2
                    dve.wait_ge(weights_in, hd + 1)
                    if hd >= 2:
                        pair_done(dve, "o", 0, hd - 2)
                    TT(two["pa"][:, hd % 2, :], two["dd"][:, hd % 2, :], mask, ALU.mult).then_inc(sb_probs, 1)
                if i < H1:
                    b = i % 2
                    dve.wait_ge(log_part, i + 1)
                    ps = full(dve, ("z", i))
                    sp_ = two["sp"][:, b, :]
                    st.do(STT(out=sp_, in0=ps[:, 0:ATT], scalar=0.0, in1=two["az"][:, b, :],
                              op0=ALU.max, op1=ALU.add))
                    TT(two["spm"][:, b, :], sp_, mask, ALU.mult).then_inc(fails, 1)
                    drains(TT(two["dd"][:, b, :], ps[:, 0:ATT], sp_, ALU.subtract), ("z", i))
                if 1 <= i <= H1:
                    hd = i - 1
                    ps = full(dve, ("t", hd))
                    drained(dve, ("z", hd))
                    drains(TT(two["la"][:, hd % 2, :], ps[:, 0:ATT], two["dd"][:, hd % 2, :], ALU.add), ("t", hd))

            norm(1, 384)
            apply(cq, cqn, par("cq_norm"), 3, normed)
            norm(2, 256)
            apply(ckv, ckvn, par("ckv_norm"), 2, normed)
            norm(3, 512)
            apply(sbT, mixed[:, 0:4, :], par("sb_out_norm"), 4, normed)
            dve.wait_ge(sincos, 1)
            sc_ = rope_t[:, 4, 0:64].rearrange("p (k b n) -> p k b n", k=2, b=TB)
            rm = a1["tsq"][:, 0:4 * 128].rearrange("p (m h n) -> p m h n", m=4, h=H1)
            for n, (src, gname) in enumerate(((qt, "q_norm"), (kt, "k_norm"))):
                what = ("uq", "ukv")[n]
                for tb in range(TB):
                    for hf in range(2):
                        drained(dve, (what, tb, hf))
                if n:
                    for tb in range(TB):
                        st.do(V.tensor_copy(kt[:, tb, :, NOPE:QKD],
                                            kpe[:, tb, :].unsqueeze(1).broadcast_to([P, H1, ROPE])))
                flat = a1[("qt", "kt")[n]].rearrange("p (n e) -> p n e", e=QKD)
                hm, hr = small[:, 8:24], small[:, 24 + 16 * n:40 + 16 * n]
                st.do(TT(tsq[:, :, :], flat, flat, ALU.mult))
                st.do(V.tensor_reduce(hm, tsq[:, :, :], AX.X, ALU.add))
                TS(hm, hm, 1.0 / QKD, EPS, ALU.mult, ALU.add).then_inc(head_ms, 1)
                dve.wait_ge(head_root, n + 1)
                st.do(V.reciprocal(hr, hr))
                st.do(TT(flat, flat, hr.unsqueeze(2).broadcast_to([P, 16, QKD]), ALU.mult))
                st.do(TT(flat, flat, par(gname).unsqueeze(1).broadcast_to([P, 16, QKD]), ALU.mult))
                for tb in range(TB):
                    x1, x2 = src[:, tb, :, NOPE:NOPE + 16], src[:, tb, :, NOPE + 16:QKD]
                    sn, cs = (sc_[:, q, tb, :].unsqueeze(1).broadcast_to([P, H1, 16]) for q in range(2))
                    TT(rm[:, 0, :, :], x1, cs, ALU.mult)
                    TT(rm[:, 1, :, :], x2, sn, ALU.mult)
                    TT(rm[:, 2, :, :], x1, sn, ALU.mult)
                    st.do(TT(rm[:, 3, :, :], x2, cs, ALU.mult))
                    st.do(TT(x1, rm[:, 0, :, :], rm[:, 1, :, :], ALU.subtract))
                    ins = TT(x2, rm[:, 2, :, :], rm[:, 3, :, :], ALU.add)
                    if tb:
                        ins.then_inc(qk_ready, 1)
                    else:
                        st.do(ins)
            for i in range(H1 + 2):
                if 1 <= i <= H1:
                    hd = i - 1
                    b = hd % 2
                    ps = full(dve, ("s", hd))
                    st.do(V.memset(ps[0:64, 0:ATT].rearrange("p (a c) -> p a c", a=6)[:, 1:6:4, :], -1e30))
                    V.reduce_max(sm(b, 0), ps[:, 0:P], AX.X)
                    st.do(V.reduce_max(sm(b, 1), ps[:, P:ATT], AX.X))
                    TS(stat[:, b, 2:4], stat[:, b, 0:2], -QKD ** -0.5, None, ALU.mult).then_inc(neg_max, 1)
                if i >= 2:
                    hd = i - 2
                    b = hd % 2
                    drained(dve, ("s", hd))
                    st.do(V.reciprocal(stat[:, b, 6:8], stat[:, b, 4:6]))
                    e = two["E"][:, b, :]
                    TS(e[:, 0:P], e[:, 0:P], sm(b, 6), None, ALU.mult)
                    TS(e[:, P:ATT], e[:, P:ATT], sm(b, 7), None, ALU.mult).then_inc(probs, 1)
            norm(4, 512)
            apply(mlaT, mixed[:, 4:8, :], par("mla_out_norm"), 4, normed)
            for c in range(4):
                ps = full(dve, ("wo", c))
                xs = x[:, 2 * c:2 * c + 2, :]
                drains(TT(xs, ps[:, :].rearrange("p (c t) -> p c t", c=2), xs, ALU.add), ("wo", c))

            norm(5)
            apply(x, h, par("ffn_norm"), KC, normed)

            def top16(vals, idx, rows):
                for m, r in enumerate(rows):
                    ins = V.max(vals[:, m, 0:8], r)
                st.do(ins)
                for m, r in enumerate(rows):
                    V.max_index(idx[:, m, 0:8], vals[:, m, 0:8], r)
                for m, r in enumerate(rows):
                    ins = V.match_replace(out=r, in_to_replace=vals[:, m, 0:8], in_values=r, imm_value=-3.0e38)
                st.do(ins)
                for m, r in enumerate(rows):
                    ins = V.max(vals[:, m, 8:16], r)
                st.do(ins)
                for m, r in enumerate(rows):
                    ins = V.max_index(idx[:, m, 8:16], vals[:, m, 8:16], r)
                st.do(ins)

            s_h = r_s[:, :, :].rearrange("p (h c) k -> p h c k", c=2)
            i_h = r_i[:, :, :].rearrange("p (h c) k -> p h c k", c=2)
            for tb in range(TB):
                for q in range(4):
                    drained(dve, ("ss", tb, q))
                top16(r_s, r_iu, [sc[:, tb, m, :] for m in range(16)])
                st.do(V.tensor_copy(r_i[:, :, :], r_iu[:, :, :]))
                st.do(TT(cand.rearrange("p h (a b) -> p h a b", a=TOPK),
                         s_h[:, :, 0, :].unsqueeze(3).broadcast_to([P, PH, TOPK, TOPK]),
                         s_h[:, :, 1, :].unsqueeze(2).broadcast_to([P, PH, TOPK, TOPK]), ALU.add))
                top16(r_b, r_bu, [cand[:, m, :] for m in range(PH)])
                st.do(V.tensor_copy(small[:, 40:48], r_b[:, :, 0]))
                TT(r_b[:, :, :], r_b[:, :, :], small[:, 40:48].unsqueeze(2).broadcast_to([P, PH, TOPK]),
                   ALU.subtract).then_inc(router_max, 1)
                flat = r_bu[:, :, :].rearrange("p h k -> p (h k)")
                TS(r_au[:, 0, :], flat, 4, None, ALU.logical_shift_right)
                st.do(TS(r_au[:, 1, :], flat, 15, None, ALU.bitwise_and))
                st.do(V.tensor_copy(r_ab[:, :, :], r_au[:, :, :]))
                for c in range(2):
                    st.do(TT(oh, iota[:, 0:TOPK].unsqueeze(1).broadcast_to([P, PH * TOPK, TOPK]),
                             r_ab[:, c, :].unsqueeze(2).broadcast_to([P, PH * TOPK, TOPK]), ALU.is_equal))
                    o4 = a2["oh"].rearrange("p (h k a) -> p h k a", h=PH, k=TOPK)
                    st.do(TT(o4, o4, i_h[:, :, c, :].unsqueeze(2).broadcast_to([P, PH, TOPK, TOPK]), ALU.mult))
                    st.do(V.tensor_reduce(r_out[:, tb, c, :], oh, AX.X, ALU.add))
                dve.wait_ge(router_exp, tb + 1)
                st.do(V.tensor_reduce(small[:, 48:56], r_b[:, :, :], AX.X, ALU.add))
                st.do(V.reciprocal(small[:, 48:56], small[:, 48:56]))
                TT(r_out[:, tb, 2, :].rearrange("p (h k) -> p h k", h=PH), r_b[:, :, :],
                   small[:, 48:56].unsqueeze(2).broadcast_to([P, PH, TOPK]), ALU.mult).then_inc(routed, 1)

            drained(dve, ("rt", 0))
            drained(dve, ("rt", 1))
            full(dve, ("u", UT - 1))
            act_out = arena[:, :].rearrange("p (j t) -> p t j", t=T)

            def weighted_rows(t, b):
                for g in range(GB):
                    TS(oneA[:, b, g, :], iota, rT[:, 0, bass.ds(t + g, 1)], rT[:, 2, bass.ds(t + g, 1)],
                             ALU.is_equal, ALU.mult)
                    ins = TS(oneB[:, b, g, :], iota, rT[:, 1, bass.ds(t + g, 1)], None, ALU.is_equal)
                ins.then_inc(one_hot, 1)

            def onto(it, i):
                b, u = use(GROUP_NO["g", 0] + i, NB)
                dve.wait_ge(bank_full[b], it + (u + 1))
                part = act_out[:, bass.ds(it * (NB * GB) + i * GB, GB), :]
                TT(part, psr[b][:, :].rearrange("p (g n) -> p g n", g=GB), part, ALU.mult)\
                    .then_inc(bank_drained[b], 1)

            weighted_rows(0, 0)
            weighted_rows(GB, 1)
            n_it = T // GB // NB
            drained(dve, ("u", UT - 1))
            drained(dve, ("u", UT - 2))
            drained(dve, ("u", UT - 3))
            drained(dve, ("u", UT - 4))
            with dve.Fori(0, n_it - 1) as it:
                for i in range(NB):
                    onto(it, i)
                    weighted_rows(it * (NB * GB) + (i + 2) * GB, i % 2)
            for i in range(NB):
                onto(n_it - 1, i)
                if i < 2:
                    weighted_rows(T - 2 * GB + i * GB, i)

            dve.wait_ge(ada_used, NADA // 2)
            ada_b = par("ada_b")
            TT(ada[:, :, :], acc[0][:, 0:2 * NADA].rearrange("p (n c) -> p n c", c=2),
               ada_b.unsqueeze(2).broadcast_to([P, NADA, 2]), ALU.add).then_inc(ada_ready, 1)
            dve.wait_ge(ada_ready, 1)
            mg, fgn = par("mix_norm_g"), par("ffn_norm_g")
            for n, (layer, part, col, g) in enumerate(((0, 1, 1, mg), (0, 1, 0, mg), (0, 4, 0, fgn),
                                                       (1, 1, 0, mg), (1, 4, 0, fgn))):
                st.do(STT(out=gsc[:, n, :], in0=mod(layer, part, col), scalar=1.0,
                          in1=g[:, 8 * layer:8 * layer + 8], op0=ALU.add, op1=ALU.mult))
            dve.wait_ge(v_used, UT)
            for c in range(4):
                xs = x[:, 2 * c:2 * c + 2, :]
                TT(xs, acc[c][:, :].rearrange("p (c t) -> p c t", c=2), xs, ALU.add).then_inc(x_added, 1)

            norm(6)
            dve.wait_ge(late_loaded, 32)
            modulate(ctxT, hc, gsc[:, 0, :], mod(0, 0, 1), normed)
            norm(7)
            dve.wait_ge(x_added, X_ADDS["peer"])
            modulate(x, h, gsc[:, 1, :], mod(0, 0), normed)
            for n in range(2):
                for c in range(3):
                    drained(dve, ("kq"[n], c))
                src = (kall[:, :, T:S2], qf)[n]
                for r in range(0, P, 64):
                    V.tensor_copy(rot[r:r + 32, :, :], src[r + 32:r + 64, :, :])
                    ins = V.tensor_copy(rot[r + 32:r + 64, :, :], src[r:r + 32, :, :])
                st.do(ins)
                TT(rot[:, :, :], rot[:, :, :], c2["sin"].unsqueeze(1).broadcast_to([P, H2, T]), ALU.mult)
                st.do(TT(src, src, c2["cos"].unsqueeze(1).broadcast_to([P, H2, T]), ALU.mult))
                ins = TT(src, src, rot[:, :, :], ALU.add)
                ins.then_inc(rotated, 1)
                dve.wait_ge(rotated, n + 1)
            for i in range(2 * H2 + 1):
                if i < 2 * H2:
                    b = i % 2
                    for c in range(2):
                        ps = full(dve, ("s2", i, c))
                        ins = V.reduce_max(sm(b, c), ps[:, :], AX.X)
                    st.do(ins)
                    TS(stat[:, b, 2:4], stat[:, b, 0:2], -SBD ** -0.5, None, ALU.mult).then_inc(neg_max2, 1)
                if i >= 1:
                    n = i - 1
                    b = n % 2
                    drained(dve, ("s2", n, 0))
                    drained(dve, ("s2", n, 1))
                    st.do(V.reciprocal(stat[:, b, 6:8], stat[:, b, 4:6]))
                    st.do(TT(sm(b, 7), sm(b, 7), lam_s, ALU.mult))
                    e0, e1 = E01[0][:, b, :], E01[1][:, b, :]
                    st.do(TS(e1, e1, sm(b, 7), None, ALU.mult))
                    STT(out=e0, in0=e0, scalar=sm(b, 6), in1=e1, op0=ALU.mult, op1=ALU.subtract)\
                        .then_inc(diff_probs, 1)
            for p_ in range(3):
                ps = full(dve, ("sn", p_))
                drains(TS(a3["osq"][:, p_ * 512:(p_ + 1) * 512], ps[:, :], 1.0 / VD, EPS, ALU.mult, ALU.add),
                       ("sn", p_))
            dve.wait_ge(o_root, 1)
            st.do(V.reciprocal(a3["orn"], a3["orn"]))
            STT(out=a3["mix2"][:, 0:H2 * T], in0=a3["oT"], scalar=subln, in1=a3["orn"], op0=ALU.mult,
                op1=ALU.mult).then_inc(mixed2, 1)
            for c in range(4):
                ps = full(dve, ("eo", c))
                for m in range(2):
                    f = 2 * c + m
                    ins = STT(out=x[:, f, :], in0=ps[:, m * T:(m + 1) * T], scalar=mod(0, 2)[:, f:f + 1],
                              in1=x[:, f, :], op0=ALU.mult, op1=ALU.add)
                drains(ins, ("eo", c))

            def ffn(layer):
                g0 = GROUP_NO["fa", layer, 0]

                def pair(it, first=False):
                    for i in range(2):
                        ba, ua = use(g0 + 2 * i, NB)
                        bb, ub = use(g0 + 2 * i + 1, NB)
                        dve.wait_ge(bank_drained[ba], it + (ua + 1))
                        dve.wait_ge(bank_full[bb], it + (ub + 1))
                        if not first:
                            dve.wait_ge(down_used, it * 2 + (NF * layer + i - 1))
                        TT(fg[:, i, :], psr[bb][:, 0:T], fs[:, i, :], ALU.mult).then_inc(bank_drained[bb], 1)

                pair(0, first=True)
                with dve.Fori(1, NF // 2) as it:
                    pair(it)
                dve.wait_ge(down_used, NF * (layer + 1))
                for f in range(KC):
                    STT(out=x[:, f, :], in0=acc[f // 2][:, (f % 2) * T:(f % 2 + 1) * T],
                        scalar=mod(layer, 5)[:, f:f + 1], in1=x[:, f, :], op0=ALU.mult, op1=ALU.add)\
                        .then_inc(x_added, 1)

            norm(8)
            drained(dve, ("eo", 3))
            modulate(x, h, gsc[:, 2, :], mod(0, 3), normed)
            ffn(0)

            norm(9)
            dve.wait_ge(x_added, X_ADDS["ffn0"])
            modulate(x, h, gsc[:, 3, :], mod(1, 0), normed)
            dve.wait_ge(padded, 1)
            pb = par("pw1_b")
            for c in range(KC):
                ps = full(dve, ("pw1", c))
                dve.wait_ge(gates, c + 1)
                drains(STT(out=upad[:, c, PADL:PADL + T], in0=ps[:, 0:T], scalar=pb[:, 2 * c:2 * c + 1],
                           in1=csig[:, c % 2, :], op0=ALU.add, op1=ALU.mult), ("pw1", c))
            for c in range(4, KC):
                drained(dve, ("pw1", c))
            dw = par("dw_w")
            for c in range(KC):
                TS(cv[:, c, :], upad[:, c, 0:T], dw[:, c * CONV:c * CONV + 1], par("dw_b")[:, c:c + 1],
                   ALU.mult, ALU.add).then_inc(dve_step, 1)
            with dve.Fori(1, CONV) as k:
                for c in range(KC):
                    dve.wait_ge(dve_step, k * KC + (st.n + c - KC + 1))
                    STT(out=cv[:, c, :], in0=upad[:, c, bass.ds(k, T)], scalar=dw[:, bass.ds(k + c * CONV, 1)],
                        in1=cv[:, c, :], op0=ALU.mult, op1=ALU.add).then_inc(dve_step, 1)
            st.n += CONV * KC
            dve.wait_ge(dve_step, st.n)
            V.tensor_copy(small[:, 7:8], small[:, 6:7]).then_inc(conv_sum, 1)
            ps = full(dve, ("mean", 0))
            drains(TS(ms[:, :], ps[:, 0:T], 1.0 / D, None, ALU.mult), ("mean", 0))
            drained(dve, ("mean", 0))
            TT(xc[:, :, :], cv[:, :, :], ms[:, :].unsqueeze(1).broadcast_to([P, KC, T]), ALU.subtract)\
                .then_inc(centred, 1)
            dve.wait_ge(centred, 1)
            norm(10)
            modulate(xc, xc, par("ln_g"), par("ln_b"), normed)
            for c in range(4):
                ps = full(dve, ("pw2", c))
                for m in range(2):
                    f = 2 * c + m
                    ins = TS(cv2[:, f, :], ps[:, m * T:(m + 1) * T], par("pw2_b")[:, f:f + 1],
                             mod(1, 2)[:, f:f + 1], ALU.add, ALU.mult)
                drains(ins, ("pw2", c))
            for c in range(4):
                drained(dve, ("pw2", c))
            TT(x[:, :, :], x[:, :, :], cv2[:, :, :], ALU.add).then_inc(x_added, 1)
            dve.wait_ge(x_added, X_ADDS["pw2"])
            norm(11)
            modulate(x, h, gsc[:, 4, :], mod(1, 3), normed)
            ffn(1)
            norm(12)
            dve.wait_ge(x_added, X_ADDS["ffn1"])
            apply(x, h, par("final_g"), KC, final)

        @block.gpsimd
        def _(pool):
            pool.wait_ge(x_added, X_ADDS["peer"])
            pool.dma_start(a3["cst2"], d["consts2"]).then_inc(late_loaded, 16)
            pool.dma_start(a3["ctx"], d["ctx"]).then_inc(late_loaded, 16)
            drained(pool, ("eo", 3))
            nc.gpsimd.memset(a4["up"], 0.0).then_inc(padded, 1)


def constants():
    f = np.float32
    p = np.arange(P)
    t = np.arange(T)
    c = {"ident": np.eye(P), "ones": np.ones((P, P)), "iota": np.broadcast_to(p, (P, P)),
         "ntri": -(p[:, None] > p[None, :]).astype(f), "nones": -np.ones((P, P)),
         "mask": np.concatenate([p[:, None] < t[None, :], (p[:, None] + P) < t[None, P:]], 1)}
    inv = f(1.0) / np.power(f(10000.0), np.arange(16, dtype=f) * f(2.0 / 32))
    c["invf"] = np.broadcast_to(inv.astype(f), (P, 16))
    c1 = np.concatenate([np.asarray(c[n], f) for n, _ in CONSTS], 1)
    inv = np.power(f(10000.0), -np.arange(0, 32, 2, dtype=f) / f(32)).astype(f)
    ang = np.concatenate([(t // 64).astype(f)[:, None] * inv, (t % 64).astype(f)[:, None] * inv], 1)
    cos, sin = np.cos(ang).T, np.sin(ang).T
    c = {"cos": np.concatenate([cos] * 4), "sin": np.concatenate([-sin, sin] * 2)}
    a = 2 * np.pi * np.outer(np.arange(64), np.arange(64)) / 64
    c["dc"] = np.kron(np.eye(2), np.cos(a) / 8)
    c["ds"] = np.kron(np.eye(2), np.sin(a) / 8)
    a = 2 * np.pi * (np.outer(t, t) % T) / T
    for n, m in (("ct", np.cos(a) / 16), ("nst", -np.sin(a) / 16)):
        c[n] = m.reshape(TB, P, T).transpose(1, 0, 2).reshape(P, TB * T)
    c2 = np.concatenate([np.asarray(c[n], f) for n, _ in CONSTS2], 1)
    return np.ascontiguousarray(c1), np.ascontiguousarray(c2)


def _by_tiles(w):
    k, n = w.shape
    return np.ascontiguousarray(w.reshape(k // P, P, n // 256, 256).transpose(2, 1, 0, 3)).reshape(n // 256, P, -1)


def _columns(v):
    return np.ascontiguousarray(v.reshape(-1, P).T)


def _feature_major(x):
    return np.ascontiguousarray(x.reshape(T, KC, P).transpose(2, 1, 0))


def kernel(**inputs):
    import concourse.bacc as _bacc
    from concourse.bass_utils import run_bass_kernel_spmd as _run

    a = {k: np.asarray(v) for k, v in inputs.items()}
    w_in = np.zeros((D, 2304), np.float32)
    w_in[:, 0:2208] = a["w_in"][0]
    ev = a["ev_w_in_2"][0]
    pw1 = a["od_pw1_w_2"][0].reshape(KC, P, 2, KC, P).transpose(3, 1, 0, 2, 4)
    up = np.stack([a["ffn_w1_2"], a["ffn_w3_2"]], 2).reshape(2, KC, P, 2, NF, P).transpose(0, 4, 2, 1, 3, 5)
    lam = np.zeros((P, 4), np.float32)
    for n, k in enumerate(("q1", "k1", "q2", "k2")):
        lam[0:64, n] = a[f"ev_lambda_{k}_2"][0]
    fw = a["ev_fourier_w_2"][0].reshape(2, 2, 64, 64).transpose(1, 2, 0, 3).reshape(P, P)
    params = {
        "attn_norm": _columns(a["attn_norm"]), "cq_norm": _columns(a["cq_norm"]),
        "ckv_norm": _columns(a["ckv_norm"]), "sb_out_norm": _columns(a["sb_out_norm"]),
        "mla_out_norm": _columns(a["mla_out_norm"]), "ffn_norm": _columns(a["ffn_norm"]),
        "ada_b": _columns(a["ada_b_2"]), "mix_norm_g": _columns(a["mix_norm_g_2"]),
        "ffn_norm_g": _columns(a["ffn_norm_g_2"]), "subln": _columns(a["ev_subln_g_2"]),
        "pw1_b": a["od_pw1_b_2"].reshape(2, KC, P).transpose(2, 1, 0).reshape(P, 16),
        "dw_w": a["od_dw_w_2"][0].reshape(CONV, KC, P).transpose(2, 1, 0).reshape(P, KC * CONV),
        "dw_b": _columns(a["od_dw_b_2"]), "ln_g": _columns(a["od_ln_g_2"]), "ln_b": _columns(a["od_ln_b_2"]),
        "pw2_b": _columns(a["od_pw2_b_2"]), "final_g": _columns(a["final_g_2"]),
        "cc": np.stack([a["c_2"][0], a["c_ctx_2"]], 1).reshape(KC, P, 2).transpose(1, 0, 2).reshape(P, 16),
        "lambdas": lam, "q_norm": np.broadcast_to(a["q_norm"], (P, QKD)),
        "k_norm": np.broadcast_to(a["k_norm"], (P, QKD)), "fw": fw,
    }
    c1, c2 = constants()
    arrays = {
        "x": _feature_major(a["x"]), "ctx": _feature_major(a["ctx_2"]).reshape(P, -1),
        "positions": np.ascontiguousarray(a["positions"].reshape(TB, P).T.astype(np.int32)),
        "consts": c1, "consts2": c2,
        "params": np.ascontiguousarray(np.concatenate([params[n] for n, _ in PARAMS], 1)),
        "w_in": _by_tiles(w_in), "w_o": _by_tiles(a["w_o"][0]), "w_q": _by_tiles(a["peer_w_q"][0]),
        "w_uq": np.ascontiguousarray(a["w_uq"][0].reshape(3, P, 2, 384).transpose(2, 1, 0, 3)).reshape(2, P, -1),
        "w_ukv": np.ascontiguousarray(a["w_ukv"][0].reshape(2, P, 1024).transpose(1, 0, 2)).reshape(1, P, -1),
        "sub_keys": np.ascontiguousarray(a["peer_sub_keys"][0].transpose(3, 1, 0, 2)).reshape(1, P, -1),
        "peer_u": np.ascontiguousarray(
            a["peer_u"][0].reshape(P, UT, 2, KC, P).transpose(1, 4, 2, 3, 0)).reshape(UT, P, -1),
        "peer_v": np.ascontiguousarray(a["peer_v"][0].reshape(P, UT, 2 * D).transpose(1, 0, 2)),
        "ada_w": np.ascontiguousarray(
            a["ada_w_2"].reshape(2, KC, P, 24, 256).transpose(0, 3, 2, 1, 4)).reshape(48, P, -1),
        "ev_q": _by_tiles(ev[:, 0:768]), "ev_k": _by_tiles(ev[:, 768:1536]), "ev_v": _by_tiles(ev[:, 1536:2304]),
        "ev_f": _by_tiles(ev[:, 2304:2560]), "ev_o": _by_tiles(a["ev_w_out_2"][0]),
        "ffn_up": np.ascontiguousarray(up).reshape(2, NF, P, -1),
        "ffn_down": np.ascontiguousarray(a["ffn_w2_2"].reshape(2, NF, P, D)),
        "pw1": np.ascontiguousarray(pw1).reshape(KC, P, -1), "pw2": _by_tiles(a["od_pw2_w_2"][0]),
    }
    nc = _bacc.Bacc("TRN2", target_bir_lowering=False, num_devices=1)
    d = {n: nc.dram_tensor(f"in_{n}", v.shape, mybir.dt.from_np(v.dtype), kind="ExternalInput").ap()
         for n, v in arrays.items()}
    d["out"] = nc.dram_tensor("out_0", (P, KC, T), F32, kind="ExternalOutput").ap()
    build(nc, d)
    r = _run(nc, [{f"in_{n}": v for n, v in arrays.items()}], core_ids=[0])
    return np.ascontiguousarray(r.results[0]["out_0"].transpose(2, 1, 0).reshape(1, T, D))
```

```python
from contextlib import ExitStack

import numpy as np

import concourse.bass as bass
from concourse import mybir

ALU = mybir.AluOpType
ACT = mybir.ActivationFunctionType
F32 = mybir.dt.float32
F32R = mybir.dt.float32r
I32 = mybir.dt.int32
U32 = mybir.dt.uint32
AX = mybir.AxisListType

P = 128
T = 256
TB = T // P
D = 1024
KC = D // P
EPS = 1e-6
H1 = 8
SBD = 64
QKD, NOPE, ROPE = 96, 64, 32
ATT = 3 * P
NKEY, TOPK, PH = 128, 16, 8
J = 128
UT = J // 2
H2, VD = 6, 128
S2 = 2 * T
FF = 2816
NF = FF // P
CONV = 31
PADL = CONV // 2
PE_CONV = 2
NADA = 96
NS = 4
SLOT = 1024
NB = 4
LAMBDA_INIT = 0.2
FF_PEEL, FF_UNROLL, FF_LOOPS = 3, 4, 4
GB = 4
ROUND = 12582912.0


def ada_after_sb(i):
    return [("ada", n) for n in range(2 * i, 2 * i + 2)] if 0 <= i < 16 else []


def ada_after_mla(i):
    return [("ada", n) for n in range(32 + 2 * i, 34 + 2 * i)] if 0 <= i < 32 else []


def plan_tiles():
    t = [("in", c) for c in range(18)]
    t += [("ada", c) for c in range(32)]
    t += [("uq", c) for c in range(3)] + [("ukv", c) for c in range(2)]
    t += [("ada", c) for c in range(32, NADA)]
    t += [("wo", c) for c in range(8)]
    t += [("pq", c) for c in range(16)] + [("sk", c) for c in range(2)]
    t += [("u", c) for c in range(J)] + [("v", c) for c in range(J)]
    t += [("ek", c) for c in range(6)] + [("ev", c) for c in range(6)]
    t += [("eq", c) for c in range(6)] + [("ef", c) for c in range(2)]
    t += [("eo", c) for c in range(8)]
    for layer in range(2):
        if layer:
            t += [("pw1", c) for c in range(16)] + [("pw2", c) for c in range(8)]
        for f in range(NF):
            t += [("a", layer, f), ("b", layer, f)]
            if f:
                t.append(("d", layer, f - 1))
        t.append(("d", layer, NF - 1))
    return t


def sb_order():
    for i in range(H1 + 2):
        if i < H1:
            yield "z", i
        if 1 <= i <= H1:
            yield "t", i - 1
        if i >= 2:
            yield "o", i - 2


def mla_order():
    for i in range(H1 + 4):
        if i < H1:
            yield "qkT", i
        if 1 <= i <= H1:
            yield "s", i - 1
        if 3 <= i < H1 + 3:
            yield "pT", i - 3
        if i >= 4:
            yield "mo", i - 4


def diff_order():
    for i in range(2 * H2 + 3):
        if i < 2 * H2:
            yield "s2", i
        if 2 <= i < 2 * H2 + 2:
            yield "aT", i - 2
        if i >= 3 and i % 2 == 0:
            yield "o2", (i - 4) // 2


def plan_groups():
    g = [("lam",), ("norm", 0)] + [("in", c) for c in range(9)]
    for what, h in sb_order():
        if what == "o":
            if h % 2 == 0:
                g.append(("o", h // 2))
        else:
            g.append((what, h))
    g += [("norm", 1), ("norm", 2), ("norm", 3)]
    g += [("uq", tb, hf) for hf in range(2) for tb in range(TB)]
    g += [("ukv", tb, hf) for hf in range(2) for tb in range(TB)]
    for what, h in mla_order():
        if what == "mo":
            if h % 2 == 0:
                g.append(("mo", h // 2))
        else:
            g.append((what, h))
    g += [("norm", 4)] + [("wo", c) for c in range(4)]
    g += [("norm", 5)] + [("pq", c) for c in range(8)]
    g += [("ss", tb, q) for tb in range(TB) for q in range(4)]
    g += [("u", c) for c in range(UT // 2)]
    g += [("rt", 0), ("rt", 1)]
    g += [("u", c) for c in range(UT // 2, UT)]
    g += [("g", c) for c in range(T // GB)]
    g += [("norm", 6), ("norm", 7)]
    for c in range(3):
        g += [("k", c), ("kc", c)]
    for c in range(3):
        g += [("v2", c), ("vc", c)]
    g += [("q", c) for c in range(3)] + [("f", 0), ("fy", 0), ("fy", 1), ("fz", 0), ("fw", 0)]
    for what, i in diff_order():
        if what == "s2":
            g += [("s2", i, 0), ("s2", i, 1)]
        else:
            g.append((what, i))
    g += [("sn", p) for p in range(3)] + [("eo", c) for c in range(4)]
    g.append(("norm", 8))
    g += [(x, 0, f) for f in range(NF) for x in ("fa", "fb")]
    g.append(("norm", 9))
    g += [("pw1", c) for c in range(8)] + [("conv", c) for c in range(KC - PE_CONV, KC)]
    g += [("mean", 0), ("norm", 10)] + [("pw2", c) for c in range(4)]
    g.append(("norm", 11))
    g += [(x, 1, f) for f in range(NF) for x in ("fa", "fb")]
    g.append(("norm", 12))
    return g


TILES = plan_tiles()
GROUPS = plan_groups()
TILE_NO = {name: n for n, name in enumerate(TILES)}
GROUP_NO = {name: n for n, name in enumerate(GROUPS)}
assert len(TILE_NO) == len(TILES) and len(GROUP_NO) == len(GROUPS)


BY_POOL = ("u", "a", "b")
BY_DVE = ("v", "d")


def split_no(n):
    return sum(t[0] in BY_POOL + BY_DVE for t in TILES[:n])


def pool_no(n):
    return sum(t[0] in BY_POOL for t in TILES[:n])


def dve_no(n):
    return sum(t[0] in BY_DVE for t in TILES[:n])


def at(it, per, value, n):
    v = value(n)
    return v if it is None else it * (value(n + per) - v) + v


LAST_TILE = {("u", c): TILE_NO["u", 2 * c + 1] for c in range(UT)}
for _l in range(2):
    for _f in range(NF):
        LAST_TILE["fa", _l, _f] = TILE_NO["a", _l, _f]
        LAST_TILE["fb", _l, _f] = TILE_NO["b", _l, _f]


def bank_fills(name):
    n = GROUP_NO[name]
    return 1 + sum(g not in LAST_TILE for g in GROUPS[n % NB:n:NB])

PARAMS = [("attn_norm", 8), ("cq_norm", 3), ("ckv_norm", 2), ("sb_out_norm", 4), ("mla_out_norm", 4),
          ("ffn_norm", 8), ("ada_b", 96), ("mix_norm_g", 16), ("ffn_norm_g", 16), ("subln", 1),
          ("pw1_b", 16), ("dw_w", 8 * CONV), ("dw_b", 8), ("ln_g", 8), ("ln_b", 8), ("pw2_b", 8),
          ("final_g", 8), ("cc", 16), ("lambdas", 4), ("q_norm", 96), ("k_norm", 96), ("fw", 128)]
CONSTS = [("ident", 128), ("ones", 128), ("iota", 128), ("ntri", 128), ("nones", 128),
          ("mask", ATT), ("invf", 16)]
CONSTS2 = [("cos", T), ("sin", T), ("dc", 128), ("ds", 128), ("ct", 2 * T), ("nst", 2 * T)]


def offsets(table):
    at, out = 0, {}
    for name, n in table:
        out[name] = (at, at + n)
        at += n
    return out, at


def build(nc, d):
    with ExitStack() as ctx:
        def sb(name, shape, dt=F32):
            return ctx.enter_context(nc.sbuf_tensor(name, shape, dt))

        def sem(name):
            return ctx.enter_context(nc.semaphore(name))

        ring = sb("ring", [P, NS, SLOT])
        arena_at = -(-nc.sbuf_base // 32) * 32
        arena = sb("arena", [P, J * T])
        wh = sb("wh", [P, 2, SLOT], F32R)
        wl = sb("wl", [P, 2, SLOT], F32R)
        x = sb("x", [P, KC, T])
        hh = sb("hh", [P, KC, T], F32R)
        hl = sb("hl", [P, KC, T], F32R)
        sq = sb("sq", [P, 2048])
        h = sq[:, :].rearrange("p (c t) -> p c t", t=T)
        fgh, fgl = (nc.alloc_sbuf_tensor_at(name, [P, 2, T], F32R, offset=arena_at + 4 * (J * T - n * 2 * T))
                    for name, n in (("fgh", 2), ("fgl", 1)))
        po, pn = offsets(PARAMS)
        co, cn = offsets(CONSTS)
        prm = sb("prm", [P, pn])
        cst = sb("cst", [P, cn])
        pos_i = sb("pos_i", [P, TB], I32)
        ms = sb("ms", [P, T])
        rms = sb("rms", [P, T])
        rinv = sb("rinv", [P, T])
        rT = sb("rT", [P, 3, T])
        ada = sb("ada", [P, NADA, 2])
        gsc = sb("gsc", [P, 5, KC])
        small = sb("small", [P, 64])
        stat = sb("stat", [P, 2, 8])
        psr = [ctx.enter_context(nc.psum_tensor(f"psr{i}", [P, 512], F32)) for i in range(NB)]
        acc = [ctx.enter_context(nc.psum_tensor(f"acc{i}", [P, 512], F32)) for i in range(4)]

        def par(name):
            return prm[:, po[name][0]:po[name][1]]

        def con(name):
            return cst[:, co[name][0]:co[name][1]]

        ident, ones, iota = con("ident"), con("ones"), con("iota")
        ntri, nones, mask = con("ntri"), con("nones"), con("mask")

        def cut(spec, base=0):
            out, at = {}, base
            for name, n in spec:
                out[name] = arena[:, at:at + n]
                at += n
            assert at <= J * T, at
            return out

        a1 = cut([("sbq", 1024), ("sbk", 1024), ("sbv", 1024), ("cq", 768), ("ckv", 512), ("kpe", 64),
                  ("az", 2 * ATT), ("sp", 2 * ATT), ("spm", 2 * ATT), ("dd", 2 * ATT), ("la", 2 * ATT),
                  ("pa", 2 * ATT), ("sbT", 1024), ("mlaT", 1024), ("mixed", 2048),
                  ("cqn", 768), ("ckvn", 512), ("qt", 1536), ("kt", 1536), ("vt", 1024),
                  ("qkT", 4096), ("E", 2 * ATT), ("PT", 2 * ATT), ("tsq", 1536), ("rope", 6 * 256),
                  ("csil", KC * 64), ("rows", 2 * P)])
        csil = a1["csil"].rearrange("p (k n) -> p k n", k=KC)
        rows = a1["rows"].rearrange("p (b n) -> p b n", b=2)
        sbq = a1["sbq"].rearrange("p (c t) -> p c t", t=T)
        sbk = a1["sbk"].rearrange("p (c t) -> p c t", t=T)
        sbv = a1["sbv"].rearrange("p (b n) -> p b n", b=TB)
        cq = a1["cq"].rearrange("p (c t) -> p c t", t=T)
        ckv = a1["ckv"].rearrange("p (c t) -> p c t", t=T)
        kpe = a1["kpe"].rearrange("p (b n) -> p b n", b=TB)
        cqn = a1["cqn"].rearrange("p (c t) -> p c t", t=T)
        ckvn = a1["ckvn"].rearrange("p (c t) -> p c t", t=T)
        two = {k: a1[k].rearrange("p (b n) -> p b n", b=2) for k in ("az", "sp", "spm", "dd", "la", "pa", "E", "PT")}
        sbT = a1["sbT"].rearrange("p (c t) -> p c t", t=T)
        mlaT = a1["mlaT"].rearrange("p (c t) -> p c t", t=T)
        mixed = a1["mixed"].rearrange("p (c t) -> p c t", t=T)
        qt = a1["qt"].rearrange("p (b h e) -> p b h e", b=TB, h=H1)
        kt = a1["kt"].rearrange("p (b h e) -> p b h e", b=TB, h=H1)
        vt = a1["vt"].rearrange("p (b h e) -> p b h e", b=TB, h=H1)
        qkT = a1["qkT"].rearrange("p (h n) -> p h n", h=H1)
        tsq = a1["tsq"].rearrange("p (n e) -> p n e", e=QKD)
        rope_t = a1["rope"].rearrange("p (k n) -> p k n", k=6)

        a2 = cut([("qT", 4096), ("sc", 4096), ("cand", 2048), ("oh", 2048)], base=J * T // 2)
        qT = a2["qT"].rearrange("p (m t) -> p m t", t=T)
        sc = a2["sc"].rearrange("p (b m n) -> p b m n", b=TB, n=NKEY)
        cand = a2["cand"].rearrange("p (h n) -> p h n", h=PH)
        oh = a2["oh"].rearrange("p (n a) -> p n a", a=TOPK)
        a2r = cut([("s", 256), ("iu", 256), ("i", 256), ("b", 128), ("bu", 128), ("ab", 256), ("au", 256),
                   ("out", TB * 384)], base=J * T // 2 + 12288)

        def halves(k, dt=F32, n=16):
            return a2r[k].bitcast(dt).rearrange("p (n k) -> p n k", n=n)

        r_s, r_iu, r_i = halves("s"), halves("iu", U32), halves("i")
        r_b, r_bu = halves("b", n=PH), halves("bu", U32, n=PH)
        r_ab, r_au = halves("ab", n=2), halves("au", U32, n=2)
        r_out = a2r["out"].rearrange("p (b q n) -> p b q n", b=TB, q=3)
        oneA = sq[:, 0:2 * GB * P].rearrange("p (b g n) -> p b g n", b=2, g=GB)
        oneB = sq[:, 1024:1024 + 2 * GB * P].rearrange("p (b g n) -> p b g n", b=2, g=GB)

        c2o, c2n = offsets(CONSTS2)
        a3 = cut([("cst2", c2n), ("ctx", 2048), ("hc", 2048), ("kall", H2 * S2), ("vall", 4 * H2 * VD),
                  ("qf", H2 * T), ("rot", H2 * T), ("fT", 2 * T), ("Y", TB * 512), ("ZT", 2 * T),
                  ("E0", 2 * S2), ("E1", 2 * S2), ("aT", 4 * T), ("oT", H2 * T), ("osq", H2 * T),
                  ("orn", H2 * T), ("mix2", 2048), ("fs", 2 * T), ("fg", 2 * T)])
        c2 = {k: a3["cst2"][:, a:b] for k, (a, b) in c2o.items()}
        ctxT = a3["ctx"].rearrange("p (c t) -> p c t", t=T)
        hc = a3["hc"].rearrange("p (c t) -> p c t", t=T)
        kall = a3["kall"].rearrange("p (h s) -> p h s", h=H2)
        vall = a3["vall"].rearrange("p (s n) -> p s n", s=4)
        qf = a3["qf"].rearrange("p (h t) -> p h t", h=H2)
        rot = a3["rot"].rearrange("p (h t) -> p h t", h=H2)
        fT = a3["fT"].rearrange("p (c t) -> p c t", c=2)
        Y = a3["Y"].rearrange("p (b n) -> p b n", b=TB)
        ZT = a3["ZT"].rearrange("p (c t) -> p c t", c=2)
        E01 = [a3[k].rearrange("p (b s) -> p b s", b=2) for k in ("E0", "E1")]
        aT = a3["aT"].rearrange("p (s t) -> p s t", s=4)
        oT = a3["oT"].rearrange("p (h t) -> p h t", h=H2)
        mix2 = a3["mix2"].rearrange("p (c t) -> p c t", t=T)
        fs = a3["fs"].rearrange("p (b t) -> p b t", b=2)
        fg = a3["fg"].rearrange("p (b t) -> p b t", b=2)
        a4 = cut([("up", KC * (T + 2 * PADL)), ("cv", 2048), ("cv2", 2048), ("xc", 2048), ("sig", 512),
                  ("diag", 2 * CONV * P)], base=c2n + 4096)
        upad = a4["up"].rearrange("p (c n) -> p c n", c=KC)
        cv = a4["cv"].rearrange("p (c t) -> p c t", t=T)
        cv2 = a4["cv2"].rearrange("p (c t) -> p c t", t=T)
        xc = a4["xc"].rearrange("p (c t) -> p c t", t=T)
        diag = a4["diag"].rearrange("p (c k n) -> p c k n", c=2, k=CONV)
        csig = a4["sig"].rearrange("p (b t) -> p b t", b=2)

        tile_ready = [sem(f"tile_ready{i}") for i in range(NS)]
        high_ready = sem("high_ready")
        low_by_pool, low_by_dve = sem("low_by_pool"), sem("low_by_dve")
        tile_used = sem("tile_used")
        h_high, h_low = sem("h_high"), sem("h_low")
        c_high, c_low = sem("c_high"), sem("c_low")
        gated = sem("gated")
        fg_high, fg_low = sem("fg_high"), sem("fg_low")
        bank_full = [sem(f"bank_full{i}") for i in range(NB)]
        bank_drained = [sem(f"bank_drained{i}") for i in range(NB)]
        x_loaded = sem("x_loaded")
        small_loaded = sem("small_loaded")
        late_loaded = sem("late_loaded")
        out_stored = sem("out_stored")
        act_step, dve_step, pool_step = sem("act_step"), sem("dve_step"), sem("pool_step")
        squares = sem("squares")
        root = sem("root")
        normed = sem("normed")
        lam_in = sem("lam_in")
        lam_exp = sem("lam_exp")
        angles = sem("angles")
        sincos = sem("sincos")
        log_part = sem("log_part")
        fails = sem("fails")
        weights_in = sem("weights_in")
        sb_probs = sem("sb_probs")
        head_ms = sem("head_ms")
        head_root = sem("head_root")
        qk_ready = sem("qk_ready")
        neg_max = sem("neg_max")
        probs = sem("probs")
        c_silu = sem("c_silu")
        router_max = sem("router_max")
        router_exp = sem("router_exp")
        routed = sem("routed")
        one_hot = sem("one_hot")
        ada_used = sem("ada_used")
        rows_copied = sem("rows_copied")
        columns_made = sem("columns_made")
        ada_ready = sem("ada_ready")
        x_added = sem("x_added")
        rotated = sem("rotated")
        neg_max2 = sem("neg_max2")
        diff_probs = sem("diff_probs")
        o_squares = sem("o_squares")
        o_root = sem("o_root")
        mixed2 = sem("mixed2")
        conv_sum = sem("conv_sum")
        centred = sem("centred")
        silued = sem("silued")
        final = sem("final")
        half_out = sem("half_out")
        gates = sem("gates")
        padded = sem("padded")
        diagonals = sem("diagonals")

        def use(n, k):
            return n % k, n // k

        def used(eng, n, it=None, per=0):
            eng.wait_ge(tile_used, at(it, per, split_no, n + 1))

        def split_high(n, it=None, per=0):
            eng, q = nc.scalar, split_no(n)
            s, u = use(n, NS)
            eng.wait_ge(tile_ready[s], at(it, per, lambda m: 16 * (m // NS + 1), n))
            if q >= 2:
                eng.wait_ge(tile_used, at(it, per, split_no, n) - 1)
            nc.scalar.activation(wh[:, q % 2, :], ring[:, s, :], ACT.Copy).then_inc(high_ready, 1)

        def split_low(eng, n, it=None, per=0):
            q = split_no(n)
            eng.wait_ge(high_ready, at(it, per, split_no, n) + 1)
            if q >= 2:
                eng.wait_ge(tile_used, at(it, per, split_no, n) - 1)
            mine = low_by_pool if TILES[n][0] in BY_POOL else low_by_dve
            eng.tensor_tensor(wl[:, q % 2, :], ring[:, n % NS, :], wh[:, q % 2, :], ALU.subtract)\
                .then_inc(mine, 1)

        def low_ready(eng, n, it=None, per=0):
            if TILES[n][0] in BY_POOL:
                eng.wait_ge(low_by_pool, at(it, per, pool_no, n) + 1)
            else:
                eng.wait_ge(low_by_dve, at(it, per, dve_no, n) + 1)

        def is_split(n):
            return n < len(TILES) and TILES[n][0] in BY_POOL + BY_DVE

        def full(eng, name):
            b = GROUP_NO[name] % NB
            if name in LAST_TILE:
                used(eng, LAST_TILE[name])
            else:
                eng.wait_ge(bank_full[b], bank_fills(name))
            return psr[b]

        def drains(ins, name):
            return ins.then_inc(bank_drained[GROUP_NO[name] % NB], 1)

        def drained(eng, name):
            b, u = use(GROUP_NO[name], NB)
            eng.wait_ge(bank_drained[b], u + 1)

        def sm(b, k):
            return stat[:, b, k:k + 1]

        def pair_done(eng, name, base, hd):
            if hd % 2 == 0:
                eng.wait_ge(half_out, base + hd // 2 + 1)
            else:
                full(eng, (name, hd // 2))

        class Steps:

            def __init__(self, eng, s):
                self.eng, self.s, self.n = eng, s, 0

            def do(self, ins):
                ins.then_inc(self.s, 1)
                self.n += 1
                self.eng.wait_ge(self.s, self.n)

        def over_ff(eng, step):
            for f in range(FF_PEEL):
                step(f)
            with eng.Fori(0, FF_LOOPS) as it:
                for i in range(FF_UNROLL):
                    step(FF_PEEL + i, it)
            for f in range(FF_PEEL + FF_UNROLL * FF_LOOPS, NF):
                step(f)

        X_ADDS = {"peer": 4, "ffn0": 12, "pw2": 13, "ffn1": 21}
        block = ctx.enter_context(nc.Block())

        @block.sync
        def _(sp):
            src = {"in": d["w_in"], "uq": d["w_uq"], "ukv": d["w_ukv"], "wo": d["w_o"], "pq": d["w_q"],
                   "sk": d["sub_keys"], "u": d["peer_u"], "ada": d["ada_w"], "v": d["peer_v"],
                   "ek": d["ev_k"], "ev": d["ev_v"], "eq": d["ev_q"], "ef": d["ev_f"], "eo": d["ev_o"],
                   "pw1": d["pw1"], "pw2": d["pw2"]}
            last_group = {"uq": ("uq", 1, 1), "ukv": ("ukv", 1, 1)}

            def released(n, it=None, per=0):
                kind, c = TILES[n][0:2]
                if is_split(n):
                    low_ready(sp, n, it, per)
                elif kind == "ada":
                    sp.wait_ge(ada_used, c + 1)
                elif kind in last_group:
                    full(sp, last_group[kind])
                elif kind == "sk":
                    full(sp, ("ss", 1, 2 * c + 1))
                elif kind in ("ek", "ev"):
                    full(sp, ({"ek": "kc", "ev": "vc"}[kind], c // 2))
                elif kind in ("eq", "ef"):
                    full(sp, (kind[1], c // 2))
                else:
                    full(sp, (kind, c // 2))

            def load(n, it=None, per=0):
                name = TILES[n]
                if n >= NS:
                    released(n - NS, it, per)
                if name[0] in ("a", "b", "d"):
                    a = d[f"ffn_{name[0]}"][name[1]]
                    a = a[name[2]] if it is None else a[it * FF_UNROLL + name[2]]
                else:
                    a = src[name[0]]
                    a = a[name[1]] if it is None else a[it * per + name[1]]
                sp.dma_start(ring[:, n % NS, 0:a.shape[1]], a).then_inc(tile_ready[n % NS], 16)

            sp.dma_start(x[:, :, :], d["x"]).then_inc(x_loaded, 16)
            sp.dma_start(cst[:, :], d["consts"]).then_inc(small_loaded, 16)
            sp.dma_start(prm[:, :], d["params"]).then_inc(small_loaded, 16)
            sp.dma_start(pos_i[:, :], d["positions"]).then_inc(small_loaded, 16)
            n = 0
            while n < len(TILES):
                kind = TILES[n][0]
                if kind in ("u", "v") and TILES[n][1] == NS:
                    count = J // NS - 1
                    with sp.Fori(0, count) as it:
                        for i in range(NS):
                            load(n + i, it, NS)
                    n += NS * count
                elif kind == "a" and TILES[n][2] == FF_PEEL:
                    with sp.Fori(0, FF_LOOPS) as it:
                        for i in range(3 * FF_UNROLL):
                            load(n + i, it, 3 * FF_UNROLL)
                    n += 3 * FF_UNROLL * FF_LOOPS
                else:
                    load(n)
                    n += 1
            sp.wait_ge(final, 1)
            sp.dma_start(d["out"], h).then_inc(out_stored, 16)
            sp.wait_ge(out_stored, 16)

        @block.tensor
        def _(pe):
            mm = nc.tensor.matmul
            g_at = [0]

            def bank(name):
                assert GROUPS[g_at[0]] == name, (GROUPS[g_at[0]], name)
                b, u = use(g_at[0], NB)
                g_at[0] += 1
                if u:
                    pe.wait_ge(bank_drained[b], u)
                return psr[b]

            def fills(ins, name):
                ins.then_inc(bank_full[GROUP_NO[name] % NB], 1)

            def tile(*name):
                s, u = use(TILE_NO[name], NS)
                pe.wait_ge(tile_ready[s], 16 * (u + 1))
                return ring[:, s, :]

            def norm(k, n, src=None):
                ps = bank(("norm", k))
                pe.wait_ge(squares, k + 1)
                for c in range(n):
                    last = mm(ps[:, 0:T], ones, sq[:, c * T:(c + 1) * T], start=(c == 0), stop=(c == n - 1))
                fills(last, ("norm", k))

            def w8(t):
                return t.rearrange("p (k n) -> p k n", k=KC)

            def features(ps, kind, c, src, chunks=(0, 1)):
                for m in chunks:
                    w = w8(tile(kind, 2 * c + m))
                    for k in range(KC):
                        last = mm(ps[:, m * T:(m + 1) * T], w[:, k, :], src[:, k, :],
                                  start=(k == 0), stop=(k == KC - 1))
                return last

            def tokens(ps, kind, c, src):
                for m in range(2):
                    w = w8(tile(kind, 2 * c + m))
                    for tb in range(TB):
                        for k in range(KC):
                            last = mm(ps[:, tb * T + m * P:tb * T + (m + 1) * P], src[:, k, tb * P:(tb + 1) * P],
                                      w[:, k, :], start=(k == 0), stop=(k == KC - 1))
                return last

            def split_product(n, products, starts=(), low_first=False, it=None, per=0):
                b = split_no(n) % 2
                pe.wait_ge(high_ready, at(it, per, split_no, n) + 1)
                for q, (out, w0, hi, lo) in enumerate(products):
                    mm(out, wh[:, b, w0:w0 + P], hi, start=(q in starts), stop=False, skip_group_check=True)
                    if not low_first:
                        mm(out, wh[:, b, w0:w0 + P], lo, start=False, stop=False, skip_group_check=True)
                low_ready(pe, n, it, per)
                for out, w0, hi, lo in products:
                    if low_first:
                        mm(out, wh[:, b, w0:w0 + P], lo, start=False, stop=False, skip_group_check=True)
                    last = mm(out, wl[:, b, w0:w0 + P], hi, start=False, stop=True, skip_group_check=True)
                last.then_inc(tile_used, 1)

            def h_parts(k):
                return hh[:, k, :], hl[:, k, :]

            def modulation(tiles):
                if not tiles:
                    return
                pair = tiles[0][1] // 2
                if pair >= 2:
                    columns(pair - 2)
                for m, name in enumerate(tiles):
                    w = w8(tile(*name))
                    for k in range(KC):
                        last = mm(acc[2 + pair % 2][64 * m:64 * m + 64, 0:P], csil[:, k, :], w[:, k, :],
                                  start=(k == 0), stop=(k == KC - 1), skip_group_check=True)
                    last.then_inc(ada_used, 1)

            def columns(pair):
                pe.wait_ge(rows_copied, pair + 1)
                sel = ident.rearrange("p (b n) -> p b n", b=2)[:, :, 0:2]
                mm(acc[0][:, 4 * pair:4 * pair + 4], rows[:, pair % 2, :], sel, start=True, stop=True)\
                    .then_inc(columns_made, 1)

            pe.wait_ge(small_loaded, 48)
            ps = bank(("lam",))
            pe.wait_ge(lam_in, 1)
            fills(mm(ps[:, 0:2], ones[0:64, :], small[0:64, 0:2], start=True, stop=True), ("lam",))

            norm(0, KC)
            pe.wait_ge(normed, 1)
            for c in range(9):
                ps = bank(("in", c))
                if c in (4, 5):
                    last = tokens(ps, "in", c, h)
                elif c < 8:
                    last = features(ps, "in", c, h)
                else:
                    features(ps, "in", c, h, (0,))
                    w = w8(tile("in", 17))
                    for tb in range(TB):
                        for k in range(KC):
                            last = mm(ps[:, T + tb * ROPE:T + (tb + 1) * ROPE], h[:, k, tb * P:(tb + 1) * P],
                                      w[:, k, 0:ROPE], start=(k == 0), stop=(k == KC - 1))
                fills(last, ("in", c))

            drained(pe, ("in", 3))
            drained(pe, ("in", 5))
            pe.wait_ge(c_silu, 1)
            for step, (what, hd) in enumerate(sb_order()):
                r = 64 * (hd % 2)
                c = hd // 2
                if what == "z":
                    ps = bank(("z", hd))
                    mm(ps[:, 0:T], sbk[r:r + 64, c, 0:P], sbq[r:r + 64, c, :], start=True, stop=True)
                    fills(mm(ps[:, T:ATT], sbk[r:r + 64, c, P:T], sbq[r:r + 64, c, P:T], start=True, stop=True),
                          ("z", hd))
                elif what == "t":
                    ps = bank(("t", hd))
                    pe.wait_ge(fails, hd + 1)
                    f = two["spm"][:, hd % 2, :]
                    mm(ps[:, 0:T], ntri, f[:, 0:T], start=True, stop=False, skip_group_check=True)
                    mm(ps[:, P:T], nones, f[:, T:ATT], start=False, stop=False, skip_group_check=True)
                    fills(mm(ps[:, T:ATT], ntri, f[:, T:ATT], start=False, stop=True, skip_group_check=True),
                          ("t", hd))
                else:
                    if hd % 2 == 0:
                        ps_o = bank(("o", c))
                    pe.wait_ge(sb_probs, hd + 1)
                    a = two["pa"][:, hd % 2, :]
                    o = ps_o[r:r + 64, 0:T]
                    mm(o, sbv[:, 0, 64 * hd:64 * hd + 64], a[:, 0:T], start=True, stop=False, skip_group_check=True)
                    last = mm(ps_o[r:r + 64, P:T], sbv[:, 1, 64 * hd:64 * hd + 64], a[:, T:ATT],
                              start=False, stop=True, skip_group_check=True)
                    if hd % 2:
                        fills(last, ("o", c))
                    else:
                        last.then_inc(half_out, 1)
                modulation(ada_after_sb(step))

            norm(1, 3)
            norm(2, 2)
            norm(3, 4)
            pe.wait_ge(normed, 3)
            w = [tile("uq", k) for k in range(3)]
            for hf in range(2):
                for tb in range(TB):
                    ps = bank(("uq", tb, hf))
                    for k in range(3):
                        last = mm(ps[:, 0:384], cqn[:, k, tb * P:(tb + 1) * P], w[k][:, hf * 384:(hf + 1) * 384],
                                  start=(k == 0), stop=(k == 2))
                    fills(last, ("uq", tb, hf))
            w = [tile("ukv", k) for k in range(2)]
            for hf in range(2):
                for tb in range(TB):
                    ps = bank(("ukv", tb, hf))
                    for k in range(2):
                        last = mm(ps[:, :], ckvn[:, k, tb * P:(tb + 1) * P], w[k][:, hf * 512:(hf + 1) * 512],
                                  start=(k == 0), stop=(k == 1))
                    fills(last, ("ukv", tb, hf))
            pe.wait_ge(qk_ready, 2)
            for step, (what, hd) in enumerate(mla_order()):
                r = 64 * (hd % 2)
                if what == "qkT":
                    ps = bank(("qkT", hd))
                    for n, src in enumerate((qt, kt)):
                        for tb in range(TB):
                            at_ = (2 * n + tb) * P
                            last = nc.tensor.transpose(ps[0:QKD, at_:at_ + P], src[:, tb, hd, :], ident)
                    fills(last, ("qkT", hd))
                elif what == "s":
                    ps = bank(("s", hd))
                    drained(pe, ("qkT", hd))
                    w = qkT[0:QKD, hd, :]
                    mm(ps[:, 0:P], w[:, 0:P], w[:, T:T + P], start=True, stop=True)
                    fills(mm(ps[:, P:ATT], w[:, P:T], w[:, T:2 * T], start=True, stop=True), ("s", hd))
                elif what == "pT":
                    ps = bank(("pT", hd))
                    pe.wait_ge(probs, hd + 1)
                    for n in range(3):
                        last = nc.tensor.transpose(ps[:, n * P:(n + 1) * P], two["E"][:, hd % 2, n * P:(n + 1) * P],
                                                   ident)
                    fills(last, ("pT", hd))
                else:
                    if hd % 2 == 0:
                        ps_o = bank(("mo", hd // 2))
                    drained(pe, ("pT", hd))
                    a = two["PT"][:, hd % 2, :]
                    mm(ps_o[r:r + 64, 0:T], vt[:, 0, hd, :], a[:, 0:T], start=True, stop=False,
                       skip_group_check=True)
                    last = mm(ps_o[r:r + 64, P:T], vt[:, 1, hd, :], a[:, T:ATT], start=False, stop=True,
                              skip_group_check=True)
                    if hd % 2:
                        fills(last, ("mo", hd // 2))
                    else:
                        last.then_inc(half_out, 1)
                modulation(ada_after_mla(step))
            columns(NADA // 2 - 2)
            columns(NADA // 2 - 1)
            norm(4, 4)
            pe.wait_ge(normed, 5)
            for c in range(4):
                ps = bank(("wo", c))
                fills(features(ps, "wo", c, mixed), ("wo", c))

            norm(5, KC)
            pe.wait_ge(normed, 6)
            for c in range(8):
                ps = bank(("pq", c))
                fills(features(ps, "pq", c, h), ("pq", c))
            w = [w8(tile("sk", q)) for q in range(2)]
            drained(pe, ("pq", 6))
            drained(pe, ("pq", 7))
            for tb in range(TB):
                for q in range(4):
                    ps = bank(("ss", tb, q))
                    for m in range(4):
                        last = mm(ps[:, m * P:(m + 1) * P], qT[:, 4 * q + m, tb * P:(tb + 1) * P],
                                  w[q // 2][:, 4 * (q % 2) + m, :], start=True, stop=True)
                    fills(last, ("ss", tb, q))
            def expert_in(half):
                t0, g0 = TILE_NO["u", half * UT], GROUP_NO["u", half * UT // 2]
                with pe.Fori(0, UT // 2 // NB) as it:
                    for i in range(NB):
                        b, ub = use(g0 + i, NB)
                        pe.wait_ge(bank_drained[b], it + ub)
                        for j in range(2):
                            split_product(t0 + 2 * i + j,
                                          [(psr[b][:, j * T:(j + 1) * T], k * P, *h_parts(k)) for k in range(KC)],
                                          (0,) if j == 0 else (), it=it, per=2 * NB)
                g_at[0] += UT // 2

            pe.wait_ge(h_low, 2)
            expert_in(0)
            pe.wait_ge(routed, 2)
            for n in range(2):
                ps = bank(("rt", n))
                for q in range(3):
                    last = nc.tensor.transpose(ps[:, q * P:(q + 1) * P], r_out[:, n, q, :], ident)
                fills(last, ("rt", n))
            expert_in(1)
            g0 = GROUP_NO["g", 0]
            with pe.Fori(0, T // GB // NB) as it:
                for q in range(NB):
                    b, ub = use(g0 + q, NB)
                    pe.wait_ge(bank_drained[b], it + ub)
                    pe.wait_ge(one_hot, it * NB + (q + 1))
                    for g in range(GB):
                        last = mm(psr[b][:, g * P:(g + 1) * P], oneA[:, q % 2, g, :], oneB[:, q % 2, g, :],
                                  start=True, stop=True)
                    last.then_inc(bank_full[b], 1)
            g_at[0] += T // GB
            pe.wait_ge(ada_ready, 1)
            t0 = TILE_NO["v", 0]

            def expert_out(it=None, first=False):
                for j in range(KC):
                    pe.wait_ge(c_low, j + 1 if it is None else it * KC + (j + 1))
                    split_product(t0 + j, [(acc[c // 2][:, (c % 2) * T:(c % 2 + 1) * T], c * P, *h_parts(j))
                                           for c in range(KC)],
                                  range(0, KC, 2) if first and j == 0 else (), low_first=True, it=it, per=KC)

            expert_out(first=True)
            with pe.Fori(1, J // KC) as it:
                expert_out(it)

            norm(6, KC)
            norm(7, KC)
            pe.wait_ge(normed, 8)
            for c in range(3):
                for what, src in (("k", h), ("kc", hc)):
                    ps = bank((what, c))
                    fills(features(ps, "ek", c, src), (what, c))
            for c in range(3):
                for what, src in (("v2", h), ("vc", hc)):
                    ps = bank((what, c))
                    fills(tokens(ps, "ev", c, src), (what, c))
            for c in range(3):
                ps = bank(("q", c))
                fills(features(ps, "eq", c, h), ("q", c))
            ps = bank(("f", 0))
            fills(features(ps, "ef", 0, h), ("f", 0))
            drained(pe, ("f", 0))
            for tb in range(TB):
                ps = bank(("fy", tb))
                for n, m in enumerate(("dc", "ds")):
                    for c in range(2):
                        last = mm(ps[:, (2 * n + c) * P:(2 * n + c + 1) * P], fT[:, c, tb * P:(tb + 1) * P], c2[m],
                                  start=True, stop=True)
                fills(last, ("fy", tb))
            ps = bank(("fz", 0))
            drained(pe, ("fy", 0))
            drained(pe, ("fy", 1))
            for c in range(2):
                for n, m in enumerate(("ct", "nst")):
                    for tb in range(TB):
                        last = mm(ps[:, c * T:(c + 1) * T], Y[:, tb, (2 * n + c) * P:(2 * n + c + 1) * P],
                                  c2[m][:, tb * T:(tb + 1) * T], start=(n + tb == 0), stop=(n + tb == 2))
            fills(last, ("fz", 0))
            ps = bank(("fw", 0))
            drained(pe, ("fz", 0))
            fw = par("fw").rearrange("p (c n) -> p c n", c=2)
            for g in range(4):
                r, c = 64 * (g % 2), g // 2
                last = mm(ps[r:r + 64, c * T:(c + 1) * T], fw[r:r + 64, c, :], ZT[r:r + 64, c, :],
                          start=True, stop=True)
            fills(last, ("fw", 0))
            pe.wait_ge(rotated, 2)
            for what, i in diff_order():
                hd, tb = i // 2, i % 2
                if what == "s2":
                    for c in range(2):
                        ps = bank(("s2", i, c))
                        fills(mm(ps[:, :], qf[64 * c:64 * c + 64, hd, tb * P:(tb + 1) * P],
                                 kall[64 * c:64 * c + 64, hd, :], start=True, stop=True), ("s2", i, c))
                elif what == "aT":
                    ps = bank(("aT", i))
                    pe.wait_ge(diff_probs, i + 1)
                    for s in range(4):
                        last = nc.tensor.transpose(ps[:, s * P:(s + 1) * P], E01[0][:, i % 2, s * P:(s + 1) * P],
                                                   ident)
                    fills(last, ("aT", i))
                else:
                    ps = bank(("o2", i))
                    drained(pe, ("aT", 2 * i))
                    drained(pe, ("aT", 2 * i + 1))
                    for s in range(4):
                        last = mm(ps[:, 0:T], vall[:, s, i * VD:(i + 1) * VD], aT[:, s, :],
                                  start=(s == 0), stop=(s == 3))
                    fills(last, ("o2", i))
            pe.wait_ge(o_squares, 1)
            for p_ in range(3):
                ps = bank(("sn", p_))
                fills(mm(ps[:, :], ones, a3["osq"][:, p_ * 512:(p_ + 1) * 512], start=True, stop=True), ("sn", p_))
            pe.wait_ge(mixed2, 1)
            drained(pe, ("fw", 0))
            for c in range(4):
                ps = bank(("eo", c))
                fills(features(ps, "eo", c, mix2), ("eo", c))

            def ffn(layer):
                per = 3 * FF_UNROLL

                def up(what, f, it):
                    n = TILE_NO[what, layer, f]
                    b, ub = use(GROUP_NO["f" + what, layer, f], NB)
                    pe.wait_ge(bank_drained[b], at(it, 2 * FF_UNROLL, lambda g: g // NB, GROUP_NO["f" + what, layer, f]))
                    split_product(n, [(psr[b][:, 0:T], k * P, *h_parts(k)) for k in range(KC)], (0,), it=it, per=per)

                def down(f, it):
                    q = NF * layer + f
                    pe.wait_ge(fg_low, q + 1 if it is None else it * FF_UNROLL + (q + 1))
                    split_product(TILE_NO["d", layer, f],
                                  [(acc[c // 2][:, (c % 2) * T:(c % 2 + 1) * T], c * P, fgh[:, f % 2, :], fgl[:, f % 2, :])
                                   for c in range(KC)], range(0, KC, 2) if f == 0 else (), it=it, per=per)

                def step(f, it=None):
                    up("a", f, it)
                    up("b", f, it)
                    if f:
                        down(f - 1, it)

                over_ff(pe, step)
                down(NF - 1, None)
                g_at[0] += 2 * NF

            norm(8, KC)
            pe.wait_ge(h_low, 4)
            ffn(0)

            norm(9, KC)
            pe.wait_ge(normed, 10)
            for c in range(8):
                ps = bank(("pw1", c))
                fills(features(ps, "pw1", c, h), ("pw1", c))
            pe.wait_ge(diagonals, PE_CONV)
            for c in range(KC - PE_CONV, KC):
                ps = bank(("conv", c))
                drained(pe, ("pw1", c))
                for k in range(CONV):
                    last = mm(ps[:, 0:T], diag[:, c - KC + PE_CONV, k, :], upad[:, c, k:k + T],
                              start=(k == 0), stop=(k == CONV - 1))
                fills(last, ("conv", c))
            ps = bank(("mean", 0))
            pe.wait_ge(conv_sum, 1)
            for c in range(KC - PE_CONV, KC):
                drained(pe, ("conv", c))
            for c in range(KC):
                last = mm(ps[:, 0:T], ones, cv[:, c, :], start=(c == 0), stop=(c == KC - 1))
            fills(last, ("mean", 0))
            norm(10, KC)
            pe.wait_ge(silued, 1)
            for c in range(4):
                ps = bank(("pw2", c))
                fills(features(ps, "pw2", c, cv), ("pw2", c))
            norm(11, KC)
            pe.wait_ge(h_low, 6)
            ffn(1)
            norm(12, KC)
            assert g_at[0] == len(GROUPS)

        @block.scalar
        def _(act):
            st = Steps(act, act_step)
            A = nc.scalar.activation

            def norm(k, src, n, waits, prev=None):
                for s, v in waits:
                    if v is None:
                        drained(act, s)
                    else:
                        act.wait_ge(s, v)
                if prev is not None:
                    full(act, prev)
                A(sq[:, 0:n * T], src, ACT.Square).then_inc(squares, 1)

            def rootof(k):
                drained(act, ("norm", k))
                A(rms[:, :], ms[:, :], ACT.Sqrt).then_inc(root, 1)

            act.wait_ge(small_loaded, 48)
            norm(0, x[:, :, :], KC, [(x_loaded, 16)])
            rootof(0)
            A(csil.rearrange("p k (r n) -> p k r n", n=2),
              par("cc").rearrange("p (k n) -> p k n", k=KC).unsqueeze(2).broadcast_to([P, KC, 32, 2]), ACT.Silu)\
                .then_inc(c_silu, 1)
            ps = full(act, ("lam",))
            drains(A(small[:, 2:4], ps[:, 0:2], ACT.Exp), ("lam",))
            act.wait_ge(angles, 1)
            A(rope_t[:, 4, 0:64], rope_t[:, 3, 0:64], ACT.Sin).then_inc(sincos, 1)

            def h_highs(k):
                act.wait_ge(normed, k + 1)
                for q in range(2):
                    A(hh[:, 4 * q:4 * q + 4, :], h[:, 4 * q:4 * q + 4, :], ACT.Copy).then_inc(h_high, 1)

            def copy_rows(tiles):
                if tiles:
                    pair = tiles[0][1] // 2
                    act.wait_ge(ada_used, 2 * (pair + 1))
                    if pair >= 2:
                        act.wait_ge(columns_made, pair - 1)
                    A(rows[:, pair % 2, :], acc[2 + pair % 2][:, 0:P], ACT.Copy).then_inc(rows_copied, 1)

            for c in range(9):
                ps = full(act, ("in", c))
                if c < 2:
                    ins = A(sbq[:, 2 * c:2 * c + 2, :], ps[:, :], ACT.Copy, scale=SBD ** -0.5)
                elif c < 4:
                    ins = A(sbk[:, 2 * c - 4:2 * c - 2, :], ps[:, :], ACT.Copy)
                elif c < 6:
                    ins = A(sbv[:, :, (c - 4) * T:(c - 3) * T], ps[:, :].rearrange("p (b n) -> p b n", b=TB), ACT.Copy)
                elif c == 6:
                    ins = A(cq[:, 0:2, :], ps[:, :], ACT.Copy)
                elif c == 7:
                    A(cq[:, 2, :], ps[:, 0:T], ACT.Copy).then_inc(act_step, 1)
                    st.n += 1
                    ins = A(ckv[:, 0, :], ps[:, T:2 * T], ACT.Copy)
                else:
                    A(ckv[:, 1, :], ps[:, 0:T], ACT.Copy).then_inc(act_step, 1)
                    st.n += 1
                    ins = A(kpe[:, :, :], ps[:, T:T + 64].rearrange("p (b n) -> p b n", b=TB), ACT.Copy)
                drains(ins, ("in", c))

            step = 0
            for i in range(H1 + 2):
                if i < H1:
                    copy_rows(ada_after_sb(step - 1))
                    step += 1
                    b = i % 2
                    ps = full(act, ("z", i))
                    if i >= 2:
                        act.wait_ge(fails, i - 1)
                    az = two["az"][:, b, :]
                    st.do(A(az, ps[:, 0:ATT], ACT.Abs))
                    st.do(A(az, az, ACT.Exp, scale=-1.0))
                    A(az, az, ACT.Ln, bias=1.0).then_inc(log_part, 1)
                if 1 <= i <= H1:
                    copy_rows(ada_after_sb(step - 1))
                    step += 1
                    hd = i - 1
                    drained(act, ("t", hd))
                    A(two["dd"][:, hd % 2, :], two["la"][:, hd % 2, :], ACT.Exp).then_inc(weights_in, 1)
                if i >= 2:
                    copy_rows(ada_after_sb(step - 1))
                    step += 1
                if i >= 2 and (i - 2) % 2 == 1:
                    c = (i - 2) // 2
                    ps = full(act, ("o", c))
                    drains(A(sbT[:, c, :], ps[:, 0:T], ACT.Copy), ("o", c))

            act.wait_ge(act_step, st.n)
            drained(act, ("in", 8))
            norm(1, cq[:, :, :], 3, [], prev=("norm", 0))
            rootof(1)
            norm(2, ckv[:, :, :], 2, [], prev=("norm", 1))
            rootof(2)
            drained(act, ("o", 3))
            norm(3, sbT[:, :, :], 4, [], prev=("norm", 2))
            rootof(3)
            for hf in range(2):
                for tb in range(TB):
                    ps = full(act, ("uq", tb, hf))
                    drains(A(qt[:, tb, 4 * hf:4 * hf + 4, :], ps[:, 0:384].rearrange("p (h e) -> p h e", h=4),
                             ACT.Copy), ("uq", tb, hf))
            for hf in range(2):
                for tb in range(TB):
                    ps = full(act, ("ukv", tb, hf))
                    kv = ps[:, :].rearrange("p (h e) -> p h e", h=4)
                    A(kt[:, tb, 4 * hf:4 * hf + 4, 0:NOPE], kv[:, :, 0:NOPE], ACT.Copy).then_inc(act_step, 1)
                    st.n += 1
                    drains(A(vt[:, tb, 4 * hf:4 * hf + 4, :], kv[:, :, NOPE:2 * NOPE], ACT.Copy), ("ukv", tb, hf))
            for n in range(2):
                act.wait_ge(head_ms, n + 1)
                A(small[:, 24 + 16 * n:40 + 16 * n], small[:, 8:24], ACT.Sqrt).then_inc(head_root, 1)
            step = 0
            for i in range(H1 + 4):
                if i < H1:
                    copy_rows(ada_after_mla(step - 1))
                    step += 1
                    ps = full(act, ("qkT", i))
                    drains(A(qkT[0:QKD, i, :], ps[0:QKD, :], ACT.Copy), ("qkT", i))
                if 1 <= i <= H1:
                    copy_rows(ada_after_mla(step - 1))
                    step += 1
                    hd = i - 1
                    b = hd % 2
                    ps = full(act, ("s", hd))
                    act.wait_ge(neg_max, hd + 1)
                    if hd >= 2:
                        full(act, ("pT", hd - 2))
                    for n, (lo, hi) in enumerate(((0, P), (P, ATT))):
                        ins = A(two["E"][:, b, lo:hi], ps[:, lo:hi], ACT.Exp, scale=QKD ** -0.5,
                                bias=sm(b, 2 + n), accum_out=sm(b, 4 + n))
                        if n == 0:
                            ins.then_inc(act_step, 1)
                            st.n += 1
                    drains(ins, ("s", hd))
                if 3 <= i < H1 + 3:
                    copy_rows(ada_after_mla(step - 1))
                    step += 1
                    hd = i - 3
                    ps = full(act, ("pT", hd))
                    if hd >= 2:
                        pair_done(act, "mo", H1 // 2, hd - 2)
                    drains(A(two["PT"][:, hd % 2, :], ps[:, 0:ATT], ACT.Copy), ("pT", hd))
                if i >= 4:
                    copy_rows(ada_after_mla(step - 1))
                    step += 1
                if i >= 4 and (i - 4) % 2 == 1:
                    c = (i - 4) // 2
                    ps = full(act, ("mo", c))
                    drains(A(mlaT[:, c, :], ps[:, 0:T], ACT.Copy), ("mo", c))
            copy_rows(ada_after_mla(step - 1))
            drained(act, ("mo", 3))
            norm(4, mlaT[:, :, :], 4, [], prev=("norm", 3))
            rootof(4)
            norm(5, x[:, :, :], KC, [(("wo", 3), None)], prev=("norm", 4))
            rootof(5)
            h_highs(5)
            for c in range(8):
                ps = full(act, ("pq", c))
                drains(A(qT[:, 2 * c:2 * c + 2, :], ps[:, :], ACT.Copy), ("pq", c))
            split_high(TILE_NO["u", 0])
            split_high(TILE_NO["u", 1])
            for tb in range(TB):
                for q in range(4):
                    ps = full(act, ("ss", tb, q))
                    drains(A(sc[:, tb, 4 * q:4 * q + 4, :], ps[:, :].rearrange("p (m n) -> p m n", n=NKEY), ACT.Copy),
                           ("ss", tb, q))
            g0, t0 = GROUP_NO["u", 0], TILE_NO["u", 0]

            def activate(it=None, last=0):
                for i in range(NB):
                    n = t0 + last + 2 * i
                    b = (g0 + (2 if last else 0) + i) % NB
                    split_high(n + 2, it, 2 * NB)
                    split_high(n + 3, it, 2 * NB)
                    used(act, n + 1, it, 2 * NB)
                    at_ = (last * T + i * 512) if it is None else it * (NB * 512) + (last * T + i * 512)
                    part = arena[:, at_:at_ + 512] if it is None else arena[:, bass.ds(at_, 512)]
                    A(part, psr[b][:, :], ACT.Gelu).then_inc(bank_drained[b], 1)

            turns = UT // NB
            for tb, (lo, hi) in enumerate(((0, 3), (3, turns // 2))):
                with act.Fori(lo, hi) as it:
                    activate(it)
                act.wait_ge(router_max, tb + 1)
                A(r_b[:, :, :], r_b[:, :, :], ACT.Exp).then_inc(router_exp, 1)
            for n in range(2):
                ps = full(act, ("rt", n))
                drains(A(rT[:, :, n * P:(n + 1) * P], ps[:, 0:3 * P].rearrange("p (q t) -> p q t", q=3), ACT.Copy),
                       ("rt", n))
            with act.Fori(0, turns // 2 - 1) as it:
                activate(it, UT)
            activate(None, J - 2 * NB)
            t0 = TILE_NO["v", 0]

            def c_highs(j, it=None):
                a = j * T if it is None else it * (KC * T) + j * T
                part = arena[:, a:a + T] if it is None else arena[:, bass.ds(a, T)]
                A(hh[:, j % KC, :], part, ACT.Copy).then_inc(c_high, 1)

            for i in range(NB):
                drained(act, ("g", T // GB - 1 - i))
            c_highs(0)
            c_highs(1)

            def step(j, it=None):
                used(act, t0 + j, it, KC)
                c_highs(j + 2, it)
                split_high(t0 + j + 2, it, KC)

            with act.Fori(0, J // KC - 1) as it:
                for j in range(KC):
                    step(j, it)
            for j in range(J - KC, J - 2):
                step(j)

            act.wait_ge(late_loaded, 32)
            norm(6, ctxT[:, :, :], KC, [(x_added, X_ADDS["peer"])], prev=("g", T // GB - 1))
            rootof(6)
            norm(7, x[:, :, :], KC, [], prev=("norm", 6))
            rootof(7)
            for c in range(3):
                ps = full(act, ("k", c))
                drains(A(kall[:, 2 * c:2 * c + 2, T:S2], ps[:, :].rearrange("p (h t) -> p h t", h=2), ACT.Copy), ("k", c))
                ps = full(act, ("kc", c))
                drains(A(kall[:, 2 * c:2 * c + 2, 0:T], ps[:, :].rearrange("p (h t) -> p h t", h=2), ACT.Copy), ("kc", c))
            for c in range(3):
                ps = full(act, ("v2", c))
                drains(A(vall[:, 2:4, c * T:(c + 1) * T], ps[:, :].rearrange("p (b n) -> p b n", b=2), ACT.Copy), ("v2", c))
                ps = full(act, ("vc", c))
                drains(A(vall[:, 0:2, c * T:(c + 1) * T], ps[:, :].rearrange("p (b n) -> p b n", b=2), ACT.Copy), ("vc", c))
            for c in range(3):
                ps = full(act, ("q", c))
                drains(A(qf[:, 2 * c:2 * c + 2, :], ps[:, :].rearrange("p (h t) -> p h t", h=2), ACT.Copy), ("q", c))
            ps = full(act, ("f", 0))
            drains(A(fT[:, :, :], ps[:, :].rearrange("p (h t) -> p h t", h=2), ACT.Copy), ("f", 0))
            for tb in range(TB):
                ps = full(act, ("fy", tb))
                drains(A(Y[:, tb, :], ps[:, :], ACT.Copy), ("fy", tb))
            ps = full(act, ("fz", 0))
            drains(A(ZT[:, :, :], ps[:, :].rearrange("p (h t) -> p h t", h=2), ACT.Copy), ("fz", 0))
            ps = full(act, ("fw", 0))
            drains(A(mix2[:, 6:8, :], ps[:, :].rearrange("p (h t) -> p h t", h=2), ACT.Copy), ("fw", 0))
            for i in range(2 * H2 + 3):
                if i < 2 * H2:
                    b = i % 2
                    act.wait_ge(neg_max2, i + 1)
                    for c in range(2):
                        ps = full(act, ("s2", i, c))
                        if i >= 2 and c == 0:
                            full(act, ("aT", i - 2))
                            act.wait_ge(diff_probs, i - 1)
                        drains(A(E01[c][:, b, :], ps[:, :], ACT.Exp, scale=SBD ** -0.5,
                                 bias=sm(b, 2 + c), accum_out=sm(b, 4 + c)), ("s2", i, c))
                if 2 <= i < 2 * H2 + 2:
                    n = i - 2
                    ps = full(act, ("aT", n))
                    if n >= 2:
                        full(act, ("o2", n // 2 - 1))
                    drains(A(aT[:, :, (n % 2) * P:(n % 2 + 1) * P], ps[:, :].rearrange("p (s t) -> p s t", s=4),
                             ACT.Copy), ("aT", n))
                if i >= 3 and i % 2 == 0:
                    hd = (i - 4) // 2
                    ps = full(act, ("o2", hd))
                    drains(A(oT[:, hd, :], ps[:, 0:T], ACT.Copy), ("o2", hd))
            drained(act, ("o2", H2 - 1))
            drained(act, ("o2", H2 - 2))
            A(a3["osq"], a3["oT"], ACT.Square).then_inc(o_squares, 1)
            for p_ in range(3):
                drained(act, ("sn", p_))
            A(a3["orn"], a3["osq"], ACT.Sqrt).then_inc(o_root, 1)

            def ffn(layer):
                per = 3 * FF_UNROLL

                def ahead(name, it):
                    n = TILE_NO[name] + 2
                    if n <= TILE_NO["d", layer, NF - 1]:
                        split_high(n, it, per)

                def step(f, it=None):
                    b = GROUP_NO["fa", layer, f] % NB
                    ahead(("a", layer, f), it)
                    used(act, TILE_NO["a", layer, f], it, per)
                    A(fs[:, f % 2, :], psr[b][:, 0:T], ACT.Silu).then_inc(bank_drained[b], 1)
                    ahead(("b", layer, f), it)
                    q = NF * layer + f + 1
                    act.wait_ge(gated, q if it is None else it * FF_UNROLL + q)
                    if f >= 2:
                        used(act, TILE_NO["d", layer, f - 2], it, per)
                    A(fgh[:, f % 2, :], fg[:, f % 2, :], ACT.Copy).then_inc(fg_high, 1)
                    if f:
                        ahead(("d", layer, f - 1), it)

                over_ff(act, step)

            norm(8, x[:, :, :], KC, [(("eo", 3), None)], prev=("norm", 7))
            rootof(8)
            h_highs(8)
            split_high(TILE_NO["a", 0, 0])
            split_high(TILE_NO["b", 0, 0])
            ffn(0)
            norm(9, x[:, :, :], KC, [(x_added, X_ADDS["ffn0"])], prev=("norm", 8))
            rootof(9)
            pb = par("pw1_b")
            for c in range(8):
                ps = full(act, ("pw1", c))
                if c >= 2:
                    drained(act, ("pw1", c - 2))
                A(csig[:, c % 2, :], ps[:, T:2 * T], ACT.Sigmoid, bias=pb[:, 2 * c + 1:2 * c + 2]).then_inc(gates, 1)
            for c in range(KC - PE_CONV, KC):
                ps = full(act, ("conv", c))
                drains(A(cv[:, c, :], ps[:, 0:T], ACT.Identity, bias=par("dw_b")[:, c:c + 1]), ("conv", c))
            act.wait_ge(centred, 1)
            norm(10, xc[:, :, :], KC, [], prev=("norm", 9))
            rootof(10)
            act.wait_ge(normed, 11)
            A(cv[:, :, :], xc[:, :, :], ACT.Silu).then_inc(silued, 1)
            norm(11, x[:, :, :], KC, [(x_added, X_ADDS["pw2"])], prev=("norm", 10))
            rootof(11)
            h_highs(11)
            split_high(TILE_NO["a", 1, 0])
            split_high(TILE_NO["b", 1, 0])
            ffn(1)
            norm(12, x[:, :, :], KC, [(x_added, X_ADDS["ffn1"])], prev=("norm", 11))
            rootof(12)

        @block.vector
        def _(dve):
            V = nc.vector
            st = Steps(dve, dve_step)
            TT, TS, STT = V.tensor_tensor, V.tensor_scalar, V.scalar_tensor_tensor

            def norm(k, n=D):
                ps = full(dve, ("norm", k))
                drains(TS(ms[:, :], ps[:, 0:T], 1.0 / n, EPS, ALU.mult, ALU.add), ("norm", k))
                dve.wait_ge(root, k + 1)
                st.do(V.reciprocal(rinv[:, :], rms[:, :]))

            def apply(src, dst, gain, n, signal):
                for c in range(n):
                    ins = STT(out=dst[:, c, :], in0=src[:, c, :], scalar=gain[:, c:c + 1], in1=rinv[:, :],
                              op0=ALU.mult, op1=ALU.mult)
                ins.then_inc(signal, 1)

            def modulate(src, dst, gain, shift, signal):
                st.do(TT(dst[:, :, :], src[:, :, :], rinv[:, :].unsqueeze(1).broadcast_to([P, KC, T]), ALU.mult))
                for c in range(KC):
                    ins = TS(dst[:, c, :], dst[:, c, :], gain[:, c:c + 1], shift[:, c:c + 1], ALU.mult, ALU.add)
                ins.then_inc(signal, 1)

            def h_lows(turn):
                for q in range(2):
                    dve.wait_ge(h_high, 2 * turn + q + 1)
                    part = slice(4 * q, 4 * q + 4)
                    TT(hl[:, part, :], h[:, part, :], hh[:, part, :], ALU.subtract).then_inc(h_low, 1)

            def mod(layer, part, col=0):
                a = 48 * layer + 8 * part
                return ada[:, a:a + 8, col]

            dve.wait_ge(small_loaded, 48)
            lam = par("lambdas")
            TT(small[0:64, 0:2], lam[0:64, 0:4:2], lam[0:64, 1:4:2], ALU.mult).then_inc(lam_in, 1)
            norm(0)
            dve.wait_ge(x_loaded, 16)
            apply(x, h, par("attn_norm"), KC, normed)
            drained(dve, ("lam",))
            st.do(TT(small[:, 4:5], small[:, 2:3], small[:, 3:4], ALU.subtract))
            st.do(TS(small[:, 5:6], small[:, 4:5], LAMBDA_INIT, None, ALU.add))
            lam_s = small[:, 5:6]
            st.do(TS(small[:, 6:7], par("subln"), 1.0 - LAMBDA_INIT, None, ALU.mult))
            subln = small[:, 6:7]
            pos, ang, turns, args = small[:, 56:58], rope_t[:, 0, 0:32], rope_t[:, 1, 0:32], rope_t[:, 3, 0:32]
            st.do(V.tensor_copy(pos, pos_i[:, :]))
            st.do(TT(ang.rearrange("p (b n) -> p b n", b=TB), con("invf").unsqueeze(1).broadcast_to([P, TB, 16]),
                     pos.unsqueeze(2).broadcast_to([P, TB, 16]), ALU.mult))
            st.do(TS(turns, ang, 1.0 / (2 * np.pi), ROUND, ALU.mult, ALU.add))
            st.do(TS(turns, turns, ROUND, None, ALU.subtract))
            c1 = 6.28125
            c2_ = float(np.float32(np.round((2 * np.pi - c1) * 2 ** 22) / 2 ** 22))
            c3 = float(2 * np.pi - c1 - c2_)
            for part in (c1, c2_, c3):
                st.do(STT(out=ang, in0=turns, scalar=-part, in1=ang, op0=ALU.mult, op1=ALU.add))
            st.do(TS(args, ang, 3.1415925, -3.1415925, ALU.min, ALU.max))
            st.do(TS(rope_t[:, 3, 32:64], args, -1.0, None, ALU.mult))
            st.do(TT(rope_t[:, 3, 32:64], rope_t[:, 3, 32:64], args, ALU.max))
            TS(rope_t[:, 3, 32:64], rope_t[:, 3, 32:64], -1.0, float(np.pi / 2), ALU.mult, ALU.add)\
                .then_inc(angles, 1)

            for i in range(H1 + 2):
                if i >= 2:
                    hd = i - 2
                    dve.wait_ge(weights_in, hd + 1)
                    if hd >= 2:
                        pair_done(dve, "o", 0, hd - 2)
                    TT(two["pa"][:, hd % 2, :], two["dd"][:, hd % 2, :], mask, ALU.mult).then_inc(sb_probs, 1)
                if i < H1:
                    b = i % 2
                    dve.wait_ge(log_part, i + 1)
                    ps = full(dve, ("z", i))
                    sp_ = two["sp"][:, b, :]
                    st.do(STT(out=sp_, in0=ps[:, 0:ATT], scalar=0.0, in1=two["az"][:, b, :],
                              op0=ALU.max, op1=ALU.add))
                    TT(two["spm"][:, b, :], sp_, mask, ALU.mult).then_inc(fails, 1)
                    drains(TT(two["dd"][:, b, :], ps[:, 0:ATT], sp_, ALU.subtract), ("z", i))
                if 1 <= i <= H1:
                    hd = i - 1
                    ps = full(dve, ("t", hd))
                    drained(dve, ("z", hd))
                    drains(TT(two["la"][:, hd % 2, :], ps[:, 0:ATT], two["dd"][:, hd % 2, :], ALU.add), ("t", hd))

            norm(1, 384)
            apply(cq, cqn, par("cq_norm"), 3, normed)
            norm(2, 256)
            apply(ckv, ckvn, par("ckv_norm"), 2, normed)
            norm(3, 512)
            apply(sbT, mixed[:, 0:4, :], par("sb_out_norm"), 4, normed)
            dve.wait_ge(sincos, 1)
            sc_ = rope_t[:, 4, 0:64].rearrange("p (k b n) -> p k b n", k=2, b=TB)
            rm = a1["tsq"][:, 0:4 * 128].rearrange("p (m h n) -> p m h n", m=4, h=H1)
            for n, (src, gname) in enumerate(((qt, "q_norm"), (kt, "k_norm"))):
                what = ("uq", "ukv")[n]
                for tb in range(TB):
                    for hf in range(2):
                        drained(dve, (what, tb, hf))
                if n:
                    for tb in range(TB):
                        st.do(V.tensor_copy(kt[:, tb, :, NOPE:QKD],
                                            kpe[:, tb, :].unsqueeze(1).broadcast_to([P, H1, ROPE])))
                flat = a1[("qt", "kt")[n]].rearrange("p (n e) -> p n e", e=QKD)
                hm, hr = small[:, 8:24], small[:, 24 + 16 * n:40 + 16 * n]
                st.do(TT(tsq[:, :, :], flat, flat, ALU.mult))
                st.do(V.tensor_reduce(hm, tsq[:, :, :], AX.X, ALU.add))
                TS(hm, hm, 1.0 / QKD, EPS, ALU.mult, ALU.add).then_inc(head_ms, 1)
                dve.wait_ge(head_root, n + 1)
                st.do(V.reciprocal(hr, hr))
                st.do(TT(flat, flat, hr.unsqueeze(2).broadcast_to([P, 16, QKD]), ALU.mult))
                st.do(TT(flat, flat, par(gname).unsqueeze(1).broadcast_to([P, 16, QKD]), ALU.mult))
                for tb in range(TB):
                    x1, x2 = src[:, tb, :, NOPE:NOPE + 16], src[:, tb, :, NOPE + 16:QKD]
                    sn, cs = (sc_[:, q, tb, :].unsqueeze(1).broadcast_to([P, H1, 16]) for q in range(2))
                    TT(rm[:, 0, :, :], x1, cs, ALU.mult)
                    TT(rm[:, 1, :, :], x2, sn, ALU.mult)
                    TT(rm[:, 2, :, :], x1, sn, ALU.mult)
                    st.do(TT(rm[:, 3, :, :], x2, cs, ALU.mult))
                    st.do(TT(x1, rm[:, 0, :, :], rm[:, 1, :, :], ALU.subtract))
                    ins = TT(x2, rm[:, 2, :, :], rm[:, 3, :, :], ALU.add)
                    if tb:
                        ins.then_inc(qk_ready, 1)
                    else:
                        st.do(ins)
            for i in range(H1 + 2):
                if 1 <= i <= H1:
                    hd = i - 1
                    b = hd % 2
                    ps = full(dve, ("s", hd))
                    st.do(V.memset(ps[0:64, 0:ATT].rearrange("p (a c) -> p a c", a=6)[:, 1:6:4, :], -1e30))
                    V.reduce_max(sm(b, 0), ps[:, 0:P], AX.X)
                    st.do(V.reduce_max(sm(b, 1), ps[:, P:ATT], AX.X))
                    TS(stat[:, b, 2:4], stat[:, b, 0:2], -QKD ** -0.5, None, ALU.mult).then_inc(neg_max, 1)
                if i >= 2:
                    hd = i - 2
                    b = hd % 2
                    drained(dve, ("s", hd))
                    st.do(V.reciprocal(stat[:, b, 6:8], stat[:, b, 4:6]))
                    e = two["E"][:, b, :]
                    TS(e[:, 0:P], e[:, 0:P], sm(b, 6), None, ALU.mult)
                    TS(e[:, P:ATT], e[:, P:ATT], sm(b, 7), None, ALU.mult).then_inc(probs, 1)
            norm(4, 512)
            apply(mlaT, mixed[:, 4:8, :], par("mla_out_norm"), 4, normed)
            for c in range(4):
                ps = full(dve, ("wo", c))
                xs = x[:, 2 * c:2 * c + 2, :]
                drains(TT(xs, ps[:, :].rearrange("p (c t) -> p c t", c=2), xs, ALU.add), ("wo", c))

            norm(5)
            apply(x, h, par("ffn_norm"), KC, normed)
            h_lows(0)

            def top16(vals, idx, rows):
                for m, r in enumerate(rows):
                    ins = V.max(vals[:, m, 0:8], r)
                st.do(ins)
                for m, r in enumerate(rows):
                    V.max_index(idx[:, m, 0:8], vals[:, m, 0:8], r)
                for m, r in enumerate(rows):
                    ins = V.match_replace(out=r, in_to_replace=vals[:, m, 0:8], in_values=r, imm_value=-3.0e38)
                st.do(ins)
                for m, r in enumerate(rows):
                    ins = V.max(vals[:, m, 8:16], r)
                st.do(ins)
                for m, r in enumerate(rows):
                    ins = V.max_index(idx[:, m, 8:16], vals[:, m, 8:16], r)
                st.do(ins)

            s_h = r_s[:, :, :].rearrange("p (h c) k -> p h c k", c=2)
            i_h = r_i[:, :, :].rearrange("p (h c) k -> p h c k", c=2)
            for tb in range(TB):
                for q in range(4):
                    drained(dve, ("ss", tb, q))
                top16(r_s, r_iu, [sc[:, tb, m, :] for m in range(16)])
                st.do(V.tensor_copy(r_i[:, :, :], r_iu[:, :, :]))
                st.do(TT(cand.rearrange("p h (a b) -> p h a b", a=TOPK),
                         s_h[:, :, 0, :].unsqueeze(3).broadcast_to([P, PH, TOPK, TOPK]),
                         s_h[:, :, 1, :].unsqueeze(2).broadcast_to([P, PH, TOPK, TOPK]), ALU.add))
                top16(r_b, r_bu, [cand[:, m, :] for m in range(PH)])
                st.do(V.tensor_copy(small[:, 40:48], r_b[:, :, 0]))
                TT(r_b[:, :, :], r_b[:, :, :], small[:, 40:48].unsqueeze(2).broadcast_to([P, PH, TOPK]),
                   ALU.subtract).then_inc(router_max, 1)
                flat = a2r["bu"].bitcast(U32)
                TS(r_au[:, 0, :], flat, 4, None, ALU.logical_shift_right)
                st.do(TS(r_au[:, 1, :], flat, 15, None, ALU.bitwise_and))
                st.do(V.tensor_copy(r_ab[:, :, :], r_au[:, :, :]))
                for c in range(2):
                    st.do(TT(oh, iota[:, 0:TOPK].unsqueeze(1).broadcast_to([P, PH * TOPK, TOPK]),
                             r_ab[:, c, :].unsqueeze(2).broadcast_to([P, PH * TOPK, TOPK]), ALU.is_equal))
                    o4 = a2["oh"].rearrange("p (h k a) -> p h k a", h=PH, k=TOPK)
                    st.do(TT(o4, o4, i_h[:, :, c, :].unsqueeze(2).broadcast_to([P, PH, TOPK, TOPK]), ALU.mult))
                    st.do(V.tensor_reduce(r_out[:, tb, c, :], oh, AX.X, ALU.add))
                dve.wait_ge(router_exp, tb + 1)
                st.do(V.tensor_reduce(small[:, 48:56], r_b[:, :, :], AX.X, ALU.add))
                st.do(V.reciprocal(small[:, 48:56], small[:, 48:56]))
                TT(r_out[:, tb, 2, :].rearrange("p (h k) -> p h k", h=PH), r_b[:, :, :],
                   small[:, 48:56].unsqueeze(2).broadcast_to([P, PH, TOPK]), ALU.mult).then_inc(routed, 1)

            dve.wait_ge(columns_made, NADA // 2)
            ada_b = par("ada_b")
            TT(ada[:, :, :], acc[0][:, 0:2 * NADA].rearrange("p (n c) -> p n c", c=2),
               ada_b.unsqueeze(2).broadcast_to([P, NADA, 2]), ALU.add).then_inc(ada_ready, 1)
            dve.wait_ge(ada_ready, 1)
            mg, fgn = par("mix_norm_g"), par("ffn_norm_g")
            for n, (layer, part, col, g) in enumerate(((0, 1, 1, mg), (0, 1, 0, mg), (0, 4, 0, fgn),
                                                       (1, 1, 0, mg), (1, 4, 0, fgn))):
                st.do(STT(out=gsc[:, n, :], in0=mod(layer, part, col), scalar=1.0,
                          in1=g[:, 8 * layer:8 * layer + 8], op0=ALU.add, op1=ALU.mult))

            drained(dve, ("rt", 0))
            drained(dve, ("rt", 1))
            full(dve, ("u", UT - 1))
            act_out = arena[:, :].rearrange("p (j t) -> p t j", t=T)

            def weighted_rows(t, b):
                for g in range(GB):
                    TS(oneA[:, b, g, :], iota, rT[:, 0, bass.ds(t + g, 1)], rT[:, 2, bass.ds(t + g, 1)],
                             ALU.is_equal, ALU.mult)
                    ins = TS(oneB[:, b, g, :], iota, rT[:, 1, bass.ds(t + g, 1)], None, ALU.is_equal)
                ins.then_inc(one_hot, 1)

            def onto(it, i):
                b = (GROUP_NO["g", 0] + i) % NB
                dve.wait_ge(bank_full[b], it + bank_fills(("g", i)))
                part = act_out[:, bass.ds(it * (NB * GB) + i * GB, GB), :]
                TT(part, psr[b][:, :].rearrange("p (g n) -> p g n", g=GB), part, ALU.mult)\
                    .then_inc(bank_drained[b], 1)

            weighted_rows(0, 0)
            weighted_rows(GB, 1)
            n_it = T // GB // NB
            for i in range(NB):
                drained(dve, ("u", UT - 1 - i))
            with dve.Fori(0, n_it - 1) as it:
                for i in range(NB):
                    onto(it, i)
                    weighted_rows(it * (NB * GB) + (i + 2) * GB, i % 2)
            for i in range(NB):
                onto(n_it - 1, i)
                if i < 2:
                    weighted_rows(T - 2 * GB + i * GB, i)

            t0 = TILE_NO["v", 0]

            def c_lows(j, it=None):
                a = j * T if it is None else it * (KC * T) + j * T
                part = arena[:, a:a + T] if it is None else arena[:, bass.ds(a, T)]
                dve.wait_ge(c_high, j + 1 if it is None else it * KC + (j + 1))
                TT(hl[:, j % KC, :], part, hh[:, j % KC, :], ALU.subtract).then_inc(c_low, 1)

            def step(j, it=None):
                used(dve, t0 + j, it, KC)
                c_lows(j + 2, it)
                split_low(nc.vector, t0 + j + 2, it, KC)

            for j in range(2):
                c_lows(j)
                split_low(nc.vector, t0 + j)
            with dve.Fori(0, J // KC - 1) as it:
                for j in range(KC):
                    step(j, it)
            for j in range(J - KC, J - 2):
                step(j)
            used(dve, TILE_NO["v", J - 1])
            for c in range(4):
                xs = x[:, 2 * c:2 * c + 2, :]
                TT(xs, acc[c][:, :].rearrange("p (c t) -> p c t", c=2), xs, ALU.add).then_inc(x_added, 1)

            norm(6)
            dve.wait_ge(late_loaded, 32)
            modulate(ctxT, hc, gsc[:, 0, :], mod(0, 0, 1), normed)
            norm(7)
            dve.wait_ge(x_added, X_ADDS["peer"])
            modulate(x, h, gsc[:, 1, :], mod(0, 0), normed)
            for n in range(2):
                for c in range(3):
                    drained(dve, ("kq"[n], c))
                src = (kall[:, :, T:S2], qf)[n]
                for r in range(0, P, 64):
                    V.tensor_copy(rot[r:r + 32, :, :], src[r + 32:r + 64, :, :])
                    ins = V.tensor_copy(rot[r + 32:r + 64, :, :], src[r:r + 32, :, :])
                st.do(ins)
                TT(rot[:, :, :], rot[:, :, :], c2["sin"].unsqueeze(1).broadcast_to([P, H2, T]), ALU.mult)
                st.do(TT(src, src, c2["cos"].unsqueeze(1).broadcast_to([P, H2, T]), ALU.mult))
                ins = TT(src, src, rot[:, :, :], ALU.add)
                ins.then_inc(rotated, 1)
                dve.wait_ge(rotated, n + 1)
            for i in range(2 * H2 + 1):
                if i < 2 * H2:
                    b = i % 2
                    for c in range(2):
                        ps = full(dve, ("s2", i, c))
                        ins = V.reduce_max(sm(b, c), ps[:, :], AX.X)
                    st.do(ins)
                    TS(stat[:, b, 2:4], stat[:, b, 0:2], -SBD ** -0.5, None, ALU.mult).then_inc(neg_max2, 1)
                if i >= 1:
                    n = i - 1
                    b = n % 2
                    drained(dve, ("s2", n, 0))
                    drained(dve, ("s2", n, 1))
                    st.do(V.reciprocal(stat[:, b, 6:8], stat[:, b, 4:6]))
                    st.do(TT(sm(b, 7), sm(b, 7), lam_s, ALU.mult))
                    e0, e1 = E01[0][:, b, :], E01[1][:, b, :]
                    st.do(TS(e1, e1, sm(b, 7), None, ALU.mult))
                    STT(out=e0, in0=e0, scalar=sm(b, 6), in1=e1, op0=ALU.mult, op1=ALU.subtract)\
                        .then_inc(diff_probs, 1)
            for p_ in range(3):
                ps = full(dve, ("sn", p_))
                drains(TS(a3["osq"][:, p_ * 512:(p_ + 1) * 512], ps[:, :], 1.0 / VD, EPS, ALU.mult, ALU.add),
                       ("sn", p_))
            dve.wait_ge(o_root, 1)
            st.do(V.reciprocal(a3["orn"], a3["orn"]))
            STT(out=a3["mix2"][:, 0:H2 * T], in0=a3["oT"], scalar=subln, in1=a3["orn"], op0=ALU.mult,
                op1=ALU.mult).then_inc(mixed2, 1)
            for c in range(4):
                ps = full(dve, ("eo", c))
                for m in range(2):
                    f = 2 * c + m
                    ins = STT(out=x[:, f, :], in0=ps[:, m * T:(m + 1) * T], scalar=mod(0, 2)[:, f:f + 1],
                              in1=x[:, f, :], op0=ALU.mult, op1=ALU.add)
                drains(ins, ("eo", c))

            def ffn(layer):
                per = 3 * FF_UNROLL

                def step(f, it=None):
                    ga, gb = GROUP_NO["fa", layer, f], GROUP_NO["fb", layer, f]
                    ba, bb = ga % NB, gb % NB
                    if f:
                        split_low(nc.vector, TILE_NO["d", layer, f - 1], it, per)
                    dve.wait_ge(bank_drained[ba], at(it, 2 * FF_UNROLL, lambda g: g // NB + 1, ga))
                    used(dve, TILE_NO["b", layer, f], it, per)
                    TT(fg[:, f % 2, :], psr[bb][:, 0:T], fs[:, f % 2, :], ALU.mult).then_inc(bank_drained[bb], 1)
                    q = NF * layer + f + 1
                    dve.wait_ge(bank_drained[bb], at(it, 2 * FF_UNROLL, lambda g: g // NB + 1, gb))
                    nc.vector.nop().then_inc(gated, 1)
                    dve.wait_ge(fg_high, q if it is None else it * FF_UNROLL + q)
                    TT(fgl[:, f % 2, :], fg[:, f % 2, :], fgh[:, f % 2, :], ALU.subtract).then_inc(fg_low, 1)

                over_ff(dve, step)
                split_low(nc.vector, TILE_NO["d", layer, NF - 1])
                used(dve, TILE_NO["d", layer, NF - 1])
                for f in range(KC):
                    STT(out=x[:, f, :], in0=acc[f // 2][:, (f % 2) * T:(f % 2 + 1) * T],
                        scalar=mod(layer, 5)[:, f:f + 1], in1=x[:, f, :], op0=ALU.mult, op1=ALU.add)\
                        .then_inc(x_added, 1)

            norm(8)
            drained(dve, ("eo", 3))
            modulate(x, h, gsc[:, 2, :], mod(0, 3), normed)
            h_lows(1)
            ffn(0)

            norm(9)
            dve.wait_ge(x_added, X_ADDS["ffn0"])
            modulate(x, h, gsc[:, 3, :], mod(1, 0), normed)
            dve.wait_ge(padded, 1)
            pb, dw = par("pw1_b"), par("dw_w")

            def gate(c):
                ps = full(dve, ("pw1", c))
                dve.wait_ge(gates, c + 1)
                drains(STT(out=upad[:, c, PADL:PADL + T], in0=ps[:, 0:T], scalar=pb[:, 2 * c:2 * c + 1],
                           in1=csig[:, c % 2, :], op0=ALU.add, op1=ALU.mult), ("pw1", c))

            def convolve(c0):
                for c in (c0, c0 + 1):
                    drained(dve, ("pw1", c))
                    TS(cv[:, c, :], upad[:, c, 0:T], dw[:, c * CONV:c * CONV + 1], par("dw_b")[:, c:c + 1],
                       ALU.mult, ALU.add).then_inc(dve_step, 1)
                with dve.Fori(1, CONV) as k:
                    for c in (c0, c0 + 1):
                        dve.wait_ge(dve_step, k * 2 + (st.n + c - c0 - 1))
                        STT(out=cv[:, c, :], in0=upad[:, c, bass.ds(k, T)], scalar=dw[:, bass.ds(k + c * CONV, 1)],
                            in1=cv[:, c, :], op0=ALU.mult, op1=ALU.add).then_inc(dve_step, 1)
                st.n += CONV * 2

            for c0, gated_by_then in ((0, (0, 1)), (2, (2, 3, 4, 5)), (4, (6, 7))):
                for c in gated_by_then:
                    gate(c)
                convolve(c0)
            dve.wait_ge(dve_step, st.n)
            for c in range(KC - PE_CONV, KC):
                drained(dve, ("conv", c))
            V.tensor_copy(small[:, 7:8], small[:, 6:7]).then_inc(conv_sum, 1)
            ps = full(dve, ("mean", 0))
            drains(TS(ms[:, :], ps[:, 0:T], 1.0 / D, None, ALU.mult), ("mean", 0))
            drained(dve, ("mean", 0))
            TT(xc[:, :, :], cv[:, :, :], ms[:, :].unsqueeze(1).broadcast_to([P, KC, T]), ALU.subtract)\
                .then_inc(centred, 1)
            dve.wait_ge(centred, 1)
            norm(10)
            modulate(xc, xc, par("ln_g"), par("ln_b"), normed)
            for c in range(4):
                ps = full(dve, ("pw2", c))
                for m in range(2):
                    f = 2 * c + m
                    ins = TS(cv2[:, f, :], ps[:, m * T:(m + 1) * T], par("pw2_b")[:, f:f + 1],
                             mod(1, 2)[:, f:f + 1], ALU.add, ALU.mult)
                drains(ins, ("pw2", c))
            for c in range(4):
                drained(dve, ("pw2", c))
            TT(x[:, :, :], x[:, :, :], cv2[:, :, :], ALU.add).then_inc(x_added, 1)
            dve.wait_ge(x_added, X_ADDS["pw2"])
            norm(11)
            modulate(x, h, gsc[:, 4, :], mod(1, 3), normed)
            h_lows(2)
            ffn(1)
            norm(12)
            dve.wait_ge(x_added, X_ADDS["ffn1"])
            apply(x, h, par("final_g"), KC, final)

        @block.gpsimd
        def _(pool):
            def lows(kind, n, count):
                with pool.Fori(0, count // 4) as it:
                    for i in range(4):
                        split_low(nc.gpsimd, n + i, it, 4)

            lows("u", TILE_NO["u", 0], J)
            pool.wait_ge(x_added, X_ADDS["peer"])
            pool.dma_start(a3["cst2"], d["consts2"]).then_inc(late_loaded, 16)
            pool.dma_start(a3["ctx"], d["ctx"]).then_inc(late_loaded, 16)
            drained(pool, ("eo", 3))
            def ffn(layer):
                def step(f, it=None):
                    for what in ("a", "b"):
                        split_low(nc.gpsimd, TILE_NO[what, layer, f], it, 3 * FF_UNROLL)

                over_ff(pool, step)

            nc.gpsimd.memset(a4["up"], 0.0).then_inc(padded, 1)
            ffn(0)
            dw = par("dw_w").rearrange("p (c k) -> p c k", c=KC)
            for c in range(PE_CONV):
                nc.gpsimd.tensor_tensor(diag[:, c, :, :], ident.unsqueeze(1).broadcast_to([P, CONV, P]),
                                        dw[:, KC - PE_CONV + c, :].unsqueeze(2).broadcast_to([P, CONV, P]),
                                        ALU.mult).then_inc(diagonals, 1)
            ffn(1)


def constants():
    f = np.float32
    p = np.arange(P)
    t = np.arange(T)
    c = {"ident": np.eye(P), "ones": np.ones((P, P)), "iota": np.broadcast_to(p, (P, P)),
         "ntri": -(p[:, None] > p[None, :]).astype(f), "nones": -np.ones((P, P)),
         "mask": np.concatenate([p[:, None] < t[None, :], (p[:, None] + P) < t[None, P:]], 1)}
    inv = f(1.0) / np.power(f(10000.0), np.arange(16, dtype=f) * f(2.0 / 32))
    c["invf"] = np.broadcast_to(inv.astype(f), (P, 16))
    c1 = np.concatenate([np.asarray(c[n], f) for n, _ in CONSTS], 1)
    inv = np.power(f(10000.0), -np.arange(0, 32, 2, dtype=f) / f(32)).astype(f)
    ang = np.concatenate([(t // 64).astype(f)[:, None] * inv, (t % 64).astype(f)[:, None] * inv], 1)
    cos, sin = np.cos(ang).T, np.sin(ang).T
    c = {"cos": np.concatenate([cos] * 4), "sin": np.concatenate([-sin, sin] * 2)}
    a = 2 * np.pi * np.outer(np.arange(64), np.arange(64)) / 64
    c["dc"] = np.kron(np.eye(2), np.cos(a) / 8)
    c["ds"] = np.kron(np.eye(2), np.sin(a) / 8)
    a = 2 * np.pi * (np.outer(t, t) % T) / T
    for n, m in (("ct", np.cos(a) / 16), ("nst", -np.sin(a) / 16)):
        c[n] = m.reshape(TB, P, T).transpose(1, 0, 2).reshape(P, TB * T)
    c2 = np.concatenate([np.asarray(c[n], f) for n, _ in CONSTS2], 1)
    return np.ascontiguousarray(c1), np.ascontiguousarray(c2)


def _by_tiles(w):
    k, n = w.shape
    return np.ascontiguousarray(w.reshape(k // P, P, n // P, P).transpose(2, 1, 0, 3)).reshape(n // P, P, -1)


def _columns(v):
    return np.ascontiguousarray(v.reshape(-1, P).T)


def _feature_major(x):
    return np.ascontiguousarray(x.reshape(T, KC, P).transpose(2, 1, 0))


def kernel(**inputs):
    import concourse.bacc as _bacc
    from concourse.bass_utils import run_bass_kernel_spmd as _run

    a = {k: np.asarray(v) for k, v in inputs.items()}
    w_in = np.zeros((D, 2304), np.float32)
    w_in[:, 0:2208] = a["w_in"][0]
    ev = a["ev_w_in_2"][0]
    pw1 = a["od_pw1_w_2"][0].reshape(KC, P, 2, KC, P).transpose(3, 2, 1, 0, 4)
    up = {n: np.ascontiguousarray(a[k].reshape(2, KC, P, NF, P).transpose(0, 3, 2, 1, 4)).reshape(2, NF, P, -1)
          for n, k in (("a", "ffn_w1_2"), ("b", "ffn_w3_2"))}
    lam = np.zeros((P, 4), np.float32)
    for n, k in enumerate(("q1", "k1", "q2", "k2")):
        lam[0:64, n] = a[f"ev_lambda_{k}_2"][0]
    fw = a["ev_fourier_w_2"][0].reshape(2, 2, 64, 64).transpose(1, 2, 0, 3).reshape(P, P)
    params = {
        "attn_norm": _columns(a["attn_norm"]), "cq_norm": _columns(a["cq_norm"]),
        "ckv_norm": _columns(a["ckv_norm"]), "sb_out_norm": _columns(a["sb_out_norm"]),
        "mla_out_norm": _columns(a["mla_out_norm"]), "ffn_norm": _columns(a["ffn_norm"]),
        "ada_b": _columns(a["ada_b_2"]), "mix_norm_g": _columns(a["mix_norm_g_2"]),
        "ffn_norm_g": _columns(a["ffn_norm_g_2"]), "subln": _columns(a["ev_subln_g_2"]),
        "pw1_b": a["od_pw1_b_2"].reshape(2, KC, P).transpose(2, 1, 0).reshape(P, 16),
        "dw_w": a["od_dw_w_2"][0].reshape(CONV, KC, P).transpose(2, 1, 0).reshape(P, KC * CONV),
        "dw_b": _columns(a["od_dw_b_2"]), "ln_g": _columns(a["od_ln_g_2"]), "ln_b": _columns(a["od_ln_b_2"]),
        "pw2_b": _columns(a["od_pw2_b_2"]), "final_g": _columns(a["final_g_2"]),
        "cc": np.stack([a["c_2"][0], a["c_ctx_2"]], 1).reshape(KC, P, 2).transpose(1, 0, 2).reshape(P, 16),
        "lambdas": lam, "q_norm": np.broadcast_to(a["q_norm"], (P, QKD)),
        "k_norm": np.broadcast_to(a["k_norm"], (P, QKD)), "fw": fw,
    }
    c1, c2 = constants()
    arrays = {
        "x": _feature_major(a["x"]), "ctx": _feature_major(a["ctx_2"]).reshape(P, -1),
        "positions": np.ascontiguousarray(a["positions"].reshape(TB, P).T.astype(np.int32)),
        "consts": c1, "consts2": c2,
        "params": np.ascontiguousarray(np.concatenate([params[n] for n, _ in PARAMS], 1)),
        "w_in": _by_tiles(w_in), "w_o": _by_tiles(a["w_o"][0]), "w_q": _by_tiles(a["peer_w_q"][0]),
        "w_uq": a["w_uq"][0].reshape(3, P, 768),
        "w_ukv": a["w_ukv"][0].reshape(2, P, 1024),
        "sub_keys": np.ascontiguousarray(
            a["peer_sub_keys"][0].transpose(3, 1, 0, 2).reshape(P, 2, 1024).transpose(1, 0, 2)),
        "peer_u": np.ascontiguousarray(
            a["peer_u"][0].reshape(P, J, KC, P).transpose(1, 3, 2, 0)).reshape(J, P, -1),
        "peer_v": np.ascontiguousarray(a["peer_v"][0].reshape(P, J, D).transpose(1, 0, 2)),
        "ada_w": np.ascontiguousarray(
            a["ada_w_2"].reshape(2, KC, P, 48, P).transpose(0, 3, 2, 1, 4)).reshape(NADA, P, -1),
        "ev_q": _by_tiles(ev[:, 0:768]), "ev_k": _by_tiles(ev[:, 768:1536]), "ev_v": _by_tiles(ev[:, 1536:2304]),
        "ev_f": _by_tiles(ev[:, 2304:2560]), "ev_o": _by_tiles(a["ev_w_out_2"][0]),
        "ffn_a": up["a"], "ffn_b": up["b"],
        "ffn_d": np.ascontiguousarray(a["ffn_w2_2"].reshape(2, NF, P, D)),
        "pw1": np.ascontiguousarray(pw1).reshape(2 * KC, P, -1), "pw2": _by_tiles(a["od_pw2_w_2"][0]),
    }
    nc = _bacc.Bacc("TRN2", target_bir_lowering=False, num_devices=1)
    d = {n: nc.dram_tensor(f"in_{n}", v.shape, mybir.dt.from_np(v.dtype), kind="ExternalInput").ap()
         for n, v in arrays.items()}
    d["out"] = nc.dram_tensor("out_0", (P, KC, T), F32, kind="ExternalOutput").ap()
    build(nc, d)
    r = _run(nc, [{f"in_{n}": v for n, v in arrays.items()}], core_ids=[0])
    return np.ascontiguousarray(r.results[0]["out_0"].transpose(2, 1, 0).reshape(1, T, D))
```

```python
from contextlib import ExitStack

import numpy as np

import concourse.bass as bass
from concourse import mybir

ALU = mybir.AluOpType
ACT = mybir.ActivationFunctionType
F32 = mybir.dt.float32
F32R = mybir.dt.float32r
I32 = mybir.dt.int32
U32 = mybir.dt.uint32
AX = mybir.AxisListType

P = 128
T = 256
TB = T // P
D = 1024
KC = D // P
EPS = 1e-6
H1 = 8
SBD = 64
QKD, NOPE, ROPE = 96, 64, 32
ATT = 3 * P
NKEY, TOPK, PH = 128, 16, 8
J = 128
UT = J // 2
H2, VD = 6, 128
S2 = 2 * T
FF = 2816
NF = FF // P
CONV = 31
PADL = CONV // 2
PE_CONV = (2, 3, 4)
NADA = 96
NS = 4
SLOT = 1024
NB = 4
LAMBDA_INIT = 0.2
FF_PEEL, FF_UNROLL, FF_LOOPS = 3, 4, 4
ACT_ROWS = 3
GB = 4
ROUND = 12582912.0


def ada_after_sb(i):
    return [("ada", n) for n in range(2 * i, 2 * i + 2)] if 0 <= i < 16 else []


def ada_after_mla(i):
    return [("ada", n) for n in range(44 + 2 * i, 46 + 2 * i)] if 0 <= i < 26 else []


ADA_BEFORE_MLA = [[("ada", n), ("ada", n + 1)] for n in range(32, 44, 2)]


def plan_tiles():
    t = [("in", c) for c in range(18)]
    t += [("ada", c) for c in range(32)]
    t += [("uq", c) for c in range(3)] + [("ukv", c) for c in range(2)]
    t += [("ada", c) for c in range(32, NADA)]
    t += [("wo", c) for c in range(8)]
    t += [("pq", c) for c in range(16)] + [("sk", c) for c in range(2)]
    t += [("u", c) for c in range(J)] + [("v", c) for c in range(J)]
    t += [("eq", c) for c in range(6)] + [("ef", c) for c in range(2)]
    t += [("ek", c) for c in range(6)] + [("ev", c) for c in range(6)]
    t += [("eo", c) for c in range(8)]
    for layer in range(2):
        if layer:
            t += [("pw1", c) for c in range(16)] + [("pw2", c) for c in range(8)]
        for f in range(NF):
            t += [("a", layer, f), ("b", layer, f)]
            if f:
                t.append(("d", layer, f - 1))
        t.append(("d", layer, NF - 1))
    return t


def sb_order():
    for i in range(H1 + 2):
        if i < H1:
            yield "z", i
        if 1 <= i <= H1:
            yield "t", i - 1
        if i >= 2:
            yield "o", i - 2


def mla_order():
    for i in range(H1 + 4):
        if i < H1:
            yield "qkT", i
        if 1 <= i <= H1:
            yield "s", i - 1
        if 3 <= i < H1 + 3:
            yield "pT", i - 3
        if i >= 4:
            yield "mo", i - 4


def diff_order():
    for i in range(2 * H2 + 3):
        if i < 2 * H2:
            yield "s2", i
        if 2 <= i < 2 * H2 + 2:
            yield "aT", i - 2
        if i >= 3 and i % 2 == 0:
            yield "o2", (i - 4) // 2


def plan_groups():
    g = [("lam",), ("norm", 0)] + [("in", c) for c in range(9)]
    for what, h in sb_order():
        if what == "o":
            if h % 2 == 0:
                g.append(("o", h // 2))
        else:
            g.append((what, h))
    g += [("norm", 1), ("norm", 2), ("norm", 3)]
    g += [("uq", tb, hf) for hf in range(2) for tb in range(TB)]
    g += [("ukv", tb, hf) for hf in range(2) for tb in range(TB)]
    for what, h in mla_order():
        if what == "mo":
            if h % 2 == 0:
                g.append(("mo", h // 2))
        else:
            g.append((what, h))
    g += [("norm", 4)] + [("wo", c) for c in range(4)]
    g += [("norm", 5)] + [("pq", c) for c in range(8)]
    g += [("ss", tb, q) for tb in range(TB) for q in range(4)]
    g += [("u", c) for c in range(UT // 2)]
    g += [("rt", 0), ("rt", 1)]
    g += [("u", c) for c in range(UT // 2, UT)]
    g += [("g", c) for c in range(T // GB)]
    g += [("norm", 6)] + [("q", c) for c in range(3)] + [("f", 0), ("norm", 7)]
    g += [("fy", 0), ("fy", 1), ("fz", 0), ("fw", 0)]
    for c in range(3):
        g += [("k", c), ("kc", c)]
    for c in range(3):
        g += [("v2", c), ("vc", c)]
    for what, i in diff_order():
        if what == "s2":
            g += [("s2", i, 0), ("s2", i, 1)]
        else:
            g.append((what, i))
    g += [("sn", p) for p in range(3)] + [("eo", c) for c in range(4)]
    g.append(("norm", 8))
    g += [(x, 0, f) for f in range(NF) for x in ("fa", "fb")]
    g.append(("norm", 9))
    g += [("pw1", c) for c in range(8)] + [("conv", c) for c in PE_CONV]
    g += [("mean", 0), ("norm", 10)] + [("pw2", c) for c in range(4)]
    g.append(("norm", 11))
    g += [(x, 1, f) for f in range(NF) for x in ("fa", "fb")]
    g.append(("norm", 12))
    return g


TILES = plan_tiles()
GROUPS = plan_groups()
TILE_NO = {name: n for n, name in enumerate(TILES)}
GROUP_NO = {name: n for n, name in enumerate(GROUPS)}
assert len(TILE_NO) == len(TILES) and len(GROUP_NO) == len(GROUPS)


NORM_CHUNKS = (8, 3, 2, 4, 4, 8, 8, 8, 8, 8, 8, 8, 8)


def squares_before(k):
    return sum((n + 1) // 2 for n in NORM_CHUNKS[:k])


BY_POOL = ("in", "pq", "u", "ek", "ev", "eq", "ef", "pw1", "a", "b")
BY_DVE = ("v", "d")


def split_no(n):
    return sum(t[0] in BY_POOL + BY_DVE for t in TILES[:n])


def pool_no(n):
    return sum(t[0] in BY_POOL for t in TILES[:n])


def dve_no(n):
    return sum(t[0] in BY_DVE for t in TILES[:n])


def at(it, per, value, n):
    v = value(n)
    return v if it is None else it * (value(n + per) - v) + v


LAST_TILE = {("u", c): TILE_NO["u", 2 * c + 1] for c in range(UT)}
LAST_TILE |= {(k, c): TILE_NO[k, 2 * c + 1] for k, n in (("in", 9), ("pq", 8), ("pw1", 8)) for c in range(n)}
LAST_TILE |= {(g, c): TILE_NO[k, 2 * c + 1] for g, k in (("k", "ek"), ("kc", "ek"), ("v2", "ev"), ("vc", "ev"), ("q", "eq"))
              for c in range(3)}
LAST_TILE["f", 0] = TILE_NO["ef", 1]
for _l in range(2):
    for _f in range(NF):
        LAST_TILE["fa", _l, _f] = TILE_NO["a", _l, _f]
        LAST_TILE["fb", _l, _f] = TILE_NO["b", _l, _f]


def bank_fills(name):
    n = GROUP_NO[name]
    return 1 + sum(g not in LAST_TILE for g in GROUPS[n % NB:n:NB])

PARAMS = [("attn_norm", 8), ("cq_norm", 3), ("ckv_norm", 2), ("sb_out_norm", 4), ("mla_out_norm", 4),
          ("ffn_norm", 8), ("ada_b", 96), ("mix_norm_g", 16), ("ffn_norm_g", 16), ("subln", 1),
          ("pw1_b", 16), ("dw_w", 8 * CONV), ("dw_b", 8), ("ln_g", 8), ("ln_b", 8), ("pw2_b", 8),
          ("final_g", 8), ("cc", 16), ("lambdas", 4), ("q_norm", 96), ("k_norm", 96), ("fw", 128)]
CONSTS = [("ident", 128), ("ones", 128), ("iota", 128), ("ntri", 128), ("nones", 128),
          ("mask", ATT), ("invf", 16)]
CONSTS2 = [("cos", T), ("sin", T), ("dc", 128), ("ds", 128), ("ct", 2 * T), ("nst", 2 * T)]


def offsets(table):
    at, out = 0, {}
    for name, n in table:
        out[name] = (at, at + n)
        at += n
    return out, at


def build(nc, d):
    with ExitStack() as ctx:
        def sb(name, shape, dt=F32):
            return ctx.enter_context(nc.sbuf_tensor(name, shape, dt))

        def sem(name):
            return ctx.enter_context(nc.semaphore(name))

        ring = sb("ring", [P, NS, SLOT])
        arena_at = -(-nc.sbuf_base // 32) * 32
        arena = sb("arena", [P, J * T])
        wh = sb("wh", [P, 2, SLOT], F32R)
        wl = sb("wl", [P, 2, SLOT], F32R)
        x = sb("x", [P, KC, T])
        hh = sb("hh", [P, KC, T], F32R)
        hl = sb("hl", [P, KC, T], F32R)
        sq = sb("sq", [P, 2048])
        h = sq[:, :].rearrange("p (c t) -> p c t", t=T)
        fgh, fgl = (nc.alloc_sbuf_tensor_at(name, [P, 2, T], F32R, offset=arena_at + 4 * (J * T - n * 2 * T))
                    for name, n in (("fgh", 2), ("fgl", 1)))
        po, pn = offsets(PARAMS)
        co, cn = offsets(CONSTS)
        prm = sb("prm", [P, pn])
        cst = sb("cst", [P, cn])
        pos_i = sb("pos_i", [P, TB], I32)
        ms = sb("ms", [P, T])
        rms = sb("rms", [P, T])
        rinv = sb("rinv", [P, T])
        rT = sb("rT", [P, 3, T])
        ada = sb("ada", [P, NADA, 2])
        gsc = sb("gsc", [P, 5, KC])
        small = sb("small", [P, 64])
        stat = sb("stat", [P, 2, 8])
        psr = [ctx.enter_context(nc.psum_tensor(f"psr{i}", [P, 512], F32)) for i in range(NB)]
        acc = [ctx.enter_context(nc.psum_tensor(f"acc{i}", [P, 512], F32)) for i in range(4)]

        def par(name):
            return prm[:, po[name][0]:po[name][1]]

        def con(name):
            return cst[:, co[name][0]:co[name][1]]

        ident, ones, iota = con("ident"), con("ones"), con("iota")
        ntri, nones, mask = con("ntri"), con("nones"), con("mask")

        def cut(spec, base=0):
            out, at = {}, base
            for name, n in spec:
                out[name] = arena[:, at:at + n]
                at += n
            assert at <= J * T, at
            return out

        a1 = cut([("sbq", 1024), ("sbk", 1024), ("sbv", 1024), ("cq", 768), ("ckv", 512), ("kpe", 64),
                  ("az", 2 * ATT), ("sp", 2 * ATT), ("spm", 2 * ATT), ("dd", 2 * ATT), ("la", 2 * ATT),
                  ("pa", 2 * ATT), ("sbT", 1024), ("mlaT", 1024), ("mixed", 2048),
                  ("cqn", 768), ("ckvn", 512), ("qt", 1536), ("kt", 1536), ("vt", 1024),
                  ("qkT", 4096), ("E", 2 * ATT), ("PT", 2 * ATT), ("tsq", 1536), ("rope", 6 * 256),
                  ("csil", KC * 64), ("rows", 2 * P)])
        csil = a1["csil"].rearrange("p (k n) -> p k n", k=KC)
        rows = a1["rows"].rearrange("p (b n) -> p b n", b=2)
        sbq = a1["sbq"].rearrange("p (c t) -> p c t", t=T)
        sbk = a1["sbk"].rearrange("p (c t) -> p c t", t=T)
        sbv = a1["sbv"].rearrange("p (b n) -> p b n", b=TB)
        cq = a1["cq"].rearrange("p (c t) -> p c t", t=T)
        ckv = a1["ckv"].rearrange("p (c t) -> p c t", t=T)
        kpe = a1["kpe"].rearrange("p (b n) -> p b n", b=TB)
        cqn = a1["cqn"].rearrange("p (c t) -> p c t", t=T)
        ckvn = a1["ckvn"].rearrange("p (c t) -> p c t", t=T)
        two = {k: a1[k].rearrange("p (b n) -> p b n", b=2) for k in ("az", "sp", "spm", "dd", "la", "pa", "E", "PT")}
        sbT = a1["sbT"].rearrange("p (c t) -> p c t", t=T)
        mlaT = a1["mlaT"].rearrange("p (c t) -> p c t", t=T)
        mixed = a1["mixed"].rearrange("p (c t) -> p c t", t=T)
        qt = a1["qt"].rearrange("p (b h e) -> p b h e", b=TB, h=H1)
        kt = a1["kt"].rearrange("p (b h e) -> p b h e", b=TB, h=H1)
        vt = a1["vt"].rearrange("p (b h e) -> p b h e", b=TB, h=H1)
        qkT = a1["qkT"].rearrange("p (h n) -> p h n", h=H1)
        tsq = a1["tsq"].rearrange("p (n e) -> p n e", e=QKD)
        rope_t = a1["rope"].rearrange("p (k n) -> p k n", k=6)

        a2 = cut([("qT", 4096), ("sc", 4096), ("cand", 2048), ("oh", 2048)], base=J * T // 2)
        qT = a2["qT"].rearrange("p (m t) -> p m t", t=T)
        sc = a2["sc"].rearrange("p (b m n) -> p b m n", b=TB, n=NKEY)
        cand = a2["cand"].rearrange("p (h n) -> p h n", h=PH)
        oh = a2["oh"].rearrange("p (n a) -> p n a", a=TOPK)
        a2r = cut([("s", 256), ("iu", 256), ("i", 256), ("b", 128), ("bu", 128), ("ab", 256), ("au", 256),
                   ("out", TB * 384)], base=J * T // 2 + 12288)

        def halves(k, dt=F32, n=16):
            return a2r[k].bitcast(dt).rearrange("p (n k) -> p n k", n=n)

        r_s, r_iu, r_i = halves("s"), halves("iu", U32), halves("i")
        r_b, r_bu = halves("b", n=PH), halves("bu", U32, n=PH)
        r_ab, r_au = halves("ab", n=2), halves("au", U32, n=2)
        r_out = a2r["out"].rearrange("p (b q n) -> p b q n", b=TB, q=3)
        oneA = sq[:, 0:2 * GB * P].rearrange("p (b g n) -> p b g n", b=2, g=GB)
        oneB = sq[:, 1024:1024 + 2 * GB * P].rearrange("p (b g n) -> p b g n", b=2, g=GB)

        c2o, c2n = offsets(CONSTS2)
        a3_spec = ([("cst2", c2n), ("ctx", 2048), ("hc", 2048), ("kall", H2 * S2), ("vall", 4 * H2 * VD),
                  ("qf", H2 * T), ("rot", H2 * T), ("fT", 2 * T), ("Y", TB * 512), ("ZT", 2 * T),
                  ("E0", 2 * S2), ("E1", 2 * S2), ("aT", 4 * T), ("oT", H2 * T), ("osq", H2 * T),
                  ("orn", H2 * T), ("mix2", 2048), ("fs", 2 * T), ("fg", 2 * T)])
        a3, a3_at = cut(a3_spec), offsets(a3_spec)[0]
        hch, hcl = (nc.alloc_sbuf_tensor_at(name, [P, KC, T], F32R, offset=arena_at + 4 * a3_at[place][0])
                    for name, place in (("hch", "ctx"), ("hcl", "osq")))
        c2 = {k: a3["cst2"][:, a:b] for k, (a, b) in c2o.items()}
        ctxT = a3["ctx"].rearrange("p (c t) -> p c t", t=T)
        hc = a3["hc"].rearrange("p (c t) -> p c t", t=T)
        kall = a3["kall"].rearrange("p (h s) -> p h s", h=H2)
        vall = a3["vall"].rearrange("p (s n) -> p s n", s=4)
        qf = a3["qf"].rearrange("p (h t) -> p h t", h=H2)
        rot = a3["rot"].rearrange("p (h t) -> p h t", h=H2)
        fT = a3["fT"].rearrange("p (c t) -> p c t", c=2)
        Y = a3["Y"].rearrange("p (b n) -> p b n", b=TB)
        ZT = a3["ZT"].rearrange("p (c t) -> p c t", c=2)
        E01 = [a3[k].rearrange("p (b s) -> p b s", b=2) for k in ("E0", "E1")]
        aT = a3["aT"].rearrange("p (s t) -> p s t", s=4)
        oT = a3["oT"].rearrange("p (h t) -> p h t", h=H2)
        mix2 = a3["mix2"].rearrange("p (c t) -> p c t", t=T)
        fs = a3["fs"].rearrange("p (b t) -> p b t", b=2)
        fg = a3["fg"].rearrange("p (b t) -> p b t", b=2)
        a4 = cut([("up", KC * (T + 2 * PADL)), ("cv", 2048), ("cv2", 2048), ("xc", 2048), ("sig", 512),
                  ("diag", len(PE_CONV) * CONV * P)], base=c2n + 4096)
        upad = a4["up"].rearrange("p (c n) -> p c n", c=KC)
        cv = a4["cv"].rearrange("p (c t) -> p c t", t=T)
        cv2 = a4["cv2"].rearrange("p (c t) -> p c t", t=T)
        xc = a4["xc"].rearrange("p (c t) -> p c t", t=T)
        diag = a4["diag"].rearrange("p (c k n) -> p c k n", k=CONV, n=P)
        csig = a4["sig"].rearrange("p (b t) -> p b t", b=2)

        tile_ready = [sem(f"tile_ready{i}") for i in range(NS)]
        high_ready = sem("high_ready")
        low_by_pool, low_by_dve = sem("low_by_pool"), sem("low_by_dve")
        tile_used = sem("tile_used")
        h_made = sem("h_made")
        h_high, h_low = sem("h_high"), sem("h_low")
        hc_high, hc_low = sem("hc_high"), sem("hc_low")
        c_high, c_low = sem("c_high"), sem("c_low")
        gated = sem("gated")
        fg_high, fg_low = sem("fg_high"), sem("fg_low")
        bank_full = [sem(f"bank_full{i}") for i in range(NB)]
        bank_drained = [sem(f"bank_drained{i}") for i in range(NB)]
        x_loaded = sem("x_loaded")
        small_loaded = sem("small_loaded")
        late_loaded = sem("late_loaded")
        out_stored = sem("out_stored")
        act_step, dve_step = sem("act_step"), sem("dve_step")
        squares = sem("squares")
        root = sem("root")
        normed = sem("normed")
        lam_in = sem("lam_in")
        lam_exp = sem("lam_exp")
        angles = sem("angles")
        sincos = sem("sincos")
        log_part = sem("log_part")
        fails = sem("fails")
        weights_in = sem("weights_in")
        sb_probs = sem("sb_probs")
        head_ms = sem("head_ms")
        head_root = sem("head_root")
        qk_ready = sem("qk_ready")
        neg_max = sem("neg_max")
        probs = sem("probs")
        c_silu = sem("c_silu")
        router_max = sem("router_max")
        router_exp = sem("router_exp")
        routed = sem("routed")
        one_hot = sem("one_hot")
        distances = sem("distances")
        plain_rows = sem("plain_rows")
        ada_used = sem("ada_used")
        rows_copied = sem("rows_copied")
        columns_made = sem("columns_made")
        ada_ready = sem("ada_ready")
        x_added = sem("x_added")
        rotated = sem("rotated")
        neg_max2 = sem("neg_max2")
        diff_probs = sem("diff_probs")
        o_squares = sem("o_squares")
        o_root = sem("o_root")
        mixed2 = sem("mixed2")
        conv_sum = sem("conv_sum")
        centred = sem("centred")
        silued = sem("silued")
        final = sem("final")
        half_out = sem("half_out")
        gates = sem("gates")
        padded = sem("padded")
        diagonals = sem("diagonals")

        def use(n, k):
            return n % k, n // k

        def used(eng, n, it=None, per=0):
            eng.wait_ge(tile_used, at(it, per, split_no, n + 1))

        def split_high(n, it=None, per=0):
            eng, q = nc.scalar, split_no(n)
            s, u = use(n, NS)
            eng.wait_ge(tile_ready[s], at(it, per, lambda m: 16 * (m // NS + 1), n))
            if q >= 2:
                eng.wait_ge(tile_used, at(it, per, split_no, n) - 1)
            nc.scalar.activation(wh[:, q % 2, :], ring[:, s, :], ACT.Copy).then_inc(high_ready, 1)

        def split_low(eng, n, it=None, per=0):
            q = split_no(n)
            eng.wait_ge(high_ready, at(it, per, split_no, n) + 1)
            if q >= 2:
                eng.wait_ge(tile_used, at(it, per, split_no, n) - 1)
            mine = low_by_pool if TILES[n][0] in BY_POOL else low_by_dve
            eng.tensor_tensor(wl[:, q % 2, :], ring[:, n % NS, :], wh[:, q % 2, :], ALU.subtract)\
                .then_inc(mine, 1)

        def low_ready(eng, n, it=None, per=0):
            if TILES[n][0] in BY_POOL:
                eng.wait_ge(low_by_pool, at(it, per, pool_no, n) + 1)
            else:
                eng.wait_ge(low_by_dve, at(it, per, dve_no, n) + 1)

        def is_split(n):
            return n < len(TILES) and TILES[n][0] in BY_POOL + BY_DVE

        def full(eng, name):
            b = GROUP_NO[name] % NB
            if name in LAST_TILE:
                used(eng, LAST_TILE[name])
            else:
                eng.wait_ge(bank_full[b], bank_fills(name))
            return psr[b]

        def drains(ins, name):
            return ins.then_inc(bank_drained[GROUP_NO[name] % NB], 1)

        def drained(eng, name):
            b, u = use(GROUP_NO[name], NB)
            eng.wait_ge(bank_drained[b], u + 1)

        def sm(b, k):
            return stat[:, b, k:k + 1]

        def pair_done(eng, name, base, hd):
            if hd % 2 == 0:
                eng.wait_ge(half_out, base + hd // 2 + 1)
            else:
                full(eng, (name, hd // 2))

        class Steps:

            def __init__(self, eng, s):
                self.eng, self.s, self.n = eng, s, 0

            def do(self, ins):
                ins.then_inc(self.s, 1)
                self.n += 1
                self.eng.wait_ge(self.s, self.n)

        def over_ff(eng, step):
            for f in range(FF_PEEL):
                step(f)
            with eng.Fori(0, FF_LOOPS) as it:
                for i in range(FF_UNROLL):
                    step(FF_PEEL + i, it)
            for f in range(FF_PEEL + FF_UNROLL * FF_LOOPS, NF):
                step(f)

        X_ADDS = {"peer": 4, "ffn0": 12, "pw2": 16, "ffn1": 24}
        block = ctx.enter_context(nc.Block())

        @block.sync
        def _(sp):
            src = {"in": d["w_in"], "uq": d["w_uq"], "ukv": d["w_ukv"], "wo": d["w_o"], "pq": d["w_q"],
                   "sk": d["sub_keys"], "u": d["peer_u"], "ada": d["ada_w"], "v": d["peer_v"],
                   "ek": d["ev_k"], "ev": d["ev_v"], "eq": d["ev_q"], "ef": d["ev_f"], "eo": d["ev_o"],
                   "pw1": d["pw1"], "pw2": d["pw2"]}
            last_group = {"uq": ("uq", 1, 1), "ukv": ("ukv", 1, 1)}

            def released(n, it=None, per=0):
                kind, c = TILES[n][0:2]
                if is_split(n):
                    low_ready(sp, n, it, per)
                elif kind == "ada":
                    sp.wait_ge(ada_used, c + 1)
                elif kind in last_group:
                    full(sp, last_group[kind])
                elif kind == "sk":
                    full(sp, ("ss", 1, 2 * c + 1))
                elif kind in ("ek", "ev"):
                    full(sp, ({"ek": "kc", "ev": "vc"}[kind], c // 2))
                elif kind in ("eq", "ef"):
                    full(sp, (kind[1], c // 2))
                else:
                    full(sp, (kind, c // 2))

            def load(n, it=None, per=0):
                name = TILES[n]
                if n >= NS:
                    released(n - NS, it, per)
                if name[0] in ("a", "b", "d"):
                    a = d[f"ffn_{name[0]}"][name[1]]
                    a = a[name[2]] if it is None else a[it * FF_UNROLL + name[2]]
                else:
                    a = src[name[0]]
                    a = a[name[1]] if it is None else a[it * per + name[1]]
                sp.dma_start(ring[:, n % NS, 0:a.shape[1]], a).then_inc(tile_ready[n % NS], 16)

            sp.dma_start(x[:, :, :], d["x"]).then_inc(x_loaded, 16)
            sp.dma_start(cst[:, :], d["consts"]).then_inc(small_loaded, 16)
            sp.dma_start(prm[:, :], d["params"]).then_inc(small_loaded, 16)
            sp.dma_start(pos_i[:, :], d["positions"]).then_inc(small_loaded, 16)
            n = 0
            while n < len(TILES):
                kind = TILES[n][0]
                if kind in ("u", "v") and TILES[n][1] == NS:
                    count = J // NS - 1
                    with sp.Fori(0, count) as it:
                        for i in range(NS):
                            load(n + i, it, NS)
                    n += NS * count
                elif kind == "a" and TILES[n][2] == FF_PEEL:
                    with sp.Fori(0, FF_LOOPS) as it:
                        for i in range(3 * FF_UNROLL):
                            load(n + i, it, 3 * FF_UNROLL)
                    n += 3 * FF_UNROLL * FF_LOOPS
                else:
                    load(n)
                    n += 1
            sp.wait_ge(final, 1)
            sp.dma_start(d["out"], h).then_inc(out_stored, 16)
            sp.wait_ge(out_stored, 16)

        @block.tensor
        def _(pe):
            mm = nc.tensor.matmul
            g_at = [0]

            def bank(name):
                assert GROUPS[g_at[0]] == name, (GROUPS[g_at[0]], name)
                b, u = use(g_at[0], NB)
                g_at[0] += 1
                if u:
                    pe.wait_ge(bank_drained[b], u)
                return psr[b]

            def fills(ins, name):
                ins.then_inc(bank_full[GROUP_NO[name] % NB], 1)

            def tile(*name):
                s, u = use(TILE_NO[name], NS)
                pe.wait_ge(tile_ready[s], 16 * (u + 1))
                return ring[:, s, :]

            def norm(k, n, src=None):
                ps = bank(("norm", k))
                assert n == NORM_CHUNKS[k]
                for c in range(n):
                    if c % 2 == 0:
                        pe.wait_ge(squares, squares_before(k) + c // 2 + 1)
                    last = mm(ps[:, 0:T], ones, sq[:, c * T:(c + 1) * T], start=(c == 0), stop=(c == n - 1))
                fills(last, ("norm", k))

            def w8(t):
                return t.rearrange("p (k n) -> p k n", k=KC)

            def features(ps, kind, c, src, chunks=(0, 1)):
                for m in chunks:
                    w = w8(tile(kind, 2 * c + m))
                    for k in range(KC):
                        last = mm(ps[:, m * T:(m + 1) * T], w[:, k, :], src[:, k, :],
                                  start=(k == 0), stop=(k == KC - 1))
                return last

            def split_product(n, products, starts=(), low_first=False, it=None, per=0, turn=None, weights_move=False):
                b = split_no(n) % 2

                def one(out, w, a, start=False, stop=False):
                    a, w = (w, a) if weights_move else (a, w)
                    return mm(out, w, a, start=start, stop=stop, skip_group_check=True)

                pe.wait_ge(high_ready, at(it, per, split_no, n) + 1)
                for q, (out, cols, hi, lo) in enumerate(products):
                    if turn is not None and q % 2 == 0 and q < KC:
                        pe.wait_ge(h_low, 4 * turn + q // 2 + 1)
                    one(out, wh[:, b, cols], hi, start=(q in starts))
                    if not low_first:
                        one(out, wh[:, b, cols], lo)
                low_ready(pe, n, it, per)
                for out, cols, hi, lo in products:
                    if low_first:
                        one(out, wh[:, b, cols], lo)
                    last = one(out, wl[:, b, cols], hi, stop=True)
                last.then_inc(tile_used, 1)

            def chunk(k, width=P):
                return slice(k * P, k * P + width)

            def hc_parts(k):
                return hch[:, k, :], hcl[:, k, :]

            def split_features(kind, c, groups, turn=None, chunks=(0, 1)):
                banks = [(bank(name), parts) for name, parts in groups]
                for m in chunks:
                    split_product(TILE_NO[kind, 2 * c + m],
                                  [(ps[:, m * T:(m + 1) * T], chunk(k), *parts(k)) for ps, parts in banks for k in range(KC)],
                                  range(0, KC * len(banks), KC) if m == 0 else (), turn=turn if m == 0 else None)
                return banks[0][0]

            def split_tokens(kind, c, groups):
                banks = [(bank(name), parts) for name, parts in groups]
                for m in range(2):
                    split_product(TILE_NO[kind, 2 * c + m],
                                  [(ps[:, tb * T + m * P:tb * T + (m + 1) * P], chunk(k),
                                    *(x_[:, tb * P:(tb + 1) * P] for x_ in parts(k)))
                                   for ps, parts in banks for tb in range(TB) for k in range(KC)],
                                  range(0, TB * KC * len(banks), TB * KC) if m == 0 else (), weights_move=True)

            def h_parts(k):
                return hh[:, k, :], hl[:, k, :]

            def modulation(tiles):
                if not tiles:
                    return
                pair = tiles[0][1] // 2
                if pair >= 2:
                    columns(pair - 2)
                for m, name in enumerate(tiles):
                    w = w8(tile(*name))
                    for k in range(KC):
                        last = mm(acc[2 + pair % 2][64 * m:64 * m + 64, 0:P], csil[:, k, :], w[:, k, :],
                                  start=(k == 0), stop=(k == KC - 1), skip_group_check=True)
                    last.then_inc(ada_used, 1)

            def columns(pair):
                pe.wait_ge(rows_copied, pair + 1)
                sel = ident.rearrange("p (b n) -> p b n", b=2)[:, :, 0:2]
                mm(acc[0][:, 4 * pair:4 * pair + 4], rows[:, pair % 2, :], sel, start=True, stop=True)\
                    .then_inc(columns_made, 1)

            pe.wait_ge(small_loaded, 48)
            ps = bank(("lam",))
            pe.wait_ge(lam_in, 1)
            fills(mm(ps[:, 0:2], ones[0:64, :], small[0:64, 0:2], start=True, stop=True), ("lam",))

            norm(0, KC)
            for c in range(9):
                if c in (4, 5):
                    split_tokens("in", c, [(("in", c), h_parts)])
                elif c < 8:
                    split_features("in", c, [(("in", c), h_parts)], turn=0 if c == 0 else None)
                else:
                    ps = split_features("in", c, [(("in", c), h_parts)], chunks=(0,))
                    split_product(TILE_NO["in", 17],
                                  [(ps[:, T + tb * ROPE:T + (tb + 1) * ROPE], chunk(k, ROPE),
                                    *(x_[:, tb * P:(tb + 1) * P] for x_ in h_parts(k)))
                                   for tb in range(TB) for k in range(KC)], weights_move=True)

            drained(pe, ("in", 3))
            drained(pe, ("in", 5))
            pe.wait_ge(c_silu, 1)
            for step, (what, hd) in enumerate(sb_order()):
                r = 64 * (hd % 2)
                c = hd // 2
                if what == "z":
                    ps = bank(("z", hd))
                    mm(ps[:, 0:T], sbk[r:r + 64, c, 0:P], sbq[r:r + 64, c, :], start=True, stop=True)
                    fills(mm(ps[:, T:ATT], sbk[r:r + 64, c, P:T], sbq[r:r + 64, c, P:T], start=True, stop=True),
                          ("z", hd))
                elif what == "t":
                    ps = bank(("t", hd))
                    pe.wait_ge(fails, hd + 1)
                    f = two["spm"][:, hd % 2, :]
                    mm(ps[:, 0:T], ntri, f[:, 0:T], start=True, stop=False, skip_group_check=True)
                    mm(ps[:, P:T], nones, f[:, T:ATT], start=False, stop=False, skip_group_check=True)
                    fills(mm(ps[:, T:ATT], ntri, f[:, T:ATT], start=False, stop=True, skip_group_check=True),
                          ("t", hd))
                else:
                    if hd % 2 == 0:
                        ps_o = bank(("o", c))
                    pe.wait_ge(sb_probs, hd + 1)
                    a = two["pa"][:, hd % 2, :]
                    o = ps_o[r:r + 64, 0:T]
                    mm(o, sbv[:, 0, 64 * hd:64 * hd + 64], a[:, 0:T], start=True, stop=False, skip_group_check=True)
                    last = mm(ps_o[r:r + 64, P:T], sbv[:, 1, 64 * hd:64 * hd + 64], a[:, T:ATT],
                              start=False, stop=True, skip_group_check=True)
                    if hd % 2:
                        fills(last, ("o", c))
                    else:
                        last.then_inc(half_out, 1)
                modulation(ada_after_sb(step))

            norm(1, 3)
            norm(2, 2)
            norm(3, 4)
            pe.wait_ge(normed, 3)
            w = [tile("uq", k) for k in range(3)]
            for hf in range(2):
                for tb in range(TB):
                    ps = bank(("uq", tb, hf))
                    for k in range(3):
                        last = mm(ps[:, 0:384], cqn[:, k, tb * P:(tb + 1) * P], w[k][:, hf * 384:(hf + 1) * 384],
                                  start=(k == 0), stop=(k == 2))
                    fills(last, ("uq", tb, hf))
            w = [tile("ukv", k) for k in range(2)]
            for hf in range(2):
                for tb in range(TB):
                    ps = bank(("ukv", tb, hf))
                    for k in range(2):
                        last = mm(ps[:, :], ckvn[:, k, tb * P:(tb + 1) * P], w[k][:, hf * 512:(hf + 1) * 512],
                                  start=(k == 0), stop=(k == 1))
                    fills(last, ("ukv", tb, hf))
            for pair in ADA_BEFORE_MLA:
                modulation(pair)
            pe.wait_ge(qk_ready, 2)
            for step, (what, hd) in enumerate(mla_order()):
                r = 64 * (hd % 2)
                if what == "qkT":
                    ps = bank(("qkT", hd))
                    for n, src in enumerate((qt, kt)):
                        for tb in range(TB):
                            at_ = (2 * n + tb) * P
                            last = nc.tensor.transpose(ps[0:QKD, at_:at_ + P], src[:, tb, hd, :], ident)
                    fills(last, ("qkT", hd))
                elif what == "s":
                    ps = bank(("s", hd))
                    drained(pe, ("qkT", hd))
                    w = qkT[0:QKD, hd, :]
                    mm(ps[:, 0:P], w[:, 0:P], w[:, T:T + P], start=True, stop=True)
                    fills(mm(ps[:, P:ATT], w[:, P:T], w[:, T:2 * T], start=True, stop=True), ("s", hd))
                elif what == "pT":
                    ps = bank(("pT", hd))
                    pe.wait_ge(probs, hd + 1)
                    for n in range(3):
                        last = nc.tensor.transpose(ps[:, n * P:(n + 1) * P], two["E"][:, hd % 2, n * P:(n + 1) * P],
                                                   ident)
                    fills(last, ("pT", hd))
                else:
                    if hd % 2 == 0:
                        ps_o = bank(("mo", hd // 2))
                    drained(pe, ("pT", hd))
                    a = two["PT"][:, hd % 2, :]
                    mm(ps_o[r:r + 64, 0:T], vt[:, 0, hd, :], a[:, 0:T], start=True, stop=False,
                       skip_group_check=True)
                    last = mm(ps_o[r:r + 64, P:T], vt[:, 1, hd, :], a[:, T:ATT], start=False, stop=True,
                              skip_group_check=True)
                    if hd % 2:
                        fills(last, ("mo", hd // 2))
                    else:
                        last.then_inc(half_out, 1)
                modulation(ada_after_mla(step))
            columns(NADA // 2 - 2)
            columns(NADA // 2 - 1)
            norm(4, 4)
            pe.wait_ge(normed, 5)
            for c in range(4):
                ps = bank(("wo", c))
                fills(features(ps, "wo", c, mixed), ("wo", c))

            norm(5, KC)
            for c in range(8):
                split_features("pq", c, [(("pq", c), h_parts)], turn=1 if c == 0 else None)
            w = [w8(tile("sk", q)) for q in range(2)]
            drained(pe, ("pq", 6))
            drained(pe, ("pq", 7))
            for tb in range(TB):
                for q in range(4):
                    ps = bank(("ss", tb, q))
                    for m in range(4):
                        last = mm(ps[:, m * P:(m + 1) * P], qT[:, 4 * q + m, tb * P:(tb + 1) * P],
                                  w[q // 2][:, 4 * (q % 2) + m, :], start=True, stop=True)
                    fills(last, ("ss", tb, q))
            def expert_in(half):
                t0, g0 = TILE_NO["u", half * UT], GROUP_NO["u", half * UT // 2]
                with pe.Fori(0, UT // 2 // NB) as it:
                    for i in range(NB):
                        b, ub = use(g0 + i, NB)
                        pe.wait_ge(bank_drained[b], it + ub)
                        for j in range(2):
                            split_product(t0 + 2 * i + j,
                                          [(psr[b][:, j * T:(j + 1) * T], chunk(k), *h_parts(k)) for k in range(KC)],
                                          (0,) if j == 0 else (), it=it, per=2 * NB)
                g_at[0] += UT // 2

            expert_in(0)
            pe.wait_ge(routed, 2)
            for n in range(2):
                ps = bank(("rt", n))
                for q in range(3):
                    last = nc.tensor.transpose(ps[:, q * P:(q + 1) * P], r_out[:, n, q, :], ident)
                fills(last, ("rt", n))
            expert_in(1)
            g0 = GROUP_NO["g", 0]
            with pe.Fori(0, T // GB // NB) as it:
                for q in range(NB):
                    b, ub = use(g0 + q, NB)
                    pe.wait_ge(bank_drained[b], it + ub)
                    pe.wait_ge(one_hot, it * NB + (q + 1))
                    pe.wait_ge(plain_rows, it * NB + (q + 1))
                    for g in range(GB):
                        last = mm(psr[b][:, g * P:(g + 1) * P], oneA[:, q % 2, g, :], oneB[:, q % 2, g, :],
                                  start=True, stop=True)
                    last.then_inc(bank_full[b], 1)
            g_at[0] += T // GB
            pe.wait_ge(ada_ready, 1)
            t0 = TILE_NO["v", 0]

            def expert_out(it=None, first=False):
                for j in range(KC):
                    pe.wait_ge(c_low, j + 1 if it is None else it * KC + (j + 1))
                    split_product(t0 + j, [(acc[c // 2][:, (c % 2) * T:(c % 2 + 1) * T], chunk(c), *h_parts(j))
                                           for c in range(KC)],
                                  range(0, KC, 2) if first and j == 0 else (), low_first=True, it=it, per=KC)

            expert_out(first=True)
            with pe.Fori(1, J // KC) as it:
                expert_out(it)

            norm(6, KC)
            for c in range(3):
                split_features("eq", c, [(("q", c), h_parts)], turn=2 if c == 0 else None)
            split_features("ef", 0, [(("f", 0), h_parts)])
            norm(7, KC)
            pe.wait_ge(late_loaded, 32)
            drained(pe, ("f", 0))
            for tb in range(TB):
                ps = bank(("fy", tb))
                for n, m in enumerate(("dc", "ds")):
                    for c in range(2):
                        last = mm(ps[:, (2 * n + c) * P:(2 * n + c + 1) * P], fT[:, c, tb * P:(tb + 1) * P], c2[m],
                                  start=True, stop=True)
                fills(last, ("fy", tb))
            ps = bank(("fz", 0))
            drained(pe, ("fy", 0))
            drained(pe, ("fy", 1))
            for c in range(2):
                for n, m in enumerate(("ct", "nst")):
                    for tb in range(TB):
                        last = mm(ps[:, c * T:(c + 1) * T], Y[:, tb, (2 * n + c) * P:(2 * n + c + 1) * P],
                                  c2[m][:, tb * T:(tb + 1) * T], start=(n + tb == 0), stop=(n + tb == 2))
            fills(last, ("fz", 0))
            ps = bank(("fw", 0))
            drained(pe, ("fz", 0))
            fw = par("fw").rearrange("p (c n) -> p c n", c=2)
            for g in range(4):
                r, c = 64 * (g % 2), g // 2
                last = mm(ps[r:r + 64, c * T:(c + 1) * T], fw[r:r + 64, c, :], ZT[r:r + 64, c, :],
                          start=True, stop=True)
            fills(last, ("fw", 0))
            pe.wait_ge(hc_low, 1)
            for c in range(3):
                split_features("ek", c, [(("k", c), h_parts), (("kc", c), hc_parts)])
            for c in range(3):
                split_tokens("ev", c, [(("v2", c), h_parts), (("vc", c), hc_parts)])
            pe.wait_ge(rotated, 2)
            for what, i in diff_order():
                hd, tb = i // 2, i % 2
                if what == "s2":
                    for c in range(2):
                        ps = bank(("s2", i, c))
                        fills(mm(ps[:, :], qf[64 * c:64 * c + 64, hd, tb * P:(tb + 1) * P],
                                 kall[64 * c:64 * c + 64, hd, :], start=True, stop=True), ("s2", i, c))
                elif what == "aT":
                    ps = bank(("aT", i))
                    pe.wait_ge(diff_probs, i + 1)
                    for s in range(4):
                        last = nc.tensor.transpose(ps[:, s * P:(s + 1) * P], E01[0][:, i % 2, s * P:(s + 1) * P],
                                                   ident)
                    fills(last, ("aT", i))
                else:
                    ps = bank(("o2", i))
                    drained(pe, ("aT", 2 * i))
                    drained(pe, ("aT", 2 * i + 1))
                    for s in range(4):
                        last = mm(ps[:, 0:T], vall[:, s, i * VD:(i + 1) * VD], aT[:, s, :],
                                  start=(s == 0), stop=(s == 3))
                    fills(last, ("o2", i))
            for p_ in range(3):
                ps = bank(("sn", p_))
                pe.wait_ge(o_squares, p_ + 1)
                fills(mm(ps[:, :], ones, a3["osq"][:, p_ * 512:(p_ + 1) * 512], start=True, stop=True), ("sn", p_))
            pe.wait_ge(mixed2, 3)
            drained(pe, ("fw", 0))
            for c in range(4):
                ps = bank(("eo", c))
                fills(features(ps, "eo", c, mix2), ("eo", c))

            def ffn(layer):
                per = 3 * FF_UNROLL

                def up(what, f, it, turn=None):
                    n = TILE_NO[what, layer, f]
                    b, ub = use(GROUP_NO["f" + what, layer, f], NB)
                    pe.wait_ge(bank_drained[b], at(it, 2 * FF_UNROLL, lambda g: g // NB, GROUP_NO["f" + what, layer, f]))
                    split_product(n, [(psr[b][:, 0:T], chunk(k), *h_parts(k)) for k in range(KC)], (0,), it=it, per=per, turn=turn)

                def down(f, it):
                    q = NF * layer + f
                    pe.wait_ge(fg_low, q + 1 if it is None else it * FF_UNROLL + (q + 1))
                    split_product(TILE_NO["d", layer, f],
                                  [(acc[c // 2][:, (c % 2) * T:(c % 2 + 1) * T], chunk(c), fgh[:, f % 2, :], fgl[:, f % 2, :])
                                   for c in range(KC)], range(0, KC, 2) if f == 0 else (), it=it, per=per)

                def step(f, it=None):
                    up("a", f, it, turn=(3, 5)[layer] if f == 0 else None)
                    up("b", f, it)
                    if f:
                        down(f - 1, it)

                over_ff(pe, step)
                down(NF - 1, None)
                g_at[0] += 2 * NF

            norm(8, KC)
            ffn(0)

            norm(9, KC)
            for c in range(8):
                split_features("pw1", c, [(("pw1", c), h_parts)], turn=4 if c == 0 else None)
            pe.wait_ge(diagonals, len(PE_CONV) * -(-CONV // 4))
            for c in PE_CONV:
                ps = bank(("conv", c))
                drained(pe, ("pw1", c))
                for k in range(CONV):
                    last = mm(ps[:, 0:T], diag[:, PE_CONV.index(c), k, :], upad[:, c, k:k + T],
                              start=(k == 0), stop=(k == CONV - 1))
                fills(last, ("conv", c))
            ps = bank(("mean", 0))
            pe.wait_ge(conv_sum, 1)
            for c in PE_CONV:
                drained(pe, ("conv", c))
            for c in range(KC):
                last = mm(ps[:, 0:T], ones, cv[:, c, :], start=(c == 0), stop=(c == KC - 1))
            fills(last, ("mean", 0))
            norm(10, KC)
            pe.wait_ge(silued, 1)
            for c in range(4):
                ps = bank(("pw2", c))
                fills(features(ps, "pw2", c, cv), ("pw2", c))
            norm(11, KC)
            ffn(1)
            norm(12, KC)
            assert g_at[0] == len(GROUPS)

        @block.scalar
        def _(act):
            st = Steps(act, act_step)
            A = nc.scalar.activation

            def norm(k, src, n, waits, prev=None, piece_ready=None):
                for s, v in waits:
                    if v is None:
                        drained(act, s)
                    else:
                        act.wait_ge(s, v)
                if prev is not None:
                    full(act, prev)
                for q in range((n + 1) // 2):
                    if piece_ready:
                        piece_ready(q)
                    c0, c1 = 2 * q, min(2 * q + 2, n)
                    A(sq[:, c0 * T:c1 * T], src[:, c0:c1, :], ACT.Square).then_inc(squares, 1)

            def added(n, step=1):
                return lambda q: act.wait_ge(x_added, n + step * (q + 1))

            def rootof(k):
                drained(act, ("norm", k))
                A(rms[:, :], ms[:, :], ACT.Sqrt).then_inc(root, 1)

            act.wait_ge(small_loaded, 48)
            norm(0, x[:, :, :], KC, [(x_loaded, 16)])
            rootof(0)
            split_high(0)
            split_high(1)
            A(csil.rearrange("p k (r n) -> p k r n", n=2),
              par("cc").rearrange("p (k n) -> p k n", k=KC).unsqueeze(2).broadcast_to([P, KC, 32, 2]), ACT.Silu)\
                .then_inc(c_silu, 1)
            ps = full(act, ("lam",))
            drains(A(small[:, 2:4], ps[:, 0:2], ACT.Exp), ("lam",))
            def h_highs(k, turn):
                for q in range(4):
                    if q < 3:
                        act.wait_ge(h_made, 3 * turn + q + 1)
                    else:
                        act.wait_ge(normed, k + 1)
                    A(hh[:, 2 * q:2 * q + 2, :], h[:, 2 * q:2 * q + 2, :], ACT.Copy).then_inc(h_high, 1)

            def first_highs(*name):
                n = TILE_NO[name]
                split_high(n)
                split_high(n + 1)

            def highs_after(*names):
                for name in names:
                    if is_split(TILE_NO[name] + 2):
                        split_high(TILE_NO[name] + 2)

            def copy_rows(tiles):
                if tiles:
                    pair = tiles[0][1] // 2
                    act.wait_ge(ada_used, 2 * (pair + 1))
                    if pair >= 2:
                        act.wait_ge(columns_made, pair - 1)
                    A(rows[:, pair % 2, :], acc[2 + pair % 2][:, 0:P], ACT.Copy).then_inc(rows_copied, 1)

            h_highs(0, 0)
            for c in range(9):
                if c == 8:
                    act.wait_ge(angles, 1)
                    A(rope_t[:, 4, 0:64], rope_t[:, 3, 0:64], ACT.Sin).then_inc(sincos, 1)
                highs_after(("in", 2 * c), ("in", 2 * c + 1))
                ps = full(act, ("in", c))
                if c < 2:
                    ins = A(sbq[:, 2 * c:2 * c + 2, :], ps[:, :], ACT.Copy, scale=SBD ** -0.5)
                elif c < 4:
                    ins = A(sbk[:, 2 * c - 4:2 * c - 2, :], ps[:, :], ACT.Copy)
                elif c < 6:
                    ins = A(sbv[:, :, (c - 4) * T:(c - 3) * T], ps[:, :].rearrange("p (b n) -> p b n", b=TB), ACT.Copy)
                elif c == 6:
                    ins = A(cq[:, 0:2, :], ps[:, :], ACT.Copy)
                elif c == 7:
                    A(cq[:, 2, :], ps[:, 0:T], ACT.Copy).then_inc(act_step, 1)
                    st.n += 1
                    ins = A(ckv[:, 0, :], ps[:, T:2 * T], ACT.Copy)
                else:
                    A(ckv[:, 1, :], ps[:, 0:T], ACT.Copy).then_inc(act_step, 1)
                    st.n += 1
                    ins = A(kpe[:, :, :], ps[:, T:T + 64].rearrange("p (b n) -> p b n", b=TB), ACT.Copy)
                drains(ins, ("in", c))

            step = 0
            for i in range(H1 + 2):
                if i < H1:
                    copy_rows(ada_after_sb(step - 1))
                    step += 1
                    b = i % 2
                    ps = full(act, ("z", i))
                    if i >= 2:
                        act.wait_ge(fails, i - 1)
                    az = two["az"][:, b, :]
                    st.do(A(az, ps[:, 0:ATT], ACT.Abs))
                    st.do(A(az, az, ACT.Exp, scale=-1.0))
                    A(az, az, ACT.Ln, bias=1.0).then_inc(log_part, 1)
                if 1 <= i <= H1:
                    copy_rows(ada_after_sb(step - 1))
                    step += 1
                    hd = i - 1
                    drained(act, ("t", hd))
                    A(two["dd"][:, hd % 2, :], two["la"][:, hd % 2, :], ACT.Exp).then_inc(weights_in, 1)
                if i >= 2:
                    copy_rows(ada_after_sb(step - 1))
                    step += 1
                if i >= 2 and (i - 2) % 2 == 1:
                    c = (i - 2) // 2
                    ps = full(act, ("o", c))
                    drains(A(sbT[:, c, :], ps[:, 0:T], ACT.Copy), ("o", c))

            act.wait_ge(act_step, st.n)
            drained(act, ("in", 8))
            norm(1, cq[:, :, :], 3, [], prev=("norm", 0))
            rootof(1)
            norm(2, ckv[:, :, :], 2, [], prev=("norm", 1))
            rootof(2)
            drained(act, ("o", 3))
            norm(3, sbT[:, :, :], 4, [], prev=("norm", 2))
            rootof(3)
            for hf in range(2):
                for tb in range(TB):
                    ps = full(act, ("uq", tb, hf))
                    drains(A(qt[:, tb, 4 * hf:4 * hf + 4, :], ps[:, 0:384].rearrange("p (h e) -> p h e", h=4),
                             ACT.Copy), ("uq", tb, hf))
            for hf in range(2):
                for tb in range(TB):
                    ps = full(act, ("ukv", tb, hf))
                    kv = ps[:, :].rearrange("p (h e) -> p h e", h=4)
                    A(kt[:, tb, 4 * hf:4 * hf + 4, 0:NOPE], kv[:, :, 0:NOPE], ACT.Copy).then_inc(act_step, 1)
                    st.n += 1
                    drains(A(vt[:, tb, 4 * hf:4 * hf + 4, :], kv[:, :, NOPE:2 * NOPE], ACT.Copy), ("ukv", tb, hf))
            for n in range(2):
                act.wait_ge(head_ms, n + 1)
                A(small[:, 24 + 16 * n:40 + 16 * n], small[:, 8:24], ACT.Sqrt).then_inc(head_root, 1)
                for pair in ADA_BEFORE_MLA[3 * n:3 * n + 3]:
                    copy_rows(pair)
            step = 0
            for i in range(H1 + 4):
                if i < H1:
                    copy_rows(ada_after_mla(step - 1))
                    step += 1
                    ps = full(act, ("qkT", i))
                    drains(A(qkT[0:QKD, i, :], ps[0:QKD, :], ACT.Copy), ("qkT", i))
                if 1 <= i <= H1:
                    copy_rows(ada_after_mla(step - 1))
                    step += 1
                    hd = i - 1
                    b = hd % 2
                    ps = full(act, ("s", hd))
                    act.wait_ge(neg_max, hd + 1)
                    if hd >= 2:
                        full(act, ("pT", hd - 2))
                    for n, (lo, hi) in enumerate(((0, P), (P, ATT))):
                        ins = A(two["E"][:, b, lo:hi], ps[:, lo:hi], ACT.Exp, scale=QKD ** -0.5,
                                bias=sm(b, 2 + n), accum_out=sm(b, 4 + n))
                        if n == 0:
                            ins.then_inc(act_step, 1)
                            st.n += 1
                    drains(ins, ("s", hd))
                if 3 <= i < H1 + 3:
                    copy_rows(ada_after_mla(step - 1))
                    step += 1
                    hd = i - 3
                    ps = full(act, ("pT", hd))
                    if hd >= 2:
                        pair_done(act, "mo", H1 // 2, hd - 2)
                    drains(A(two["PT"][:, hd % 2, :], ps[:, 0:ATT], ACT.Copy), ("pT", hd))
                if i >= 4:
                    copy_rows(ada_after_mla(step - 1))
                    step += 1
                if i >= 4 and (i - 4) % 2 == 1:
                    c = (i - 4) // 2
                    ps = full(act, ("mo", c))
                    drains(A(mlaT[:, c, :], ps[:, 0:T], ACT.Copy), ("mo", c))
            copy_rows(ada_after_mla(step - 1))
            drained(act, ("mo", 3))
            norm(4, mlaT[:, :, :], 4, [], prev=("norm", 3))
            rootof(4)
            norm(5, x[:, :, :], KC, [], prev=("norm", 4), piece_ready=lambda q: drained(act, ("wo", q)))
            first_highs("pq", 0)
            rootof(5)
            h_highs(5, 1)
            for c in range(8):
                highs_after(("pq", 2 * c), ("pq", 2 * c + 1))
                ps = full(act, ("pq", c))
                drains(A(qT[:, 2 * c:2 * c + 2, :], ps[:, :], ACT.Copy), ("pq", c))
            split_high(TILE_NO["u", 0])
            split_high(TILE_NO["u", 1])
            for tb in range(TB):
                for q in range(4):
                    ps = full(act, ("ss", tb, q))
                    drains(A(sc[:, tb, 4 * q:4 * q + 4, :], ps[:, :].rearrange("p (m n) -> p m n", n=NKEY), ACT.Copy),
                           ("ss", tb, q))
            g0, t0 = GROUP_NO["u", 0], TILE_NO["u", 0]

            def activate(it=None, last=0):
                for i in range(NB):
                    n = t0 + last + 2 * i
                    b = (g0 + (2 if last else 0) + i) % NB
                    split_high(n + 2, it, 2 * NB)
                    split_high(n + 3, it, 2 * NB)
                    used(act, n + 1, it, 2 * NB)
                    at_ = (last * T + i * 512) if it is None else it * (NB * 512) + (last * T + i * 512)
                    part = arena[:, at_:at_ + 512] if it is None else arena[:, bass.ds(at_, 512)]
                    A(part, psr[b][:, :], ACT.Gelu).then_inc(bank_drained[b], 1)

            turns = UT // NB
            for tb, (lo, hi) in enumerate(((0, 3), (3, turns // 2))):
                with act.Fori(lo, hi) as it:
                    activate(it)
                act.wait_ge(router_max, tb + 1)
                A(r_b[:, :, :], r_b[:, :, :], ACT.Exp).then_inc(router_exp, 1)
            for n in range(2):
                ps = full(act, ("rt", n))
                drains(A(rT[:, :, n * P:(n + 1) * P], ps[:, 0:3 * P].rearrange("p (q t) -> p q t", q=3), ACT.Copy),
                       ("rt", n))
            with act.Fori(0, turns // 2 - 1) as it:
                activate(it, UT)
            activate(None, J - 2 * NB)
            def plain(t, b, g_no, it=None):
                if g_no >= 2:
                    name = ("g", g_no - 2)
                    act.wait_ge(bank_full[GROUP_NO[name] % NB],
                                bank_fills(name) if it is None else it + bank_fills(name))
                for g in range(ACT_ROWS):
                    A(oneB[:, b, g, :], iota, ACT.Abs, scale=-1.0, bias=rT[:, 1, bass.ds(t + g, 1)])\
                        .then_inc(distances, 1)
                n = (g_no + 1) * ACT_ROWS
                act.wait_ge(distances, n if it is None else it * (NB * ACT_ROWS) + n)
                part = oneB[:, b, 0:ACT_ROWS, :]
                A(part, part, ACT.Relu, scale=-1.0, bias=1.0).then_inc(plain_rows, 1)

            drained(act, ("rt", 0))
            drained(act, ("rt", 1))
            for i in range(2):
                plain(i * GB, i, i)
            with act.Fori(0, T // GB // NB - 1) as it:
                for i in range(NB):
                    plain(it * (NB * GB) + (i + 2) * GB, i % 2, i + 2, it)
            for i in range(2):
                plain(T - 2 * GB + i * GB, i, T // GB - 2 + i)
            t0 = TILE_NO["v", 0]

            def c_highs(j, it=None):
                a = j * T if it is None else it * (KC * T) + j * T
                part = arena[:, a:a + T] if it is None else arena[:, bass.ds(a, T)]
                A(hh[:, j % KC, :], part, ACT.Copy).then_inc(c_high, 1)

            for i in range(NB):
                drained(act, ("g", T // GB - 1 - i))
            c_highs(0)
            c_highs(1)

            def step(j, it=None):
                used(act, t0 + j, it, KC)
                c_highs(j + 2, it)
                split_high(t0 + j + 2, it, KC)

            with act.Fori(0, J // KC - 1) as it:
                for j in range(KC):
                    step(j, it)
            for j in range(J - KC, J - 2):
                step(j)

            norm(6, x[:, :, :], KC, [], prev=("g", T // GB - 1), piece_ready=added(0))
            first_highs("eq", 0)
            rootof(6)
            h_highs(6, 2)
            for c in range(3):
                highs_after(("eq", 2 * c), ("eq", 2 * c + 1))
                ps = full(act, ("q", c))
                drains(A(qf[:, 2 * c:2 * c + 2, :], ps[:, :].rearrange("p (h t) -> p h t", h=2), ACT.Copy), ("q", c))
                if c == 1:
                    norm(7, ctxT[:, :, :], KC, [(late_loaded, 32), (h_low, 12)], prev=("norm", 6))
            highs_after(("ef", 0), ("ef", 1))
            ps = full(act, ("f", 0))
            drains(A(fT[:, :, :], ps[:, :].rearrange("p (h t) -> p h t", h=2), ACT.Copy), ("f", 0))
            rootof(7)
            for tb in range(TB):
                ps = full(act, ("fy", tb))
                drains(A(Y[:, tb, :], ps[:, :], ACT.Copy), ("fy", tb))
            act.wait_ge(normed, 8)
            A(hch[:, :, :], hc, ACT.Copy).then_inc(hc_high, 1)
            ps = full(act, ("fz", 0))
            drains(A(ZT[:, :, :], ps[:, :].rearrange("p (h t) -> p h t", h=2), ACT.Copy), ("fz", 0))
            ps = full(act, ("fw", 0))
            drains(A(mix2[:, 6:8, :], ps[:, :].rearrange("p (h t) -> p h t", h=2), ACT.Copy), ("fw", 0))
            for c in range(3):
                highs_after(("ek", 2 * c), ("ek", 2 * c + 1))
                ps = full(act, ("k", c))
                drains(A(kall[:, 2 * c:2 * c + 2, T:S2], ps[:, :].rearrange("p (h t) -> p h t", h=2), ACT.Copy), ("k", c))
                ps = full(act, ("kc", c))
                drains(A(kall[:, 2 * c:2 * c + 2, 0:T], ps[:, :].rearrange("p (h t) -> p h t", h=2), ACT.Copy), ("kc", c))
            for c in range(3):
                highs_after(("ev", 2 * c), ("ev", 2 * c + 1))
                ps = full(act, ("v2", c))
                drains(A(vall[:, 2:4, c * T:(c + 1) * T], ps[:, :].rearrange("p (b n) -> p b n", b=2), ACT.Copy), ("v2", c))
                ps = full(act, ("vc", c))
                drains(A(vall[:, 0:2, c * T:(c + 1) * T], ps[:, :].rearrange("p (b n) -> p b n", b=2), ACT.Copy), ("vc", c))
            for i in range(2 * H2 + 3):
                if i < 2 * H2:
                    b = i % 2
                    act.wait_ge(neg_max2, i + 1)
                    for c in range(2):
                        ps = full(act, ("s2", i, c))
                        if i >= 2 and c == 0:
                            full(act, ("aT", i - 2))
                            act.wait_ge(diff_probs, i - 1)
                        drains(A(E01[c][:, b, :], ps[:, :], ACT.Exp, scale=SBD ** -0.5,
                                 bias=sm(b, 2 + c), accum_out=sm(b, 4 + c)), ("s2", i, c))
                if 2 <= i < 2 * H2 + 2:
                    n = i - 2
                    ps = full(act, ("aT", n))
                    if n >= 2:
                        full(act, ("o2", n // 2 - 1))
                    drains(A(aT[:, :, (n % 2) * P:(n % 2 + 1) * P], ps[:, :].rearrange("p (s t) -> p s t", s=4),
                             ACT.Copy), ("aT", n))
                if i >= 3 and i % 2 == 0:
                    hd = (i - 4) // 2
                    ps = full(act, ("o2", hd))
                    drains(A(oT[:, hd, :], ps[:, 0:T], ACT.Copy), ("o2", hd))
            drained(act, ("o2", H2 - 1))
            drained(act, ("o2", H2 - 2))
            pieces = [slice(p_ * 512, (p_ + 1) * 512) for p_ in range(3)]
            for piece in pieces:
                A(a3["osq"][:, piece], a3["oT"][:, piece], ACT.Square).then_inc(o_squares, 1)
            for p_, piece in enumerate(pieces):
                drained(act, ("sn", p_))
                A(a3["orn"][:, piece], a3["osq"][:, piece], ACT.Sqrt).then_inc(o_root, 1)

            def ffn(layer):
                per = 3 * FF_UNROLL

                def ahead(name, it):
                    n = TILE_NO[name] + 2
                    if n <= TILE_NO["d", layer, NF - 1]:
                        split_high(n, it, per)

                def step(f, it=None):
                    b = GROUP_NO["fa", layer, f] % NB
                    ahead(("a", layer, f), it)
                    used(act, TILE_NO["a", layer, f], it, per)
                    A(fs[:, f % 2, :], psr[b][:, 0:T], ACT.Silu).then_inc(bank_drained[b], 1)
                    ahead(("b", layer, f), it)
                    q = NF * layer + f + 1
                    act.wait_ge(gated, q if it is None else it * FF_UNROLL + q)
                    if f >= 2:
                        used(act, TILE_NO["d", layer, f - 2], it, per)
                    A(fgh[:, f % 2, :], fg[:, f % 2, :], ACT.Copy).then_inc(fg_high, 1)
                    if f:
                        ahead(("d", layer, f - 1), it)

                over_ff(act, step)

            norm(8, x[:, :, :], KC, [], prev=("norm", 7), piece_ready=lambda q: drained(act, ("eo", q)))
            first_highs("a", 0, 0)
            rootof(8)
            h_highs(8, 3)
            ffn(0)
            norm(9, x[:, :, :], KC, [], prev=("norm", 8), piece_ready=added(X_ADDS["peer"], 2))
            first_highs("pw1", 0)
            rootof(9)
            h_highs(9, 4)
            pb = par("pw1_b")
            for c in range(8):
                highs_after(("pw1", 2 * c), ("pw1", 2 * c + 1))
                ps = full(act, ("pw1", c))
                if c >= 2:
                    drained(act, ("pw1", c - 2))
                A(csig[:, c % 2, :], ps[:, T:2 * T], ACT.Sigmoid, bias=pb[:, 2 * c + 1:2 * c + 2]).then_inc(gates, 1)
            for c in PE_CONV:
                ps = full(act, ("conv", c))
                drains(A(cv[:, c, :], ps[:, 0:T], ACT.Identity, bias=par("dw_b")[:, c:c + 1]), ("conv", c))
            act.wait_ge(centred, 1)
            norm(10, xc[:, :, :], KC, [], prev=("norm", 9))
            rootof(10)
            act.wait_ge(normed, 11)
            A(cv[:, :, :], xc[:, :, :], ACT.Silu).then_inc(silued, 1)
            norm(11, x[:, :, :], KC, [], prev=("norm", 10), piece_ready=added(X_ADDS["ffn0"]))
            first_highs("a", 1, 0)
            rootof(11)
            h_highs(11, 5)
            ffn(1)
            norm(12, x[:, :, :], KC, [], prev=("norm", 11), piece_ready=added(X_ADDS["pw2"], 2))
            rootof(12)

        @block.vector
        def _(dve):
            V = nc.vector
            st = Steps(dve, dve_step)
            TT, TS, STT = V.tensor_tensor, V.tensor_scalar, V.scalar_tensor_tensor

            def norm(k, n=D):
                ps = full(dve, ("norm", k))
                drains(TS(ms[:, :], ps[:, 0:T], 1.0 / n, EPS, ALU.mult, ALU.add), ("norm", k))
                dve.wait_ge(root, k + 1)
                st.do(V.reciprocal(rinv[:, :], rms[:, :]))

            def quarters(dst, ins, c):
                if dst is h and c % 2 and c < KC - 1:
                    ins.then_inc(h_made, 1)

            def apply(src, dst, gain, n, signal):
                for c in range(n):
                    ins = STT(out=dst[:, c, :], in0=src[:, c, :], scalar=gain[:, c:c + 1], in1=rinv[:, :],
                              op0=ALU.mult, op1=ALU.mult)
                    if signal is normed:
                        quarters(dst, ins, c)
                ins.then_inc(signal, 1)

            def modulate(src, dst, gain, shift, signal):
                n0 = st.n
                for c in range(0, KC, 2):
                    TT(dst[:, c:c + 2, :], src[:, c:c + 2, :], rinv[:, :].unsqueeze(1).broadcast_to([P, 2, T]), ALU.mult)\
                        .then_inc(dve_step, 1)
                    st.n += 1
                for c in range(KC):
                    dve.wait_ge(dve_step, n0 + c // 2 + 1)
                    ins = TS(dst[:, c, :], dst[:, c, :], gain[:, c:c + 1], shift[:, c:c + 1], ALU.mult, ALU.add)
                    quarters(dst, ins, c)
                ins.then_inc(signal, 1)

            def h_lows(turn):
                for q in range(4):
                    dve.wait_ge(h_high, 4 * turn + q + 1)
                    part = slice(2 * q, 2 * q + 2)
                    TT(hl[:, part, :], h[:, part, :], hh[:, part, :], ALU.subtract).then_inc(h_low, 1)

            def mod(layer, part, col=0):
                a = 48 * layer + 8 * part
                return ada[:, a:a + 8, col]

            dve.wait_ge(small_loaded, 48)
            lam = par("lambdas")
            TT(small[0:64, 0:2], lam[0:64, 0:4:2], lam[0:64, 1:4:2], ALU.mult).then_inc(lam_in, 1)
            norm(0)
            dve.wait_ge(x_loaded, 16)
            apply(x, h, par("attn_norm"), KC, normed)
            h_lows(0)
            drained(dve, ("lam",))
            st.do(TT(small[:, 4:5], small[:, 2:3], small[:, 3:4], ALU.subtract))
            st.do(TS(small[:, 5:6], small[:, 4:5], LAMBDA_INIT, None, ALU.add))
            lam_s = small[:, 5:6]
            st.do(TS(small[:, 6:7], par("subln"), 1.0 - LAMBDA_INIT, None, ALU.mult))
            subln = small[:, 6:7]
            pos, ang, turns, args = small[:, 56:58], rope_t[:, 0, 0:32], rope_t[:, 1, 0:32], rope_t[:, 3, 0:32]
            st.do(V.tensor_copy(pos, pos_i[:, :]))
            st.do(TT(ang.rearrange("p (b n) -> p b n", b=TB), con("invf").unsqueeze(1).broadcast_to([P, TB, 16]),
                     pos.unsqueeze(2).broadcast_to([P, TB, 16]), ALU.mult))
            st.do(TS(turns, ang, 1.0 / (2 * np.pi), ROUND, ALU.mult, ALU.add))
            st.do(TS(turns, turns, ROUND, None, ALU.subtract))
            c1 = 6.28125
            c2_ = float(np.float32(np.round((2 * np.pi - c1) * 2 ** 22) / 2 ** 22))
            c3 = float(2 * np.pi - c1 - c2_)
            for part in (c1, c2_, c3):
                st.do(STT(out=ang, in0=turns, scalar=-part, in1=ang, op0=ALU.mult, op1=ALU.add))
            st.do(TS(args, ang, 3.1415925, -3.1415925, ALU.min, ALU.max))
            st.do(TS(rope_t[:, 3, 32:64], args, -1.0, None, ALU.mult))
            st.do(TT(rope_t[:, 3, 32:64], rope_t[:, 3, 32:64], args, ALU.max))
            TS(rope_t[:, 3, 32:64], rope_t[:, 3, 32:64], -1.0, float(np.pi / 2), ALU.mult, ALU.add)\
                .then_inc(angles, 1)

            for i in range(H1 + 2):
                if i >= 2:
                    hd = i - 2
                    dve.wait_ge(weights_in, hd + 1)
                    if hd >= 2:
                        pair_done(dve, "o", 0, hd - 2)
                    TT(two["pa"][:, hd % 2, :], two["dd"][:, hd % 2, :], mask, ALU.mult).then_inc(sb_probs, 1)
                if i < H1:
                    b = i % 2
                    dve.wait_ge(log_part, i + 1)
                    ps = full(dve, ("z", i))
                    sp_ = two["sp"][:, b, :]
                    st.do(STT(out=sp_, in0=ps[:, 0:ATT], scalar=0.0, in1=two["az"][:, b, :],
                              op0=ALU.max, op1=ALU.add))
                    TT(two["spm"][:, b, :], sp_, mask, ALU.mult).then_inc(fails, 1)
                    drains(TT(two["dd"][:, b, :], ps[:, 0:ATT], sp_, ALU.subtract), ("z", i))
                if 1 <= i <= H1:
                    hd = i - 1
                    ps = full(dve, ("t", hd))
                    drained(dve, ("z", hd))
                    drains(TT(two["la"][:, hd % 2, :], ps[:, 0:ATT], two["dd"][:, hd % 2, :], ALU.add), ("t", hd))

            norm(1, 384)
            apply(cq, cqn, par("cq_norm"), 3, normed)
            norm(2, 256)
            apply(ckv, ckvn, par("ckv_norm"), 2, normed)
            norm(3, 512)
            apply(sbT, mixed[:, 0:4, :], par("sb_out_norm"), 4, normed)
            dve.wait_ge(sincos, 1)
            sc_ = rope_t[:, 4, 0:64].rearrange("p (k b n) -> p k b n", k=2, b=TB)
            rm = a1["tsq"][:, 0:4 * 128].rearrange("p (m h n) -> p m h n", m=4, h=H1)
            for n, (src, gname) in enumerate(((qt, "q_norm"), (kt, "k_norm"))):
                what = ("uq", "ukv")[n]
                for tb in range(TB):
                    for hf in range(2):
                        drained(dve, (what, tb, hf))
                if n:
                    for tb in range(TB):
                        st.do(V.tensor_copy(kt[:, tb, :, NOPE:QKD],
                                            kpe[:, tb, :].unsqueeze(1).broadcast_to([P, H1, ROPE])))
                flat = a1[("qt", "kt")[n]].rearrange("p (n e) -> p n e", e=QKD)
                hm, hr = small[:, 8:24], small[:, 24 + 16 * n:40 + 16 * n]
                st.do(TT(tsq[:, :, :], flat, flat, ALU.mult))
                st.do(V.tensor_reduce(hm, tsq[:, :, :], AX.X, ALU.add))
                TS(hm, hm, 1.0 / QKD, EPS, ALU.mult, ALU.add).then_inc(head_ms, 1)
                dve.wait_ge(head_root, n + 1)
                st.do(V.reciprocal(hr, hr))
                st.do(TT(flat, flat, hr.unsqueeze(2).broadcast_to([P, 16, QKD]), ALU.mult))
                st.do(TT(flat, flat, par(gname).unsqueeze(1).broadcast_to([P, 16, QKD]), ALU.mult))
                for tb in range(TB):
                    x1, x2 = src[:, tb, :, NOPE:NOPE + 16], src[:, tb, :, NOPE + 16:QKD]
                    sn, cs = (sc_[:, q, tb, :].unsqueeze(1).broadcast_to([P, H1, 16]) for q in range(2))
                    TT(rm[:, 0, :, :], x1, cs, ALU.mult)
                    TT(rm[:, 1, :, :], x2, sn, ALU.mult)
                    TT(rm[:, 2, :, :], x1, sn, ALU.mult)
                    st.do(TT(rm[:, 3, :, :], x2, cs, ALU.mult))
                    st.do(TT(x1, rm[:, 0, :, :], rm[:, 1, :, :], ALU.subtract))
                    ins = TT(x2, rm[:, 2, :, :], rm[:, 3, :, :], ALU.add)
                    if tb:
                        ins.then_inc(qk_ready, 1)
                    else:
                        st.do(ins)
            for i in range(H1 + 2):
                if 1 <= i <= H1:
                    hd = i - 1
                    b = hd % 2
                    ps = full(dve, ("s", hd))
                    st.do(V.memset(ps[0:64, 0:ATT].rearrange("p (a c) -> p a c", a=6)[:, 1:6:4, :], -1e30))
                    V.reduce_max(sm(b, 0), ps[:, 0:P], AX.X)
                    st.do(V.reduce_max(sm(b, 1), ps[:, P:ATT], AX.X))
                    TS(stat[:, b, 2:4], stat[:, b, 0:2], -QKD ** -0.5, None, ALU.mult).then_inc(neg_max, 1)
                if i >= 2:
                    hd = i - 2
                    b = hd % 2
                    drained(dve, ("s", hd))
                    st.do(V.reciprocal(stat[:, b, 6:8], stat[:, b, 4:6]))
                    e = two["E"][:, b, :]
                    TS(e[:, 0:P], e[:, 0:P], sm(b, 6), None, ALU.mult)
                    TS(e[:, P:ATT], e[:, P:ATT], sm(b, 7), None, ALU.mult).then_inc(probs, 1)
            norm(4, 512)
            apply(mlaT, mixed[:, 4:8, :], par("mla_out_norm"), 4, normed)
            for c in range(4):
                ps = full(dve, ("wo", c))
                xs = x[:, 2 * c:2 * c + 2, :]
                drains(TT(xs, ps[:, :].rearrange("p (c t) -> p c t", c=2), xs, ALU.add), ("wo", c))

            norm(5)
            apply(x, h, par("ffn_norm"), KC, normed)
            h_lows(1)

            def top16(vals, idx, rows):
                for m, r in enumerate(rows):
                    ins = V.max(vals[:, m, 0:8], r)
                st.do(ins)
                for m, r in enumerate(rows):
                    V.max_index(idx[:, m, 0:8], vals[:, m, 0:8], r)
                for m, r in enumerate(rows):
                    ins = V.match_replace(out=r, in_to_replace=vals[:, m, 0:8], in_values=r, imm_value=-3.0e38)
                st.do(ins)
                for m, r in enumerate(rows):
                    ins = V.max(vals[:, m, 8:16], r)
                st.do(ins)
                for m, r in enumerate(rows):
                    ins = V.max_index(idx[:, m, 8:16], vals[:, m, 8:16], r)
                st.do(ins)

            s_h = r_s[:, :, :].rearrange("p (h c) k -> p h c k", c=2)
            i_h = r_i[:, :, :].rearrange("p (h c) k -> p h c k", c=2)
            for tb in range(TB):
                for q in range(4):
                    drained(dve, ("ss", tb, q))
                top16(r_s, r_iu, [sc[:, tb, m, :] for m in range(16)])
                st.do(V.tensor_copy(r_i[:, :, :], r_iu[:, :, :]))
                st.do(TT(cand.rearrange("p h (a b) -> p h a b", a=TOPK),
                         s_h[:, :, 0, :].unsqueeze(3).broadcast_to([P, PH, TOPK, TOPK]),
                         s_h[:, :, 1, :].unsqueeze(2).broadcast_to([P, PH, TOPK, TOPK]), ALU.add))
                top16(r_b, r_bu, [cand[:, m, :] for m in range(PH)])
                st.do(V.tensor_copy(small[:, 40:48], r_b[:, :, 0]))
                TT(r_b[:, :, :], r_b[:, :, :], small[:, 40:48].unsqueeze(2).broadcast_to([P, PH, TOPK]),
                   ALU.subtract).then_inc(router_max, 1)
                flat = a2r["bu"].bitcast(U32)
                TS(r_au[:, 0, :], flat, 4, None, ALU.logical_shift_right)
                st.do(TS(r_au[:, 1, :], flat, 15, None, ALU.bitwise_and))
                st.do(V.tensor_copy(r_ab[:, :, :], r_au[:, :, :]))
                for c in range(2):
                    st.do(TT(oh, iota[:, 0:TOPK].unsqueeze(1).broadcast_to([P, PH * TOPK, TOPK]),
                             r_ab[:, c, :].unsqueeze(2).broadcast_to([P, PH * TOPK, TOPK]), ALU.is_equal))
                    o4 = a2["oh"].rearrange("p (h k a) -> p h k a", h=PH, k=TOPK)
                    st.do(TT(o4, o4, i_h[:, :, c, :].unsqueeze(2).broadcast_to([P, PH, TOPK, TOPK]), ALU.mult))
                    st.do(V.tensor_reduce(r_out[:, tb, c, :], oh, AX.X, ALU.add))
                dve.wait_ge(router_exp, tb + 1)
                st.do(V.tensor_reduce(small[:, 48:56], r_b[:, :, :], AX.X, ALU.add))
                st.do(V.reciprocal(small[:, 48:56], small[:, 48:56]))
                TT(r_out[:, tb, 2, :].rearrange("p (h k) -> p h k", h=PH), r_b[:, :, :],
                   small[:, 48:56].unsqueeze(2).broadcast_to([P, PH, TOPK]), ALU.mult).then_inc(routed, 1)

            dve.wait_ge(columns_made, NADA // 2)
            ada_b = par("ada_b")
            TT(ada[:, :, :], acc[0][:, 0:2 * NADA].rearrange("p (n c) -> p n c", c=2),
               ada_b.unsqueeze(2).broadcast_to([P, NADA, 2]), ALU.add).then_inc(ada_ready, 1)
            dve.wait_ge(ada_ready, 1)
            mg, fgn = par("mix_norm_g"), par("ffn_norm_g")
            for n, (layer, part, col, g) in enumerate(((0, 1, 1, mg), (0, 1, 0, mg), (0, 4, 0, fgn),
                                                       (1, 1, 0, mg), (1, 4, 0, fgn))):
                st.do(STT(out=gsc[:, n, :], in0=mod(layer, part, col), scalar=1.0,
                          in1=g[:, 8 * layer:8 * layer + 8], op0=ALU.add, op1=ALU.mult))

            drained(dve, ("rt", 0))
            drained(dve, ("rt", 1))
            full(dve, ("u", UT - 1))
            act_out = arena[:, :].rearrange("p (j t) -> p t j", t=T)

            def weighted_rows(t, b):
                for g in range(GB):
                    ins = TS(oneA[:, b, g, :], iota, rT[:, 0, bass.ds(t + g, 1)], rT[:, 2, bass.ds(t + g, 1)],
                             ALU.is_equal, ALU.mult)
                for g in range(ACT_ROWS, GB):
                    ins = TS(oneB[:, b, g, :], iota, rT[:, 1, bass.ds(t + g, 1)], None, ALU.is_equal)
                ins.then_inc(one_hot, 1)

            def onto(it, i):
                b = (GROUP_NO["g", 0] + i) % NB
                dve.wait_ge(bank_full[b], it + bank_fills(("g", i)))
                part = act_out[:, bass.ds(it * (NB * GB) + i * GB, GB), :]
                TT(part, psr[b][:, :].rearrange("p (g n) -> p g n", g=GB), part, ALU.mult)\
                    .then_inc(bank_drained[b], 1)

            weighted_rows(0, 0)
            weighted_rows(GB, 1)
            n_it = T // GB // NB
            for i in range(NB):
                drained(dve, ("u", UT - 1 - i))
            with dve.Fori(0, n_it - 1) as it:
                for i in range(NB):
                    onto(it, i)
                    weighted_rows(it * (NB * GB) + (i + 2) * GB, i % 2)
            for i in range(NB):
                onto(n_it - 1, i)
                if i < 2:
                    weighted_rows(T - 2 * GB + i * GB, i)

            t0 = TILE_NO["v", 0]

            def c_lows(j, it=None):
                a = j * T if it is None else it * (KC * T) + j * T
                part = arena[:, a:a + T] if it is None else arena[:, bass.ds(a, T)]
                dve.wait_ge(c_high, j + 1 if it is None else it * KC + (j + 1))
                TT(hl[:, j % KC, :], part, hh[:, j % KC, :], ALU.subtract).then_inc(c_low, 1)

            def step(j, it=None):
                used(dve, t0 + j, it, KC)
                c_lows(j + 2, it)
                split_low(nc.vector, t0 + j + 2, it, KC)

            for j in range(2):
                c_lows(j)
                split_low(nc.vector, t0 + j)
            with dve.Fori(0, J // KC - 1) as it:
                for j in range(KC):
                    step(j, it)
            for j in range(J - KC, J - 2):
                step(j)
            used(dve, TILE_NO["v", J - 1])
            for c in range(4):
                xs = x[:, 2 * c:2 * c + 2, :]
                TT(xs, acc[c][:, :].rearrange("p (c t) -> p c t", c=2), xs, ALU.add).then_inc(x_added, 1)

            norm(6)
            dve.wait_ge(x_added, X_ADDS["peer"])
            modulate(x, h, gsc[:, 1, :], mod(0, 0), normed)
            h_lows(2)
            norm(7)
            dve.wait_ge(late_loaded, 32)
            modulate(ctxT, hc, gsc[:, 0, :], mod(0, 0, 1), normed)
            for n in range(2):
                for c in range(3):
                    drained(dve, ("qk"[n], c))
                src = (qf, kall[:, :, T:S2])[n]
                for r in range(0, P, 64):
                    V.tensor_copy(rot[r:r + 32, :, :], src[r + 32:r + 64, :, :])
                    ins = V.tensor_copy(rot[r + 32:r + 64, :, :], src[r:r + 32, :, :])
                st.do(ins)
                TT(rot[:, :, :], rot[:, :, :], c2["sin"].unsqueeze(1).broadcast_to([P, H2, T]), ALU.mult)
                st.do(TT(src, src, c2["cos"].unsqueeze(1).broadcast_to([P, H2, T]), ALU.mult))
                ins = TT(src, src, rot[:, :, :], ALU.add)
                ins.then_inc(rotated, 1)
                dve.wait_ge(rotated, n + 1)
            for i in range(2 * H2 + 1):
                if i < 2 * H2:
                    b = i % 2
                    for c in range(2):
                        ps = full(dve, ("s2", i, c))
                        ins = V.reduce_max(sm(b, c), ps[:, :], AX.X)
                    st.do(ins)
                    TS(stat[:, b, 2:4], stat[:, b, 0:2], -SBD ** -0.5, None, ALU.mult).then_inc(neg_max2, 1)
                if i >= 1:
                    n = i - 1
                    b = n % 2
                    drained(dve, ("s2", n, 0))
                    drained(dve, ("s2", n, 1))
                    st.do(V.reciprocal(stat[:, b, 6:8], stat[:, b, 4:6]))
                    st.do(TT(sm(b, 7), sm(b, 7), lam_s, ALU.mult))
                    e0, e1 = E01[0][:, b, :], E01[1][:, b, :]
                    st.do(TS(e1, e1, sm(b, 7), None, ALU.mult))
                    STT(out=e0, in0=e0, scalar=sm(b, 6), in1=e1, op0=ALU.mult, op1=ALU.subtract)\
                        .then_inc(diff_probs, 1)
            for p_ in range(3):
                ps = full(dve, ("sn", p_))
                drains(TS(a3["osq"][:, p_ * 512:(p_ + 1) * 512], ps[:, :], 1.0 / VD, EPS, ALU.mult, ALU.add),
                       ("sn", p_))
            for p_ in range(3):
                piece = slice(p_ * 512, (p_ + 1) * 512)
                dve.wait_ge(o_root, p_ + 1)
                st.do(V.reciprocal(a3["orn"][:, piece], a3["orn"][:, piece]))
                STT(out=a3["mix2"][:, piece], in0=a3["oT"][:, piece], scalar=subln, in1=a3["orn"][:, piece],
                    op0=ALU.mult, op1=ALU.mult).then_inc(mixed2, 1)
            for c in range(4):
                ps = full(dve, ("eo", c))
                for m in range(2):
                    f = 2 * c + m
                    ins = STT(out=x[:, f, :], in0=ps[:, m * T:(m + 1) * T], scalar=mod(0, 2)[:, f:f + 1],
                              in1=x[:, f, :], op0=ALU.mult, op1=ALU.add)
                drains(ins, ("eo", c))

            def ffn(layer):
                per = 3 * FF_UNROLL

                def step(f, it=None):
                    ga, gb = GROUP_NO["fa", layer, f], GROUP_NO["fb", layer, f]
                    ba, bb = ga % NB, gb % NB
                    if f:
                        split_low(nc.vector, TILE_NO["d", layer, f - 1], it, per)
                    dve.wait_ge(bank_drained[ba], at(it, 2 * FF_UNROLL, lambda g: g // NB + 1, ga))
                    used(dve, TILE_NO["b", layer, f], it, per)
                    TT(fg[:, f % 2, :], psr[bb][:, 0:T], fs[:, f % 2, :], ALU.mult).then_inc(bank_drained[bb], 1)
                    q = NF * layer + f + 1
                    dve.wait_ge(bank_drained[bb], at(it, 2 * FF_UNROLL, lambda g: g // NB + 1, gb))
                    nc.vector.nop().then_inc(gated, 1)
                    dve.wait_ge(fg_high, q if it is None else it * FF_UNROLL + q)
                    TT(fgl[:, f % 2, :], fg[:, f % 2, :], fgh[:, f % 2, :], ALU.subtract).then_inc(fg_low, 1)

                over_ff(dve, step)
                split_low(nc.vector, TILE_NO["d", layer, NF - 1])
                used(dve, TILE_NO["d", layer, NF - 1])
                for f in range(KC):
                    STT(out=x[:, f, :], in0=acc[f // 2][:, (f % 2) * T:(f % 2 + 1) * T],
                        scalar=mod(layer, 5)[:, f:f + 1], in1=x[:, f, :], op0=ALU.mult, op1=ALU.add)\
                        .then_inc(x_added, 1)

            norm(8)
            drained(dve, ("eo", 3))
            modulate(x, h, gsc[:, 2, :], mod(0, 3), normed)
            h_lows(3)
            ffn(0)

            norm(9)
            dve.wait_ge(x_added, X_ADDS["ffn0"])
            modulate(x, h, gsc[:, 3, :], mod(1, 0), normed)
            h_lows(4)
            dve.wait_ge(padded, 1)
            pb, dw = par("pw1_b"), par("dw_w")

            def gate(c):
                ps = full(dve, ("pw1", c))
                dve.wait_ge(gates, c + 1)
                drains(STT(out=upad[:, c, PADL:PADL + T], in0=ps[:, 0:T], scalar=pb[:, 2 * c:2 * c + 1],
                           in1=csig[:, c % 2, :], op0=ALU.add, op1=ALU.mult), ("pw1", c))

            def convolve(chunks):
                for c in chunks:
                    drained(dve, ("pw1", c))
                    TS(cv[:, c, :], upad[:, c, 0:T], dw[:, c * CONV:c * CONV + 1], par("dw_b")[:, c:c + 1],
                       ALU.mult, ALU.add).then_inc(dve_step, 1)
                n = len(chunks)
                with dve.Fori(1, CONV) as k:
                    for i, c in enumerate(chunks):
                        dve.wait_ge(dve_step, k * n + (st.n + i - n + 1))
                        STT(out=cv[:, c, :], in0=upad[:, c, bass.ds(k, T)], scalar=dw[:, bass.ds(k + c * CONV, 1)],
                            in1=cv[:, c, :], op0=ALU.mult, op1=ALU.add).then_inc(dve_step, 1)
                st.n += CONV * n

            for c in range(4):
                gate(c)
            convolve((0, 1))
            for c in range(4, KC):
                gate(c)
            convolve((5, 6, 7))
            dve.wait_ge(dve_step, st.n)
            for c in PE_CONV:
                drained(dve, ("conv", c))
            V.tensor_copy(small[:, 7:8], small[:, 6:7]).then_inc(conv_sum, 1)
            ps = full(dve, ("mean", 0))
            drains(TS(ms[:, :], ps[:, 0:T], 1.0 / D, None, ALU.mult), ("mean", 0))
            drained(dve, ("mean", 0))
            TT(xc[:, :, :], cv[:, :, :], ms[:, :].unsqueeze(1).broadcast_to([P, KC, T]), ALU.subtract)\
                .then_inc(centred, 1)
            dve.wait_ge(centred, 1)
            norm(10)
            modulate(xc, xc, par("ln_g"), par("ln_b"), normed)
            for c in range(4):
                ps = full(dve, ("pw2", c))
                for m in range(2):
                    f = 2 * c + m
                    ins = TS(cv2[:, f, :], ps[:, m * T:(m + 1) * T], par("pw2_b")[:, f:f + 1],
                             mod(1, 2)[:, f:f + 1], ALU.add, ALU.mult)
                drains(ins, ("pw2", c))
            for c in range(4):
                drained(dve, ("pw2", c))
                xs = x[:, 2 * c:2 * c + 2, :]
                TT(xs, xs, cv2[:, 2 * c:2 * c + 2, :], ALU.add).then_inc(x_added, 1)
            dve.wait_ge(x_added, X_ADDS["pw2"])
            norm(11)
            modulate(x, h, gsc[:, 4, :], mod(1, 3), normed)
            h_lows(5)
            ffn(1)
            norm(12)
            dve.wait_ge(x_added, X_ADDS["ffn1"])
            apply(x, h, par("final_g"), KC, final)

        @block.gpsimd
        def _(pool):
            def lows(n, count):
                with pool.Fori(0, count // 4) as it:
                    for i in range(4):
                        split_low(nc.gpsimd, n + i, it, 4)
                for i in range(count - count % 4, count):
                    split_low(nc.gpsimd, n + i)

            split_low(nc.gpsimd, 0)
            split_low(nc.gpsimd, 1)
            lows(2, 16)
            lows(TILE_NO["pq", 0], 16)
            lows(TILE_NO["u", 0], J)
            pool.wait_ge(x_added, X_ADDS["peer"])
            pool.dma_start(a3["cst2"], d["consts2"]).then_inc(late_loaded, 16)
            pool.dma_start(a3["ctx"], d["ctx"]).then_inc(late_loaded, 16)
            lows(TILE_NO["eq", 0], 8)
            pool.wait_ge(hc_high, 1)
            nc.gpsimd.tensor_tensor(hcl[:, :, :], hc, hch[:, :, :], ALU.subtract).then_inc(hc_low, 1)
            lows(TILE_NO["ek", 0], 12)
            drained(pool, ("eo", 3))
            dw = par("dw_w").rearrange("p (c k) -> p c k", c=KC)
            pieces = [(i, k, min(k + 4, CONV)) for i in range(len(PE_CONV)) for k in range(0, CONV, 4)]

            def diagonal(n):
                for _ in range(min(n, len(pieces))):
                    i, k0, k1 = pieces.pop(0)
                    nc.gpsimd.tensor_tensor(
                        diag[:, i, k0:k1, :], ident.unsqueeze(1).broadcast_to([P, k1 - k0, P]),
                        dw[:, PE_CONV[i], k0:k1].unsqueeze(2).broadcast_to([P, k1 - k0, P]),
                        ALU.mult).then_inc(diagonals, 1)

            def ffn(layer):
                def step(f, it=None):
                    for what in ("a", "b"):
                        split_low(nc.gpsimd, TILE_NO[what, layer, f], it, 3 * FF_UNROLL)
                    if layer == 0 and it is None:
                        diagonal(3)

                over_ff(pool, step)

            nc.gpsimd.memset(a4["up"], 0.0).then_inc(padded, 1)
            diagonal(6)
            ffn(0)
            assert not pieces
            lows(TILE_NO["pw1", 0], 16)
            ffn(1)


def constants():
    f = np.float32
    p = np.arange(P)
    t = np.arange(T)
    c = {"ident": np.eye(P), "ones": np.ones((P, P)), "iota": np.broadcast_to(p, (P, P)),
         "ntri": -(p[:, None] > p[None, :]).astype(f), "nones": -np.ones((P, P)),
         "mask": np.concatenate([p[:, None] < t[None, :], (p[:, None] + P) < t[None, P:]], 1)}
    inv = f(1.0) / np.power(f(10000.0), np.arange(16, dtype=f) * f(2.0 / 32))
    c["invf"] = np.broadcast_to(inv.astype(f), (P, 16))
    c1 = np.concatenate([np.asarray(c[n], f) for n, _ in CONSTS], 1)
    inv = np.power(f(10000.0), -np.arange(0, 32, 2, dtype=f) / f(32)).astype(f)
    ang = np.concatenate([(t // 64).astype(f)[:, None] * inv, (t % 64).astype(f)[:, None] * inv], 1)
    cos, sin = np.cos(ang).T, np.sin(ang).T
    c = {"cos": np.concatenate([cos] * 4), "sin": np.concatenate([-sin, sin] * 2)}
    a = 2 * np.pi * np.outer(np.arange(64), np.arange(64)) / 64
    c["dc"] = np.kron(np.eye(2), np.cos(a) / 8)
    c["ds"] = np.kron(np.eye(2), np.sin(a) / 8)
    a = 2 * np.pi * (np.outer(t, t) % T) / T
    for n, m in (("ct", np.cos(a) / 16), ("nst", -np.sin(a) / 16)):
        c[n] = m.reshape(TB, P, T).transpose(1, 0, 2).reshape(P, TB * T)
    c2 = np.concatenate([np.asarray(c[n], f) for n, _ in CONSTS2], 1)
    return np.ascontiguousarray(c1), np.ascontiguousarray(c2)


def _by_tiles(w):
    k, n = w.shape
    return np.ascontiguousarray(w.reshape(k // P, P, n // P, P).transpose(2, 1, 0, 3)).reshape(n // P, P, -1)


def _columns(v):
    return np.ascontiguousarray(v.reshape(-1, P).T)


def _feature_major(x):
    return np.ascontiguousarray(x.reshape(T, KC, P).transpose(2, 1, 0))


def kernel(**inputs):
    import concourse.bacc as _bacc
    from concourse.bass_utils import run_bass_kernel_spmd as _run

    a = {k: np.asarray(v) for k, v in inputs.items()}
    w_in = np.zeros((D, 2304), np.float32)
    w_in[:, 0:2208] = a["w_in"][0]
    ev = a["ev_w_in_2"][0]
    pw1 = a["od_pw1_w_2"][0].reshape(KC, P, 2, KC, P).transpose(3, 2, 1, 0, 4)
    up = {n: np.ascontiguousarray(a[k].reshape(2, KC, P, NF, P).transpose(0, 3, 2, 1, 4)).reshape(2, NF, P, -1)
          for n, k in (("a", "ffn_w1_2"), ("b", "ffn_w3_2"))}
    lam = np.zeros((P, 4), np.float32)
    for n, k in enumerate(("q1", "k1", "q2", "k2")):
        lam[0:64, n] = a[f"ev_lambda_{k}_2"][0]
    fw = a["ev_fourier_w_2"][0].reshape(2, 2, 64, 64).transpose(1, 2, 0, 3).reshape(P, P)
    params = {
        "attn_norm": _columns(a["attn_norm"]), "cq_norm": _columns(a["cq_norm"]),
        "ckv_norm": _columns(a["ckv_norm"]), "sb_out_norm": _columns(a["sb_out_norm"]),
        "mla_out_norm": _columns(a["mla_out_norm"]), "ffn_norm": _columns(a["ffn_norm"]),
        "ada_b": _columns(a["ada_b_2"]), "mix_norm_g": _columns(a["mix_norm_g_2"]),
        "ffn_norm_g": _columns(a["ffn_norm_g_2"]), "subln": _columns(a["ev_subln_g_2"]),
        "pw1_b": a["od_pw1_b_2"].reshape(2, KC, P).transpose(2, 1, 0).reshape(P, 16),
        "dw_w": a["od_dw_w_2"][0].reshape(CONV, KC, P).transpose(2, 1, 0).reshape(P, KC * CONV),
        "dw_b": _columns(a["od_dw_b_2"]), "ln_g": _columns(a["od_ln_g_2"]), "ln_b": _columns(a["od_ln_b_2"]),
        "pw2_b": _columns(a["od_pw2_b_2"]), "final_g": _columns(a["final_g_2"]),
        "cc": np.stack([a["c_2"][0], a["c_ctx_2"]], 1).reshape(KC, P, 2).transpose(1, 0, 2).reshape(P, 16),
        "lambdas": lam, "q_norm": np.broadcast_to(a["q_norm"], (P, QKD)),
        "k_norm": np.broadcast_to(a["k_norm"], (P, QKD)), "fw": fw,
    }
    c1, c2 = constants()
    arrays = {
        "x": _feature_major(a["x"]), "ctx": _feature_major(a["ctx_2"]).reshape(P, -1),
        "positions": np.ascontiguousarray(a["positions"].reshape(TB, P).T.astype(np.int32)),
        "consts": c1, "consts2": c2,
        "params": np.ascontiguousarray(np.concatenate([params[n] for n, _ in PARAMS], 1)),
        "w_in": _by_tiles(w_in), "w_o": _by_tiles(a["w_o"][0]), "w_q": _by_tiles(a["peer_w_q"][0]),
        "w_uq": a["w_uq"][0].reshape(3, P, 768),
        "w_ukv": a["w_ukv"][0].reshape(2, P, 1024),
        "sub_keys": np.ascontiguousarray(
            a["peer_sub_keys"][0].transpose(3, 1, 0, 2).reshape(P, 2, 1024).transpose(1, 0, 2)),
        "peer_u": np.ascontiguousarray(
            a["peer_u"][0].reshape(P, J, KC, P).transpose(1, 3, 2, 0)).reshape(J, P, -1),
        "peer_v": np.ascontiguousarray(a["peer_v"][0].reshape(P, J, D).transpose(1, 0, 2)),
        "ada_w": np.ascontiguousarray(
            a["ada_w_2"].reshape(2, KC, P, 48, P).transpose(0, 3, 2, 1, 4)).reshape(NADA, P, -1),
        "ev_q": _by_tiles(ev[:, 0:768]), "ev_k": _by_tiles(ev[:, 768:1536]), "ev_v": _by_tiles(ev[:, 1536:2304]),
        "ev_f": _by_tiles(ev[:, 2304:2560]), "ev_o": _by_tiles(a["ev_w_out_2"][0]),
        "ffn_a": up["a"], "ffn_b": up["b"],
        "ffn_d": np.ascontiguousarray(a["ffn_w2_2"].reshape(2, NF, P, D)),
        "pw1": np.ascontiguousarray(pw1).reshape(2 * KC, P, -1), "pw2": _by_tiles(a["od_pw2_w_2"][0]),
    }
    nc = _bacc.Bacc("TRN2", target_bir_lowering=False, num_devices=1)
    d = {n: nc.dram_tensor(f"in_{n}", v.shape, mybir.dt.from_np(v.dtype), kind="ExternalInput").ap()
         for n, v in arrays.items()}
    d["out"] = nc.dram_tensor("out_0", (P, KC, T), F32, kind="ExternalOutput").ap()
    build(nc, d)
    r = _run(nc, [{f"in_{n}": v for n, v in arrays.items()}], core_ids=[0])
    return np.ascontiguousarray(r.results[0]["out_0"].transpose(2, 1, 0).reshape(1, T, D))
```
